# Optimizing a Trainium2 kernel written in Bass

```python
import math
import jax, jax.numpy as jnp
from jax import lax
import numpy as np

D_MODEL = 1024
BATCH = 1
SEQ = 256
DEPTH = 1

CHUNK = 64
LEFT_CHUNKS = 8
BAND = LEFT_CHUNKS + 1
N_HEADS = 16
HEAD_DIM = 64
D_ATTN = N_HEADS * HEAD_DIM
MAX_REL = 128
D_RNN = D_MODEL
N_RG_BLOCKS = 16
RG_BLOCK = D_RNN // N_RG_BLOCKS
CONV_W = 4
RG_C = 8.0
D_FF = ((8 * D_MODEL // 3 + 255) // 256) * 256
IN_COLS = 3 * D_ATTN + 2 * D_RNN + 2 * D_MODEL
EPS = 1e-6
NEG_INF = -1e30


def rmsnorm(x, g):
    xf = x.astype(jnp.float32)
    var = jnp.mean(xf * xf, axis=-1, keepdims=True)
    return (xf * lax.rsqrt(var + EPS) * g.astype(jnp.float32)).astype(x.dtype)

def rel_bias_band(table):
    i = jnp.arange(CHUNK)[:, None]
    m = jnp.arange(BAND * CHUNK)[None, :]
    dist = i - m + LEFT_CHUNKS * CHUNK
    idx = jnp.clip(dist, -MAX_REL, MAX_REL) + MAX_REL
    return table[:, idx]

def chunked_band_attention(q, k, v, rel_table):
    B, S, _ = q.shape
    nc = S // CHUNK
    q = q.reshape(B, nc, CHUNK, N_HEADS, HEAD_DIM)
    k = k.reshape(B, nc, CHUNK, N_HEADS, HEAD_DIM)
    v = v.reshape(B, nc, CHUNK, N_HEADS, HEAD_DIM)
    pad = jnp.zeros((B, LEFT_CHUNKS, CHUNK, N_HEADS, HEAD_DIM), k.dtype)
    kp = jnp.concatenate([pad, k], axis=1)
    vp = jnp.concatenate([pad, v], axis=1)
    kb = jnp.concatenate([kp[:, j:j + nc] for j in range(BAND)], axis=2)
    vb = jnp.concatenate([vp[:, j:j + nc] for j in range(BAND)], axis=2)
    scale = 1.0 / math.sqrt(HEAD_DIM)
    s = jnp.einsum('bnqhd,bnkhd->bhnqk', q, kb).astype(jnp.float32) * scale
    s = s + rel_bias_band(rel_table).astype(jnp.float32)[None, :, None, :, :]
    key_chunk = jnp.arange(nc)[:, None] - LEFT_CHUNKS + (jnp.arange(BAND * CHUNK)[None, :] // CHUNK)
    valid = key_chunk >= 0
    s = jnp.where(valid[None, None, :, None, :], s, NEG_INF)
    p = jax.nn.softmax(s, axis=-1).astype(v.dtype)
    o = jnp.einsum('bhnqk,bnkhd->bnqhd', p, vb)
    return o.reshape(B, S, D_ATTN)

def causal_depthwise_conv(x, w, b):
    S = x.shape[1]
    xp = jnp.pad(x, ((0, 0), (CONV_W - 1, 0), (0, 0)))
    y = sum(xp[:, j:j + S] * w[j] for j in range(CONV_W))
    return y + b

def rg_lru(x, w_r, b_r, w_i, b_i, lam):
    B, S, D = x.shape
    xb = x.reshape(B, S, N_RG_BLOCKS, RG_BLOCK)
    r = jax.nn.sigmoid(jnp.einsum('bsnd,nde->bsne', xb, w_r).reshape(B, S, D) + b_r)
    i = jax.nn.sigmoid(jnp.einsum('bsnd,nde->bsne', xb, w_i).reshape(B, S, D) + b_i)
    log_a = -RG_C * r.astype(jnp.float32) * jax.nn.softplus(-lam.astype(jnp.float32))
    a = jnp.exp(log_a)
    mult = jnp.sqrt(-jnp.expm1(2.0 * log_a))
    bx = mult * (i * x).astype(jnp.float32)

    def combine(left, right):
        a1, b1 = left
        a2, b2 = right
        return a1 * a2, a2 * b1 + b2

    _, h = lax.associative_scan(combine, (a, bx), axis=1)
    return h.astype(x.dtype)

def first_inputs(seed: int = 0) -> dict:
    key = jax.random.key(seed)
    ks = jax.random.split(key, 20)
    L = DEPTH

    def nrm(k, shape, fan_in):
        return jax.random.normal(k, shape, jnp.float32) * (fan_in ** -0.5)

    x = jax.random.normal(ks[0], (BATCH, SEQ, D_MODEL), jnp.float32)
    norm_mix_g = 1.0 + 0.05 * jax.random.normal(ks[1], (L, D_MODEL), jnp.float32)
    w_in = nrm(ks[2], (L, D_MODEL, IN_COLS), D_MODEL)
    b_merge = 0.01 * jax.random.normal(ks[3], (L, 2 * D_MODEL), jnp.float32)
    rel_table = 0.5 * jax.random.normal(ks[4], (L, N_HEADS, 2 * MAX_REL + 1), jnp.float32)
    w_attn_out = nrm(ks[5], (L, D_ATTN, D_MODEL), D_ATTN)
    conv_w = nrm(ks[6], (L, CONV_W, D_RNN), CONV_W)
    conv_b = 0.01 * jax.random.normal(ks[7], (L, D_RNN), jnp.float32)
    w_rg_r = nrm(ks[8], (L, N_RG_BLOCKS, RG_BLOCK, RG_BLOCK), RG_BLOCK)
    b_rg_r = 0.01 * jax.random.normal(ks[9], (L, D_RNN), jnp.float32)
    w_rg_i = nrm(ks[10], (L, N_RG_BLOCKS, RG_BLOCK, RG_BLOCK), RG_BLOCK)
    b_rg_i = 0.01 * jax.random.normal(ks[11], (L, D_RNN), jnp.float32)
    u = jax.random.uniform(ks[12], (L, D_RNN), jnp.float32, 0.9, 0.999)
    a0 = u ** (1.0 / RG_C)
    rg_lambda = jnp.log(a0) - jnp.log1p(-a0)
    w_rnn_out = nrm(ks[13], (L, D_RNN, D_MODEL), D_RNN)
    w_o = nrm(ks[14], (L, D_MODEL, D_MODEL), D_MODEL)
    norm_ffn_g = 1.0 + 0.05 * jax.random.normal(ks[15], (L, D_MODEL), jnp.float32)
    w_ffn_in = nrm(ks[16], (L, D_MODEL, 2 * D_FF), D_MODEL)
    w_ffn_out = nrm(ks[17], (L, D_FF, D_MODEL), D_FF)
    final_norm_g = 1.0 + 0.05 * jax.random.normal(ks[18], (D_MODEL,), jnp.float32)
    return {"x": x, "norm_mix_g": norm_mix_g, "w_in": w_in, "b_merge": b_merge,
            "rel_table": rel_table, "w_attn_out": w_attn_out, "conv_w": conv_w,
            "conv_b": conv_b, "w_rg_r": w_rg_r, "b_rg_r": b_rg_r, "w_rg_i": w_rg_i,
            "b_rg_i": b_rg_i, "rg_lambda": rg_lambda, "w_rnn_out": w_rnn_out, "w_o": w_o,
            "norm_ffn_g": norm_ffn_g, "w_ffn_in": w_ffn_in, "w_ffn_out": w_ffn_out,
            "final_norm_g": final_norm_g}

def first_block(x, norm_mix_g, w_in, b_merge, rel_table, w_attn_out, conv_w, conv_b,
              w_rg_r, b_rg_r, w_rg_i, b_rg_i, rg_lambda, w_rnn_out, w_o,
              norm_ffn_g, w_ffn_in, w_ffn_out, final_norm_g):
    h = x
    splits = [D_ATTN, 2 * D_ATTN, 3 * D_ATTN, 3 * D_ATTN + D_RNN,
              3 * D_ATTN + 2 * D_RNN, 3 * D_ATTN + 2 * D_RNN + D_MODEL]
    for l in range(DEPTH):
        xn = rmsnorm(h, norm_mix_g[l])
        u = jnp.einsum('bsd,de->bse', xn, w_in[l])
        q, k, v, xr, gr, ga, gb = jnp.split(u, splits, axis=-1)
        ya = chunked_band_attention(q, k, v, rel_table[l]) @ w_attn_out[l]
        xc = causal_depthwise_conv(xr, conv_w[l], conv_b[l])
        hr = rg_lru(xc, w_rg_r[l], b_rg_r[l], w_rg_i[l], b_rg_i[l], rg_lambda[l])
        yb = (hr * jax.nn.gelu(gr)) @ w_rnn_out[l]
        gates = jax.nn.sigmoid(jnp.concatenate([ga, gb], axis=-1) + b_merge[l])
        g_a, g_b = jnp.split(gates, 2, axis=-1)
        h = h + (g_a * ya + g_b * yb) @ w_o[l]
        hn = rmsnorm(h, norm_ffn_g[l])
        gu = hn @ w_ffn_in[l]
        g, up = jnp.split(gu, 2, axis=-1)
        h = h + (jax.nn.silu(g) * up) @ w_ffn_out[l]
    return rmsnorm(h, final_norm_g)


GRID_W = 64
NEG_INF_2 = -1e30

NA_HEADS = 8
NA_HEAD_DIM = 64
NA_WIN_H = 8
NA_WIN_W = 16
NA_QBLOCK_W = 16
NA_BAND_W = NA_QBLOCK_W + NA_WIN_W
NA_WIDTH = NA_HEADS * NA_HEAD_DIM

MLA_HEADS = 8
MLA_QK_NOPE = 64
MLA_QK_ROPE = 32
MLA_V_DIM = 64
MLA_Q_LORA = 256
MLA_KV_LORA = 128
MLA_QBLOCK = 128
MLA_WIDTH = MLA_HEADS * MLA_V_DIM
ROPE_THETA = 10000.0

MIX_WIDTH = NA_WIDTH + MLA_WIDTH
D_IN = 3 * NA_WIDTH + MLA_Q_LORA + MLA_KV_LORA + MLA_QK_ROPE
D_FF_2 = 2816


def rms_norm(x, g):
    xf = x.astype(jnp.float32)
    y = xf * lax.rsqrt(jnp.mean(xf * xf, axis=-1, keepdims=True) + EPS)
    return (y * g.astype(jnp.float32)).astype(x.dtype)

def swiglu(h, w_gu, w_down):
    gate, up = jnp.split(h @ w_gu, 2, axis=-1)
    return (jax.nn.silu(gate) * up) @ w_down

def grid_rope_tables(seq):
    t = jnp.arange(seq)
    row = (t // GRID_W).astype(jnp.float32)
    col = (t % GRID_W).astype(jnp.float32)
    n_freq = MLA_QK_ROPE // 4
    inv_freq = 1.0 / (ROPE_THETA ** (jnp.arange(n_freq, dtype=jnp.float32) / n_freq))
    ang = jnp.concatenate([row[:, None] * inv_freq[None, :], col[:, None] * inv_freq[None, :]], axis=-1)
    return jnp.cos(ang), jnp.sin(ang)

def apply_rope(x, cos, sin):
    xf = x.astype(jnp.float32)
    x1, x2 = jnp.split(xf, 2, axis=-1)
    return jnp.concatenate([x1 * cos - x2 * sin, x2 * cos + x1 * sin], axis=-1).astype(x.dtype)

def neighbourhood_attention(q, k, v, rpb):
    B, S, H, D = q.shape
    R = S // GRID_W
    KH = min(NA_WIN_H, R)
    NCB = GRID_W // NA_QBLOCK_W
    rows = jnp.arange(R)
    row_start = jnp.clip(rows - KH // 2, 0, R - KH)
    key_rows = row_start[:, None] + jnp.arange(KH)
    c0 = jnp.arange(NCB) * NA_QBLOCK_W
    band_start = jnp.clip(c0 - NA_WIN_W // 2, 0, GRID_W - NA_BAND_W)
    key_cols = band_start[:, None] + jnp.arange(NA_BAND_W)
    q_cols = c0[:, None] + jnp.arange(NA_QBLOCK_W)
    win_start = jnp.clip(q_cols - NA_WIN_W // 2, 0, GRID_W - NA_WIN_W)
    kc = key_cols[:, None, :]
    col_mask = (kc >= win_start[..., None]) & (kc < win_start[..., None] + NA_WIN_W)
    row_off = key_rows - rows[:, None] + (NA_WIN_H - 1)
    col_off = jnp.clip(kc - q_cols[:, :, None] + (NA_WIN_W - 1), 0, 2 * NA_WIN_W - 2)
    bias = rpb.astype(jnp.float32)[:, row_off[:, None, None, :, None], col_off[None, :, :, None, :]]
    bias = bias.transpose(1, 2, 0, 3, 4, 5)
    bias = jnp.where(col_mask[:, None, :, None, :], bias, NEG_INF_2)
    qg = q.reshape(B, R, NCB, NA_QBLOCK_W, H, D)
    ridx = key_rows[:, None, :, None]
    cidx = key_cols[None, :, None, :]
    kg = k.reshape(B, R, GRID_W, H, D)[:, ridx, cidx]
    vg = v.reshape(B, R, GRID_W, H, D)[:, ridx, cidx]
    s = jnp.einsum('brnqhd,brnijhd->brnhqij', qg, kg).astype(jnp.float32) * (D ** -0.5)
    s = s + bias[None]
    sh = s.shape
    p = jax.nn.softmax(s.reshape(sh[:-2] + (sh[-2] * sh[-1],)), axis=-1).reshape(sh)
    o = jnp.einsum('brnhqij,brnijhd->brnqhd', p.astype(v.dtype), vg)
    return o.reshape(B, S, H * D)

def latent_attention(c_q, c_kv, k_rope, q_norm_g, w_uq, kv_norm_g, w_ukv, cos, sin):
    B, S, _ = c_q.shape
    H = MLA_HEADS
    q = (rms_norm(c_q, q_norm_g) @ w_uq).reshape(B, S, H, MLA_QK_NOPE + MLA_QK_ROPE)
    q_nope, q_rot = jnp.split(q, [MLA_QK_NOPE], axis=-1)
    kv = (rms_norm(c_kv, kv_norm_g) @ w_ukv).reshape(B, S, H, MLA_QK_NOPE + MLA_V_DIM)
    k_nope, v = jnp.split(kv, [MLA_QK_NOPE], axis=-1)
    q_rot = apply_rope(q_rot, cos[:, None, :], sin[:, None, :])
    k_rot = apply_rope(k_rope, cos, sin)
    scale = (MLA_QK_NOPE + MLA_QK_ROPE) ** -0.5
    nqb = S // MLA_QBLOCK

    def block(args):
        qn, qr = args
        s = (jnp.einsum('bqhd,bkhd->bhqk', qn, k_nope)
             + jnp.einsum('bqhd,bkd->bhqk', qr, k_rot)).astype(jnp.float32) * scale
        p = jax.nn.softmax(s, axis=-1)
        return jnp.einsum('bhqk,bkhd->bqhd', p.astype(v.dtype), v)

    qn_b = q_nope.reshape(B, nqb, MLA_QBLOCK, H, MLA_QK_NOPE).swapaxes(0, 1)
    qr_b = q_rot.reshape(B, nqb, MLA_QBLOCK, H, MLA_QK_ROPE).swapaxes(0, 1)
    o = lax.map(block, (qn_b, qr_b))
    return o.swapaxes(0, 1).reshape(B, S, H * MLA_V_DIM)

def second_inputs(seed: int = 0) -> dict:
    key = jax.random.key(seed)
    ks = iter(jax.random.split(key, 32))

    def w(shape, fan_in):
        return jax.random.normal(next(ks), shape, jnp.float32) * (fan_in ** -0.5)

    def gain(n):
        return 1.0 + 0.05 * jax.random.normal(next(ks), (DEPTH, n), jnp.float32)

    L = DEPTH
    return {
        "x": jax.random.normal(next(ks), (BATCH, SEQ, D_MODEL), jnp.float32),
        "ffn1_pre_g": gain(D_MODEL),
        "ffn1_w_gu": w((L, D_MODEL, 2 * D_FF_2), D_MODEL),
        "ffn1_w_down": w((L, D_FF_2, D_MODEL), D_FF_2),
        "ffn1_post_g": gain(D_MODEL),
        "mix_pre_g": gain(D_MODEL),
        "w_in": w((L, D_MODEL, D_IN), D_MODEL),
        "na_rpb": 0.1 * jax.random.normal(next(ks), (L, NA_HEADS, 2 * NA_WIN_H - 1, 2 * NA_WIN_W - 1), jnp.float32),
        "mla_q_norm_g": gain(MLA_Q_LORA),
        "mla_w_uq": w((L, MLA_Q_LORA, MLA_HEADS * (MLA_QK_NOPE + MLA_QK_ROPE)), MLA_Q_LORA),
        "mla_kv_norm_g": gain(MLA_KV_LORA),
        "mla_w_ukv": w((L, MLA_KV_LORA, MLA_HEADS * (MLA_QK_NOPE + MLA_V_DIM)), MLA_KV_LORA),
        "na_out_norm_g": gain(NA_WIDTH),
        "mla_out_norm_g": gain(MLA_WIDTH),
        "w_out": w((L, MIX_WIDTH, D_MODEL), MIX_WIDTH),
        "mix_post_g": gain(D_MODEL),
        "ffn2_pre_g": gain(D_MODEL),
        "ffn2_w_gu": w((L, D_MODEL, 2 * D_FF_2), D_MODEL),
        "ffn2_w_down": w((L, D_FF_2, D_MODEL), D_FF_2),
        "ffn2_post_g": gain(D_MODEL),
    }

def second_block(x, ffn1_pre_g, ffn1_w_gu, ffn1_w_down, ffn1_post_g, mix_pre_g, w_in, na_rpb,
              mla_q_norm_g, mla_w_uq, mla_kv_norm_g, mla_w_ukv, na_out_norm_g, mla_out_norm_g,
              w_out, mix_post_g, ffn2_pre_g, ffn2_w_gu, ffn2_w_down, ffn2_post_g):
    B, S, _ = x.shape
    cos, sin = grid_rope_tables(S)
    split_at = [NA_WIDTH, 2 * NA_WIDTH, 3 * NA_WIDTH,
                3 * NA_WIDTH + MLA_Q_LORA, 3 * NA_WIDTH + MLA_Q_LORA + MLA_KV_LORA]
    h = x
    for l in range(DEPTH):
        f = swiglu(rms_norm(h, ffn1_pre_g[l]), ffn1_w_gu[l], ffn1_w_down[l])
        h = h + 0.5 * rms_norm(f, ffn1_post_g[l])
        z = rms_norm(h, mix_pre_g[l]) @ w_in[l]
        q_na, k_na, v_na, c_q, c_kv, k_rope = jnp.split(z, split_at, axis=-1)
        hs = (B, S, NA_HEADS, NA_HEAD_DIM)
        o_na = neighbourhood_attention(q_na.reshape(hs), k_na.reshape(hs), v_na.reshape(hs), na_rpb[l])
        o_mla = latent_attention(c_q, c_kv, k_rope, mla_q_norm_g[l], mla_w_uq[l],
                                 mla_kv_norm_g[l], mla_w_ukv[l], cos, sin)
        mixed = jnp.concatenate([rms_norm(o_na, na_out_norm_g[l]),
                                 rms_norm(o_mla, mla_out_norm_g[l])], axis=-1) @ w_out[l]
        h = h + rms_norm(mixed, mix_post_g[l])
        f = swiglu(rms_norm(h, ffn2_pre_g[l]), ffn2_w_gu[l], ffn2_w_down[l])
        h = h + 0.5 * rms_norm(f, ffn2_post_g[l])
    return h


def setup_inputs(seed=0):
    out = dict(first_inputs(seed))
    for name, value in second_inputs(seed + 1).items():
        if name != "x":
            out[name + "_2"] = value
    return out


def reference(
    x, norm_mix_g, w_in, b_merge, rel_table, w_attn_out, conv_w, conv_b, w_rg_r, b_rg_r, w_rg_i,
    b_rg_i, rg_lambda, w_rnn_out, w_o, norm_ffn_g, w_ffn_in, w_ffn_out, final_norm_g,
    ffn1_pre_g_2, ffn1_w_gu_2, ffn1_w_down_2, ffn1_post_g_2, mix_pre_g_2, w_in_2, na_rpb_2,
    mla_q_norm_g_2, mla_w_uq_2, mla_kv_norm_g_2, mla_w_ukv_2, na_out_norm_g_2, mla_out_norm_g_2,
    w_out_2, mix_post_g_2, ffn2_pre_g_2, ffn2_w_gu_2, ffn2_w_down_2, ffn2_post_g_2,
):
    x = first_block(
        x, norm_mix_g, w_in, b_merge, rel_table, w_attn_out, conv_w, conv_b, w_rg_r, b_rg_r,
        w_rg_i, b_rg_i, rg_lambda, w_rnn_out, w_o, norm_ffn_g, w_ffn_in, w_ffn_out,
        final_norm_g,
    )
    return second_block(
        x, ffn1_pre_g_2, ffn1_w_gu_2, ffn1_w_down_2, ffn1_post_g_2, mix_pre_g_2, w_in_2,
        na_rpb_2, mla_q_norm_g_2, mla_w_uq_2, mla_kv_norm_g_2, mla_w_ukv_2, na_out_norm_g_2,
        mla_out_norm_g_2, w_out_2, mix_post_g_2, ffn2_pre_g_2, ffn2_w_gu_2, ffn2_w_down_2,
        ffn2_post_g_2,
    )


_drawn_inputs = setup_inputs


def setup_inputs(seed=0):
    import zlib

    import numpy as np

    out = dict(_drawn_inputs(seed))
    spreads = {}
    factors = {'b_merge': 31.612, 'b_rg_r': 57.103, 'b_rg_i': 39.148, 'ffn2_post_g_2': 3.29}
    for name, (base, spread) in spreads.items():
        noise = np.random.default_rng([zlib.crc32(name.encode()), seed]).standard_normal(out[name].shape)
        drawn = base * np.exp(spread * noise) if base else spread * noise
        out[name] = __import__('jax').numpy.asarray(drawn.astype(out[name].dtype))
    for name, factor in factors.items():
        out[name] = (out[name] * factor).astype(out[name].dtype)
    return out
```

```python
import numpy as np

import concourse.bass as bass
from concourse import mybir

F32 = mybir.dt.float32
F32R = mybir.dt.float32r
BF16 = mybir.dt.bfloat16
ACT = mybir.ActivationFunctionType
ALU = mybir.AluOpType

P = 128
D = 1024
T = 256
MT = T // P
KT = D // P
W = 512
RING = 4
SLAB = 1024
HEADS = 16
HD = 64
FF = 2816
FT = FF // P
FG = FF // 256
EPS = 1e-6
MASKED = -1e30
MLA_SCALE = 96 ** -0.5
GELU_C = 0.7978845608028654
CHUNK = 64


def starts(parts):
    out, at = {}, 0
    for name, n in parts:
        out[name] = at
        at += n
    out["end"] = at
    return out


S = starts([("in", 56), ("rnn", 8), ("attn", 8), ("o", 8), ("f1i", 4 * FG), ("f1o", 22), ("f2i", 4 * FG),
            ("f2o", 22), ("in2", 16), ("uq", 2), ("ukv", 1), ("out2", 8), ("f3i", 4 * FG), ("f3o", 22)])
G = starts([("in", 14), ("rnn", 2), ("attn", 2), ("o", 2), ("f1i", FG), ("f1o", 2), ("f2i", FG), ("f2o", 2),
            ("in2", 4), ("uq", 2), ("ukv", 2), ("na", 1), ("mla", 1), ("top", 2), ("bot", 2), ("f3i", FG), ("f3o", 2)])
X = starts([("x", 4), ("par", 1), ("xg", 8), ("gate", 8), ("qk", 8), ("p1", 16), ("at", 4), ("mt", 4), ("h1", 4),
            ("f1", FG), ("h2", 4), ("f2", FG), ("h3", 4), ("c", 2), ("nqk", 4), ("pna0", 6), ("mqk", 8),
            ("pna1", 2), ("pm0", 3), ("ona", 2), ("pm1", 5), ("omla", 2), ("h4", 4), ("f3", FG)])
HI = starts([("x", 8), ("rg", 1), ("at", 4), ("mt", 4), ("h1", 8), ("f1", FG), ("h2", 8), ("f2", FG), ("h3", 8),
             ("c", 3), ("ona", 4), ("omla", 4), ("h4", 8), ("f3", FG)])
STATS = [("x", D, 1), ("h1", D, 4), ("h2", D, 1), ("x2", D, 4), ("f2", D, 4), ("h3", D, 1), ("q", 256, 1),
         ("kv", 128, 1), ("na", 512, 1), ("mla", 512, 1), ("mix", D, 1), ("h4", D, 4), ("f3", D, 4)]
ST = {name: n for n, (name, _, _) in enumerate(STATS)}
SQUARES = []
for _n in ("x",):
    SQUARES += [(_n, 0, m) for m in range(MT)]
for _n in ("h1", "h2"):
    SQUARES += [(_n, c, m) for c in range(2) for m in range(MT)]
SQUARES += [("x2", 0, m) for m in range(MT)]
for _n in ("f2", "h3"):
    SQUARES += [(_n, c, m) for c in range(2) for m in range(MT)]
SQUARES += [(_n, 0, m) for _n in ("q", "kv", "na", "mla") for m in range(MT)]
for _n in ("mix", "h4", "f3"):
    SQUARES += [(_n, c, m) for c in range(2) for m in range(MT)]
SQ = {key: n for n, key in enumerate(SQUARES)}
TWO_HALVES = {key[0] for key in SQUARES if key[1] == 1}

PAR = starts([("mix_g", 8), ("ffn_g", 8), ("fin_g", 8), ("f2_g", 8), ("mix2_g", 8), ("f3_g", 8), ("conv_w", 32),
              ("conv_b", 8), ("b_r", 8), ("b_i", 8), ("lam", 8), ("q_g", 2), ("kv_g", 1), ("na_g", 4), ("mla_g", 4)])


def build(nc, a, out):
    top = [16512]

    def place(name, shape, dt, at=None):
        size = int(np.prod(shape[1:])) * (2 if dt == BF16 else 4)
        size = (size + 31) // 32 * 32
        if at is None:
            at = top[0]
            top[0] += size
        return nc.alloc_sbuf_tensor_at(name, shape, dt, offset=at)

    def size_of(*dims):
        return 4 * int(np.prod(dims))

    w_raw = place("w_raw", [P, RING, SLAB], F32)
    w_hi = place("w_hi", [P, RING, SLAB], F32R)
    w_lo = place("w_lo", [P, RING, SLAB], F32R)
    h = place("h", [P, MT, D], F32)
    xt_hi = place("xt_hi", [P, KT, T], F32R)
    xt_lo = place("xt_lo", [P, KT, T], F32R)
    ident = place("ident", [P, P], F32)
    par_rows = place("par_rows", [P, P], F32)
    par = place("par", [P, P], F32)
    gain_x = place("gain_x", [P, KT], F32)
    small = place("small", [P, 16, KT], F32)
    ssq = place("ssq", [P, len(STATS), 2, MT], F32)
    ms = place("ms", [P, len(STATS), MT], F32)
    rs = place("rs", [P, len(STATS), MT], F32)
    coef = place("coef", [P, 8, MT], F32)
    minus_half = place("minus_half", [P, MT], F32)
    junk = place("junk", [P, D], BF16)
    base = top[0]

    u = place("u", [P, 7, MT, D], F32)
    xrT_at = top[0]
    xrT = place("xrT", [P, KT, T + 4], F32)
    ti = place("ti", [P, KT, T], F32)
    yt_hi = place("yt_hi", [P, KT, T], F32R, at=xrT_at)
    yt_lo = place("yt_lo", [P, KT, T], F32R, at=xrT_at + size_of(KT, T))
    grT = place("grT", [P, KT, T], F32)
    qkT = place("qkT", [P, 2 * KT, T], F32)
    bias1 = place("bias1", [P, 2, 4, T], F32)
    blockdiag = place("blockdiag", [P, 16, P], F32)
    b_merge = place("b_merge", [P, 2 * D], F32)
    q_stage = place("q_stage", [P, 4, T], F32)
    sb1 = place("sb1", [P, 2, 384], F32)
    pt1 = place("pt1", [P, 2, 384], F32)
    ext_sb = nc.alloc_sbuf_tensor_at("ext_sb", [HEADS, 384], F32, offset=top[0] - size_of(2, 384))
    mx1 = place("mx1", [P, 2, 4], F32)
    carrier = place("carrier", [P, 8], F32)
    free_marks = place("free_marks", [P, 8], F32)
    nm1 = place("nm1", [P, 2, 4], F32)
    sum1 = place("sum1", [P, 2, 4], F32)
    inv1 = place("inv1", [P, 2, 4], F32)
    assert top[0] <= 229368, top[0]
    flat = lambda t: t[:, :, :].rearrange("p a b -> p (a b)")
    xcT = u[:, 0].rearrange("p m n -> p (m n)").rearrange("p (k t) -> p k t", t=T)
    trT = u[:, 1].rearrange("p m n -> p (m n)").rearrange("p (k t) -> p k t", t=T)
    gel = u[:, 5].rearrange("p m n -> p (m n)").rearrange("p (k t) -> p k t", t=T)
    sq = u[:, 6].rearrange("p m n -> p (m n)").rearrange("p (k t) -> p k t", t=T)
    att = u[:, 2]
    merged = u[:, 3]

    top[0] = base
    hid_hi = place("hid_hi", [P, FT, T], F32R)
    hid_lo = place("hid_lo", [P, FT, T], F32R)
    th = place("th", [P, MT, 256], F32)
    u1 = place("u1", [P, MT, 256], F32)
    hid = place("hid", [P, 2, MT, 256], F32)
    below = top[0]
    f = place("f", [P, MT, D], F32)
    row_gain = place("row_gain", [P, 4, D], F32)
    ext2_sb = place("ext2_sb", [8, 7, P], F32)
    rpb_sb = place("rpb_sb", [8, 15, 31], F32)
    bias2 = place("bias2", [P, 8, 6, 64], F32)
    na_mask = place("na_mask", [P, 64], F32)
    cos = place("cos", [P, MT, 16], F32)
    sin = place("sin", [P, MT, 16], F32)

    u2 = place("u2", [P, MT, 1952], F32)
    mqT = place("mqT", [96, 8, T], F32)
    mkT = place("mkT", [96, 8, T], F32)
    mx2 = place("mx2", [P, 2, 2], F32)
    nm2 = place("nm2", [P, 2, 2], F32)
    sum2 = place("sum2", [P, 2, MT, 8], F32)
    inv2 = place("inv2", [P, 2, MT, 8], F32)
    assert top[0] <= 229368, top[0]
    top[0] = base
    nqk = place("nqk", [P, 8, T], F32)
    c_hi = place("c_hi", [P, 3, T], F32R)
    c_lo = place("c_lo", [P, 3, T], F32R)
    mq = place("mq", [P, MT, 8, 96], F32)
    mk = place("mk", [P, MT, 8, 96], F32)
    mv = place("mv", [P, MT, 8, 64], F32)
    o2 = place("o2", [P, 2, MT, 512], F32)
    rope = place("rope", [P, 4, MT, 8, 16], F32)
    kr = place("kr", [P, 4, MT, 16], F32)
    sb2 = place("sb2", [P, 2, W], F32)
    pt2 = place("pt2", [P, 2, W], F32)
    assert top[0] <= below, (top[0], below)

    acc = [nc.alloc_psum_tensor(f"acc{b}", [P, W], F32) for b in range(4)]
    tp = [nc.alloc_psum_tensor(f"tp{b}", [P, W], F32) for b in range(2)]
    sc = [nc.alloc_psum_tensor(f"sc{b}", [P, W], F32) for b in range(2)]

    ext_dram = nc.dram_tensor("ext_dram", [HEADS, 384], F32)
    ext2_dram = nc.dram_tensor("ext2_dram", [8, 7, P], F32)

    sem = nc.alloc_semaphore
    raw_landed = [sem(f"raw_landed{b}") for b in range(RING)]
    hi_done = [sem(f"hi_done{b}") for b in range(RING)]
    lo_done = [sem(f"lo_done{b}") for b in range(RING)]
    slab_used = [sem(f"slab_used{b}") for b in range(RING)]
    acc0_full = [sem(f"acc0_full{b}") for b in range(2)]
    acc_drained = [sem(f"acc_drained{b}") for b in range(4)]
    tp_full = [sem(f"tp_full{b}") for b in range(2)]
    tp_free = [sem(f"tp_free{b}") for b in range(2)]
    hi_written = sem("hi_written")
    ssq_done, ms_done, rs_done = sem("ssq_done"), sem("ms_done"), sem("rs_done")
    x_landed = [sem("x_landed0"), sem("x_landed1")]
    ident_landed, gain_x_landed, par_landed = sem("ident_landed"), sem("gain_x_landed"), sem("par_landed")
    par_done = sem("par_done")
    bd_zero, bd_landed, q_zero = sem("bd_zero"), sem("bd_landed"), sem("q_zero")
    merge_landed = sem("merge_landed")
    table_landed, ext_done, ext_stored, bias_landed = sem("table_landed"), sem("ext_done"), sem("ext_stored"), [sem("bias_landed0"), sem("bias_landed1")]
    set_up, warm = sem("set_up"), sem("warm")
    consts_ready = sem("consts_ready")
    abs_lam, exp_lam = sem("abs_lam"), sem("exp_lam")
    conv_done = sem("conv_done")
    gates_done, decay_done = sem("gates_done"), sem("decay_done")
    mult2_done, mult_done, bx_done, rec_done = sem("mult2_done"), sem("mult_done"), sem("bx_done"), sem("rec_done")
    gelu_arg, gelu_tanh, rg_out = sem("gelu_arg"), sem("gelu_tanh"), sem("rg_out")
    yt_ready = sem("yt_ready")
    staged, scores_done, ttr_done, negmax_done = sem("staged"), sem("scores_done"), sem("ttr_done"), sem("negmax_done")
    probs_done, pv_done, inv_done, o_drained = sem("probs_done"), sem("pv_done"), sem("inv_done"), sem("o_drained")
    gate_tanh = sem("gate_tanh")
    m_ready = sem("m_ready")
    coef_done = sem("coef_done")
    x2_ready = sem("x2_ready")
    tanh_done, u1_done = sem("tanh_done"), sem("u1_done")
    rows_landed, late_landed = sem("rows_landed"), sem("late_landed")
    ext2_done, ext2_stored, bias2_landed, bias2_ready = sem("ext2_done"), sem("ext2_stored"), sem("bias2_landed"), sem("bias2_ready")
    h_new = sem("h_new")
    kv_half = sem("kv_half")
    mk_nope = sem("mk_nope")
    rope_q, rope_k = sem("rope_q"), sem("rope_k")
    scores2, ttr2, max2, negmax2, probs2, pv2 = (sem("scores2"), sem("ttr2"), sem("max2"), sem("negmax2"), sem("probs2"), sem("pv2"))
    inv2_done = sem("inv2_done")
    top_added = sem("top_added")
    out_ready, out_stored = sem("out_ready"), sem("out_stored")
    dve_step, pool_step = sem("dve_step"), sem("pool_step")

    def n_of(n, i=0, per=0):
        return n if isinstance(i, int) and i == 0 else i * per + n

    def wait(e, s, n, i=0, per=0):
        assert n > 0 or isinstance(i, int), "a wait in a loop starts above zero"
        if not (isinstance(i, int) and n + i * per <= 0):
            e.wait_ge(s, n_of(n, i, per))

    def wait_acc(e, g, m, last_slab, i=0, slab_turns=0, acc_turns=0):
        if m == 0:
            wait(e, acc0_full[g % 2], g // 2 + 1, i, acc_turns)
        else:
            wait(e, slab_used[last_slab % RING], last_slab // RING + 1, i, slab_turns)

    def wait_drained(e, g, m, i=0, turns=0):
        wait(e, acc_drained[g % 2 * 2 + m], g // 2 + 2, i, turns)

    def wait_bank(e, g, m, i=0, turns=0):
        wait(e, acc_drained[g % 2 * 2 + m], g // 2 + 1, i, turns)

    def wait_tp_full(e, x, i=0, turns=0):
        wait(e, tp_full[x % 2], x // 2 + 1, i, turns)

    def wait_tp_free(e, x, i=0, turns=0):
        wait(e, tp_free[x % 2], x // 2 + 1, i, turns)

    def prob_use(n):
        for name, first, count in (("pna0", 0, 6), ("pna1", 6, 2), ("pm0", 8, 3), ("pm1", 11, 5)):
            if first <= n < first + count:
                return X[name] + n - first

    def two(bank, parts=P):
        return bank[0:parts, :].rearrange("p (k t) -> p k t", k=2)

    block = nc.Block()
    with block:
        @block.sync
        def _(sp):
            def slab(s, halves, i=0, turns=0):
                if s >= RING or turns:
                    wait(sp, lo_done[s % RING], s // RING, i, turns)
                for dst, src in halves:
                    sp.dma_start(dst, src).then_inc(raw_landed[s % RING], 32 // len(halves))

            def rect(s, w, row, col, n=W):
                dst = w_raw[:, s % RING, 0:2 * n].rearrange("p (j n) -> p j n", j=2)
                return [(dst, w.rearrange("(r p) n -> p r n", p=P)[:, row // P:row // P + 2, bass.ds(col, n)])]

            def gate_up(s, w, row, col):
                src = w.rearrange("(r p) (g n) -> r p g n", p=P, g=2)
                return [(w_raw[:, s % RING, j * W:(j + 1) * W].rearrange("p (g n) -> p g n", g=2),
                         src[row // P + j][:, :, bass.ds(col, 256)]) for j in range(2)]

            def rows_k(w, s0, groups, col0):
                with sp.Fori(0, groups) as c:
                    for q in range(4):
                        s = s0 + q
                        slab(s, rect(s, w, 256 * q, c * W + col0), c, 1)

            def ffn_in(w, s0):
                with sp.Fori(0, FG) as c:
                    for q in range(4):
                        slab(s0 + q, gate_up(s0 + q, w, 256 * q, c * 256), c, 1)

            def ffn_out(w, s0, after={}):
                for n in range(22):
                    slab(s0 + n, rect(s0 + n, w, 256 * (n % 11), n // 11 * W))
                    if n in after:
                        after[n]()

            xv = a["x"].rearrange("b (m p) d -> p (b m) d", p=P)
            sp.dma_start(h[:, 0, :], xv[:, 0, :]).then_inc(x_landed[0], 16)
            sp.dma_start(h[:, 1, :], xv[:, 1, :]).then_inc(x_landed[1], 16)
            w_in = a["w_in"][0]
            for q in range(4):
                slab(q, rect(q, w_in, 256 * q, 3 * D))
            for name, key in (("mix_g", "norm_mix_g"), ("ffn_g", "norm_ffn_g"), ("fin_g", "final_norm_g"),
                              ("f2_g", "ffn1_pre_g_2"), ("mix2_g", "mix_pre_g_2"), ("f3_g", "ffn2_pre_g_2"),
                              ("conv_w", "conv_w"), ("conv_b", "conv_b"), ("b_r", "b_rg_r"), ("b_i", "b_rg_i"),
                              ("lam", "rg_lambda"), ("q_g", "mla_q_norm_g_2"), ("kv_g", "mla_kv_norm_g_2"),
                              ("na_g", "na_out_norm_g_2"), ("mla_g", "mla_out_norm_g_2")):
                v = a[key]
                v = v.rearrange("(r c) -> r c", c=P) if len(v.shape) == 1 else \
                    v.rearrange("a (r c) -> (a r) c", c=P) if len(v.shape) == 2 else \
                    v.rearrange("a b (r c) -> (a b r) c", c=P)
                sp.dma_start(par_rows[PAR[name]:PAR[name] + v.shape[0], :], v).then_inc(par_landed, 16)
            rows_k(w_in, 4, 3, 3 * D + W)
            sp.wait_ge(bd_zero, 1)
            for n, key in enumerate(("w_rg_r", "w_rg_i")):
                wv = a[key][0].rearrange("(k two) d e -> two d k e", two=2)
                for side in range(2):
                    sp.dma_start(blockdiag[64 * side:64 * side + 64, 8 * n:8 * n + 8, 64 * side:64 * side + 64],
                                  wv[side]).then_inc(bd_landed, 16)
            sp.dma_start(ext_sb[:, 0:256], a["rel_table"][0][:, 1:257]).then_inc(table_landed, 16)
            sp.dma_start(b_merge[:], a["b_merge"][0].partition_broadcast(P)).then_inc(merge_landed, 16)
            rows_k(w_in, 16, 6, 0)
            sp.wait_ge(ext_done, 1)
            sp.dma_start(ext_dram.ap(), ext_sb[:]).then_inc(ext_stored, 16)
            sp.wait_ge(ext_stored, 16)
            strips = bass.AP(ext_dram, 0, [[1, P], [384, HEADS], [1, T]])
            with sp.Fori(0, 2) as i:
                for g in range(2):
                    for q in range(4):
                        s = 40 + 4 * g + q
                        slab(s, rect(s, w_in, 256 * q, i * D + (5 * D + g * W)), i, 2)
                    wait(sp, ttr_done, 8 * g + 1, i, 16)
                    heads = strips[:, bass.ds(i * 8 + 4 * g, 4), :]
                    sp.dma_start(bias1[0:CHUNK, g, :, CHUNK:T], heads[0:CHUNK, :, CHUNK:T]).then_inc(bias_landed[g], 16)
                    sp.dma_start(bias1[CHUNK:P, g], heads[CHUNK:P]).then_inc(bias_landed[g], 16)
            rows_k(a["w_rnn_out"][0], S["rnn"], 2, 0)
            rows_k(a["w_attn_out"][0], S["attn"], 2, 0)
            rows_k(a["w_o"][0], S["o"], 2, 0)
            ffn_in(a["w_ffn_in"][0], S["f1i"])
            for n, name in enumerate(("final_norm_g", "ffn1_post_g_2", "mix_post_g_2", "ffn2_post_g_2")):
                if n == 0:
                    for m in range(MT):
                        wait_drained(sp, G["o"] + 1, m)
                v = a[name] if name == "final_norm_g" else a[name][0]
                sp.dma_start(row_gain[:, n, :], v.partition_broadcast(P)).then_inc(rows_landed, 16)
            sp.dma_start(na_mask[0:64, :], a["c_mask"]).then_inc(late_landed, 16)
            sp.dma_start(na_mask[64:128, :], a["c_mask"]).then_inc(late_landed, 16)
            sp.dma_start(cos[:], a["c_cos"].rearrange("(m p) n -> p m n", p=P)).then_inc(late_landed, 16)
            sp.dma_start(sin[:], a["c_sin"].rearrange("(m p) n -> p m n", p=P)).then_inc(late_landed, 16)
            sp.dma_start(rpb_sb[:], a["na_rpb_2"][0]).then_inc(late_landed, 16)

            def store_ext2():
                sp.wait_ge(ext2_done, 1)
                sp.dma_start(ext2_dram.ap(), ext2_sb[:]).then_inc(ext2_stored, 16)

            def load_bias2(hd):
                sp.wait_ge(ext2_stored, 16)
                for qr in range(2):
                    src = bass.AP(ext2_dram, (hd * 7 + 1 - qr) * P, [[1, 64], [P, 6], [1, 64]])
                    sp.dma_start(bias2[64 * qr:64 * qr + 64, hd], src).then_inc(bias2_landed, 16)

            ffn_out(a["w_ffn_out"][0], S["f1o"],
                    after={10: store_ext2, **{12 + hd: lambda hd=hd: load_bias2(hd) for hd in range(8)}})
            ffn_in(a["ffn1_w_gu_2"][0], S["f2i"])
            ffn_out(a["ffn1_w_down_2"][0], S["f2o"])
            w2 = a["w_in_2"][0]
            for q in range(4):
                slab(S["in2"] + q, rect(S["in2"] + q, w2, 256 * q, 1536, 416))
            rows_k(w2, S["in2"] + 4, 3, 0)
            slab(S["uq"], rect(S["uq"], a["mla_w_uq_2"][0], 0, 0))
            slab(S["uq"] + 1, rect(S["uq"] + 1, a["mla_w_uq_2"][0], 0, W, 256))
            slab(S["ukv"], [(w_raw[:, S["ukv"] % RING, :], a["mla_w_ukv_2"][0])])
            for q in range(8):
                half, c, r = q // 4, q // 2 % 2, q % 2
                s = S["out2"] + q
                slab(s, rect(s, a["w_out_2"][0], 512 * half + 256 * r, c * W))
            ffn_in(a["ffn2_w_gu_2"][0], S["f3i"])
            ffn_out(a["ffn2_w_down_2"][0], S["f3o"])
            ov = out.rearrange("b (m p) d -> p (b m) d", p=P)
            for n in range(4):
                c, m = n // 2, n % 2
                sp.wait_ge(out_ready, n + 1)
                sp.dma_start(ov[:, m, c * W:(c + 1) * W], h[:, m, c * W:(c + 1) * W]).then_inc(out_stored, 16)
            sp.wait_ge(out_stored, 64)

        @block.scalar
        def _(act):
            def feed(s, n=1, i=0, turns=0):
                for q in range(s, min(s + n, S["end"])):
                    b = q % RING
                    wait(act, raw_landed[b], 32 * (q // RING + 1), i, 32 * turns)
                    wait(act, slab_used[b], q // RING, i, turns)
                    act.activation(w_hi[:, b, :], w_raw[:, b, :], ACT.Copy).then_inc(hi_done[b], 1)

            def square(stat, c, m, src):
                n = SQ[stat, c, m]
                wait(act, ssq_done, n) if n > 0 else act.wait_ge(warm, 1)
                act.activation(junk[:, 0:src.free_size()], src, ACT.Square,
                               accum_out=ssq[:, ST[stat], c, m:m + 1]).then_inc(ssq_done, 1)

            def split(x, tiles, gain, dst, scale=1.0, i=0, turns=0):
                wait_tp_full(act, x, i, turns)
                if gain is None:
                    act.activation(dst, two(tp[x % 2]), ACT.Copy, scale=scale).then_inc(hi_written, 1)
                else:
                    for n, k in enumerate(tiles):
                        act.activation(dst[:, k, :], tp[x % 2][:, n * T:(n + 1) * T], ACT.Copy,
                                       scale=gain[:, k:k + 1]).then_inc(hi_written, 1)

            act.dma_start(ident[:], a["c_ident"]).then_inc(ident_landed, 16)
            with nc.allow_non_contiguous_dma(reason="a column of gains"):
                act.dma_start(gain_x[:], a["norm_mix_g"][0].rearrange("(k p) -> p k", p=P)).then_inc(gain_x_landed, 16)
            act.wait_ge(set_up, 1)
            act.activation(junk[:, 0:MT], minus_half[:], ACT.Exp).then_inc(warm, 1)
            act.wait_ge(gain_x_landed, 16)
            for n in range(4):
                split(X["x"] + n, (2 * n, 2 * n + 1), gain_x, xt_hi)
                if n > 0:
                    feed(n - 1, 1)
            feed(3, 1)
            for m in range(MT):
                square("x", 0, m, h[:, m, :])
            with act.Fori(0, 2) as i:
                feed(4, 8, i, 2)
            act.wait_ge(set_up, 2)
            for n in range(4):
                x = X["xg"] + 2 * n
                wait_tp_full(act, x)
                act.activation(xrT[:, 2 * n:2 * n + 2, 3:3 + T],
                               two(tp[x % 2]), ACT.Copy).then_inc(tp_free[x % 2], 1)
            act.wait_ge(abs_lam, 1)
            act.activation(small[:, 1, :], small[:, 0, :], ACT.Exp, scale=-1.0).then_inc(exp_lam, 1)
            feed(20, 11)
            act.wait_ge(consts_ready, 1)
            for n in range(KT):
                x = X["gate"] + n
                wait_tp_full(act, x)
                act.activation(trT[:, n, :], tp[x % 2][:, 0:T], ACT.Tanh, scale=0.5,
                               bias=small[:, 8, n:n + 1]).then_inc(gates_done, 1)
                act.activation(ti[:, n, :], tp[x % 2][:, T:2 * T], ACT.Tanh, scale=0.5,
                               bias=small[:, 9, n:n + 1]).then_inc(tp_free[x % 2], 1)
            act.wait_ge(conv_done, KT)
            for n in range(KT):
                act.wait_ge(gates_done, n + 1)
                act.activation(xrT[:, n, 0:T], trT[:, n, :], ACT.Exp, scale=small[:, 7, n:n + 1],
                               bias=small[:, 7, n:n + 1]).then_inc(decay_done, 1)
                act.activation(trT[:, n, :], trT[:, n, :], ACT.Tanh, scale=small[:, 6, n:n + 1],
                               bias=small[:, 6, n:n + 1]).then_inc(decay_done, 1)
                if n % 2 and n < 7:
                    feed(31 + n // 2, 1)
            feed(34, 1)
            act.wait_ge(gelu_arg, 3)
            act.activation(gel, gel, ACT.Tanh, scale=GELU_C).then_inc(gelu_tanh, 1)
            feed(35, 1)
            act.wait_ge(mult2_done, 2)
            act.activation(sq, sq, ACT.Sqrt).then_inc(mult_done, 1)
            feed(36, 2)
            for n in range(4):
                x = X["qk"] + 2 * n
                wait_tp_full(act, x)
                act.activation(qkT[:, 2 * n:2 * n + 2, :], two(tp[x % 2]),
                               ACT.Copy, scale=HD ** -0.5).then_inc(tp_free[x % 2], 1)
                feed((38, 39, 41, 42)[n], (1, 2, 1, 1)[n])
            act.wait_ge(rg_out, 1)
            act.activation(flat(yt_hi), trT.rearrange("p k t -> p (k t)"), ACT.Copy).then_inc(hi_written, 1)
            feed(43, 1)
            def exps1(par_, r, i):
                for hh in range(2):
                    wait(act, negmax_done, 2 * par_ + r + 1, i, 4)
                    for m in range(MT):
                        cols = slice(0, P) if m == 0 else slice(P, 384)
                        v = sb1[:, hh, cols]
                        ins = act.activation(v, v, ACT.Exp, bias=nm1[:, r, 2 * hh + m:2 * hh + m + 1],
                                             accum_out=sum1[:, r, 2 * hh + m:2 * hh + m + 1])
                    ins.then_inc(probs_done, 1)

            def probs_T1(par_, r, i):
                for hh in range(2):
                    x = X["p1"] + 4 * par_ + 2 * r + hh
                    wait_tp_full(act, x, i, 4)
                    act.activation(pt1[:, hh, :], tp[x % 2][:, 0:384], ACT.Copy).then_inc(tp_free[x % 2], 1)

            with act.Fori(0, 2) as i:
                for g in range(2):
                    s = 44 + 4 * g
                    exps1(g, 0, i)
                    feed(s, 2, i, 2)
                    probs_T1(g, 0, i)
                    exps1(g, 1, i)
                    feed(s + 2, 1, i, 2)
                    probs_T1(g, 1, i)
                    feed(s + 3, 1, i, 2)
                    for m in range(MT):
                        wait_drained(act, G["in"] + 10 + g, m, i, 1)
                        v = u[:, bass.ds(i + 5, 1), m, g * W:(g + 1) * W]
                        act.activation(v, v, ACT.Tanh, scale=0.5).then_inc(gate_tanh, 1)
            feed(S["rnn"] + 4, 4)
            for n in range(4):
                split(X["at"] + n, None, None, xt_hi[:, 2 * n:2 * n + 2, :])
                if n == 1:
                    feed(S["rnn"] + 8, 1)
            feed(S["rnn"] + 9, 3)
            feed(S["attn"] + 4, 7)
            for n in range(2):
                split(X["mt"] + n, None, None, yt_hi[:, 2 * n:2 * n + 2, :], 0.5)
            feed(S["attn"] + 11, 2)
            for n in range(2, 4):
                split(X["mt"] + n, None, None, yt_hi[:, 2 * n:2 * n + 2, :], 0.5)
            feed(S["o"] + 5, 3)
            for m in range(MT):
                wait_drained(act, G["o"], m)
                square("h1", 0, m, h[:, m, 0:W])
            feed(S["o"] + 8, 3)
            ffn_g = par[:, PAR["ffn_g"]:PAR["ffn_g"] + KT]
            for n in range(2):
                split(X["h1"] + n, (2 * n, 2 * n + 1), ffn_g, xt_hi)
            feed(S["o"] + 11, 1)

            def ffn(s_in, s_out, g_in, x_hid, x_h, gain, stat, before, half1, hr, after_first):
                before()
                feed(s_in + 4, 1)
                if x_h is not None:
                    for n in range(2, 4):
                        split(x_h + n, (2 * n, 2 * n + 1), gain, xt_hi)
                feed(s_in + 5, 1)
                half1()
                feed(s_in + 6, 1)
                after_first()
                feed(s_in + 7, 1)

                def tanhs(g, i=0):
                    for m in range(MT):
                        wait_acc(act, g_in + g, m, s_in + 4 * g + 3, i, 2, 1)
                        wait_drained(act, g_in + g - 1, m, i, 1)
                        act.activation(th[:, m, :], acc[(g_in + g) % 2 * 2 + m][:, 0:256], ACT.Tanh,
                                       scale=hr[:, m:m + 1]).then_inc(tanh_done, 1)

                wait(act, rs_done if stat is not None else coef_done, stat if stat is not None else 2)
                tanhs(0)
                with act.Fori(0, (FG - 1) // 2) as i:
                    for q in range(2):
                        g = 1 + q
                        feed(s_in + 4 * g + 4, 2, i, 2)
                        split(x_hid + g - 1, None, None, hid_hi[:, bass.ds(i * 4 + 2 * (g - 1), 2), :], 1.0, i, 1)
                        feed(s_in + 4 * g + 6, 2, i, 2)
                        tanhs(g, i)
                feed(s_out + 4, 2)
                split(x_hid + FG - 1, None, None, hid_hi[:, FT - 2:FT, :])

            def squares_h(stat, c, g_o):
                for m in range(MT):
                    wait_drained(act, g_o, m)
                    square(stat, c, m, h[:, m, c * W:(c + 1) * W])

            ffn(S["f1i"], S["f1o"], G["f1i"], X["f1"], X["h1"], ffn_g, ST["h1"] + 1,
                lambda: squares_h("h1", 1, G["o"] + 1), lambda: None, rs[:, ST["h1"]], lambda: None)
            feed(S["f1o"] + 6, 9)
            squares_h("h2", 0, G["f1o"])
            feed(S["f1o"] + 15, 7)
            f2_gain = small[:, 11, :]
            for n in range(2):
                split(X["h2"] + n, (2 * n, 2 * n + 1), f2_gain, xt_hi)
            feed(S["f1o"] + 22, 4)

            def second():
                for m in range(MT):
                    act.wait_ge(x2_ready, m + 1)
                    square("x2", 0, m, h[:, m, :])

            ffn(S["f2i"], S["f2o"], G["f2i"], X["f2"], X["h2"], f2_gain, None,
                lambda: squares_h("h2", 1, G["f1o"] + 1), lambda: None, coef[:, 1], second)

            def post_squares(stat, c, g, last_slab):
                for m in range(MT):
                    wait_acc(act, g, m, last_slab)
                    square(stat, c, m, acc[g % 2 * 2 + m][:, :])

            feed(S["f2o"] + 6, 9)
            post_squares("f2", 0, G["f2o"], S["f2o"] + 10)
            feed(S["f2o"] + 15, 11)
            post_squares("f2", 1, G["f2o"] + 1, S["f2o"] + 21)
            mix2_g = par[:, PAR["mix2_g"]:PAR["mix2_g"] + KT]
            for n in range(2):
                split(X["h3"] + n, (2 * n, 2 * n + 1), mix2_g, xt_hi)
            feed(S["in2"] + 4, 1)
            split(X["h3"] + 2, (4, 5), mix2_g, xt_hi)
            feed(S["in2"] + 5, 1)
            split(X["h3"] + 3, (6, 7), mix2_g, xt_hi)
            for c in range(2):
                for m in range(MT):
                    square("h3", c, m, h[:, m, c * W:(c + 1) * W])
            feed(S["in2"] + 6, 4)
            for stat, c0, n in (("q", 1536, 256), ("kv", 1792, 128)):
                for m in range(MT):
                    wait_drained(act, G["in2"], m)
                    square(stat, 0, m, u2[:, m, c0:c0 + n])
            split(X["c"], (0, 1), par[:, PAR["q_g"]:PAR["q_g"] + 2], c_hi)
            split(X["c"] + 1, (2,), par[:, PAR["kv_g"] - 2:PAR["kv_g"] + 1], c_hi)
            feed(S["in2"] + 10, 8)
            for n in range(2):
                x = X["nqk"] + 2 * n
                wait_tp_full(act, x)
                act.activation(nqk[:, 2 * n:2 * n + 2, :], two(tp[x % 2]),
                               ACT.Copy, scale=HD ** -0.5).then_inc(tp_free[x % 2], 1)
            feed(S["ukv"], 1)
            for n in range(16):
                latent = n >= 8
                act.wait_ge(negmax2, n + 1)
                if n >= 2:
                    wait_tp_full(act, prob_use(n - 2))
                for m in range(MT):
                    dst = sb2[:, n % 2, m * T:(m + 1) * T]
                    src = sc[n % 2][:, m * T:(m + 1) * T] if latent else dst
                    ins = act.activation(dst, src, ACT.Exp, scale=MLA_SCALE if latent else 1.0,
                                         bias=nm2[:, n % 2, m:m + 1],
                                         accum_out=sum2[:, n // 8, m, n % 8:n % 8 + 1])
                ins.then_inc(probs2, 1)
                if n == 5:
                    for k in range(4):
                        x = X["mqk"] + 2 * k
                        wait_tp_full(act, x)
                        act.activation(mqT[:, 2 * k:2 * k + 2, :], two(tp[x % 2], 96), ACT.Copy).then_inc(tp_free[x % 2], 1)
                if n == 10:
                    for m in range(MT):
                        wait_drained(act, G["na"], m)
                        square("na", 0, m, o2[:, 0, m, :])
                if n == 11:
                    for k in range(2):
                        split(X["ona"] + k, (2 * k, 2 * k + 1), par[:, PAR["na_g"]:PAR["na_g"] + 4], xt_hi)
                if 1 <= n < 5:
                    feed(S["out2"] + n - 1, 1)
                if n == 15:
                    feed(S["out2"] + 4, 4)
            for k in range(2):
                split(X["omla"] + k, (4 + 2 * k, 5 + 2 * k), par[:, PAR["mla_g"] - 4:PAR["mla_g"] + 4], xt_hi)
            for m in range(MT):
                square("mla", 0, m, o2[:, 1, m, :])
            feed(S["out2"] + 8, 4)
            for c in range(2):
                for m in range(MT):
                    wait_drained(act, G["bot"] + c, m)
                    square("mix", c, m, f[:, m, c * W:(c + 1) * W])
            f3_g = par[:, PAR["f3_g"]:PAR["f3_g"] + KT]
            for n in range(2):
                split(X["h4"] + n, (2 * n, 2 * n + 1), f3_g, xt_hi)

            def squares_h4():
                for c in range(2):
                    for m in range(MT):
                        square("h4", c, m, h[:, m, c * W:(c + 1) * W])

            ffn(S["f3i"], S["f3o"], G["f3i"], X["f3"], X["h4"], f3_g, ST["h4"] + 1, lambda: None, squares_h4, rs[:, ST["h4"]],
                lambda: None)
            feed(S["f3o"] + 6, 9)
            post_squares("f3", 0, G["f3o"], S["f3o"] + 10)
            feed(S["f3o"] + 15, 7)
            post_squares("f3", 1, G["f3o"] + 1, S["f3o"] + 21)


        @block.tensor
        def _(pe):
            def slab_products(s, j_tiles, lhs, width, banks, first, last, i=0, turns=0, done=None):
                hi, lo = lhs
                for m in range(MT):
                    for n, (j, k) in enumerate(j_tiles):
                        rows = slice(m * P, (m + 1) * P)
                        wh = w_hi[:, s % RING, j * width:(j + 1) * width]
                        wl = w_lo[:, s % RING, j * width:(j + 1) * width]
                        o = banks[m][:, 0:width]
                        end = last and n == len(j_tiles) - 1
                        pe.matmul(o, hi[:, k, rows], wh, start=first and n == 0, stop=False)
                        pe.matmul(o, lo[:, k, rows], wh, start=False, stop=False)
                        mm = pe.matmul(o, hi[:, k, rows], wl, start=False, stop=end)
                    if m == 0 and last:
                        mm.then_inc(done[0], 1)
                    if m == 1:
                        mm.then_inc(done[1], 1)

            def group(s, g, lhs, slabs, i=0, slab_turns=0, acc_turns=0, width=W, k0=0, ready=None, after={}):
                for q in range(slabs):
                    wait(pe, lo_done[(s + q) % RING], (s + q) // RING + 1, i, slab_turns)
                    if ready is not None:
                        ready(q)
                    if q == 0:
                        for m in range(MT):
                            wait_bank(pe, g, m, i, acc_turns)
                    slab_products(s + q, [(0, k0 + 2 * q), (1, k0 + 2 * q + 1)], lhs, width,
                                  acc[g % 2 * 2:g % 2 * 2 + 2], q == 0, q == slabs - 1,
                                  done=(acc0_full[g % 2], slab_used[(s + q) % RING]))
                    if q in after:
                        after[q]()

            def turn(x, pieces, i=0, turns=0):
                wait(pe, tp_free[x % 2], x // 2, i, turns)
                for col, src in pieces:
                    rows, cols = src.shape[0], int(np.prod(src.shape[1:]))
                    t = pe.transpose(tp[x % 2][0:cols, col:col + rows], src, ident[0:rows, 0:rows])
                t.then_inc(tp_full[x % 2], 1)

            def turn_tiles(x, src, tiles, i=0, turns=0):
                turn(x, [(n * T + m * P, src[:, m, k * P:(k + 1) * P]) for n, k in enumerate(tiles) for m in range(MT)],
                     i, turns)

            def pairs_ready(x):
                return lambda q: wait_tp_free(pe, x + q)

            XT, YT, HID = (xt_hi, xt_lo), (yt_hi, yt_lo), (hid_hi, hid_lo)

            pe.wait_ge(ident_landed, 16)
            for m in range(MT):
                pe.wait_ge(x_landed[m], 16)
            for n in range(4):
                turn_tiles(X["x"] + n, h, (2 * n, 2 * n + 1))
            ready = pairs_ready(X["x"])
            with pe.Fori(0, 2) as i:
                for g in range(2):
                    group(4 * g, g, XT, 4, i, 2, 1, ready=ready)

            def turn_xr_gr(tile_pairs):
                for g in range(4):
                    for m in range(MT):
                        wait_drained(pe, g, m)
                for n in tile_pairs:
                    turn_tiles(X["xg"] + 2 * n, u[:, 0], (2 * n, 2 * n + 1))
                    turn_tiles(X["xg"] + 2 * n + 1, u[:, 1], (2 * n, 2 * n + 1))

            def turn_parameters():
                pe.wait_ge(par_landed, 16 * 15)
                turn(X["par"], [(0, par_rows[0:PAR["end"], :])])
                turn_xr_gr((0, 1))

            group(16, 4, XT, 4, after={0: turn_parameters, 1: lambda: turn_xr_gr((2, 3))})
            group(20, 5, XT, 4)

            def gates():
                pe.wait_ge(bd_landed, 64)
                for n in range(KT):
                    x = X["gate"] + n
                    pe.wait_ge(conv_done, n + 1)
                    wait(pe, tp_free[x % 2], x // 2)
                    pe.matmul(tp[x % 2][:, 0:T], blockdiag[:, n, :], xcT[:, n, :], start=True, stop=True)
                    pe.matmul(tp[x % 2][:, T:2 * T], blockdiag[:, KT + n, :], xcT[:, n, :], start=True,
                              stop=True).then_inc(tp_full[x % 2], 1)

            def turn_q_k(n):
                for sec in (2, 3):
                    for m in range(MT):
                        wait_drained(pe, 2 * sec + n // 2, m)
                    turn_tiles(X["qk"] + 2 * n + sec - 2, u[:, sec], (2 * n, 2 * n + 1))

            group(24, 6, XT, 4, after={2: gates})
            group(28, 7, XT, 4)
            group(32, 8, XT, 4, after={1: lambda: turn_q_k(0), 2: lambda: turn_q_k(1)})
            group(36, 9, XT, 4, after={0: lambda: turn_q_k(2), 1: lambda: turn_q_k(3)})
            wait_tp_free(pe, X["qk"] + 6)
            wait_tp_free(pe, X["qk"] + 7)

            def scores1(g, r, i):
                wait(pe, staged, 2 * g + 2, i, 4)
                for hh in range(2):
                    tile = i * 4 + (2 * g + r + KT)
                    for m in range(MT):
                        n = P * (m + 1)
                        mm = pe.matmul(sc[hh][:, P * m:P * m + n], q_stage[:, 2 * r + hh, m * P:(m + 1) * P],
                                       qkT[:, bass.ds(tile, 1), 0:n].rearrange("p a n -> p (a n)"),
                                       start=True, stop=True)
                    mm.then_inc(scores_done, 1)

            def turn_probs1(g, r, i):
                for hh in range(2):
                    wait(pe, probs_done, 4 * g + 2 * r + hh + 1, i, 8)
                    wait(pe, o_drained, 4 * g + 2 * r + hh + 1, i, 8)
                    turn(X["p1"] + 4 * g + 2 * r + hh, [(P * n, sb1[:, hh, P * n:P * (n + 1)]) for n in range(3)], i, 4)

            def values1(g, r, i):
                for hh in range(2):
                    x = X["p1"] + 4 * g + 2 * r + hh
                    wait_tp_free(pe, x, i, 4)
                    o = tp[x % 2][:, 384:512]
                    head = i * 8 + (4 * g + 2 * r + hh)
                    v = [u[:, 4, m, bass.ds(head * HD, HD)] for m in range(MT)]
                    pe.matmul(o[:, 0:HD], pt1[:, hh, 0:P], v[0], start=True, stop=True)
                    pe.matmul(o[:, HD:2 * HD], pt1[:, hh, P:2 * P], v[0], start=True, stop=False)
                    pe.matmul(o[:, HD:2 * HD], pt1[:, hh, 2 * P:3 * P], v[1], start=False,
                              stop=True).then_inc(pv_done, 1)

            with pe.Fori(0, 2) as i:
                for g in range(2):
                    scores1(g, 0, i)

                    def second_round(g=g):
                        turn_probs1(g, 0, i)
                        scores1(g, 1, i)

                    group(40 + 4 * g, 10 + g, XT, 4, i, 2, 1,
                          after={1: second_round, 2: lambda g=g: values1(g, 0, i)})
                    turn_probs1(g, 1, i)
                    values1(g, 1, i)

            def turn_att(uses):
                wait(pe, o_drained, 18)
                for n in uses:
                    turn_tiles(X["at"] + n, att, (2 * n, 2 * n + 1))

            pe.wait_ge(yt_ready, 1)
            group(S["rnn"], G["rnn"], YT, 4)
            group(S["rnn"] + 4, G["rnn"] + 1, YT, 4, after={0: lambda: turn_att((0, 1)), 1: lambda: turn_att((2, 3))})

            def turn_merged(half):
                wait(pe, m_ready, 2 * half + 2)
                for n in (2 * half, 2 * half + 1):
                    turn_tiles(X["mt"] + n, merged, (2 * n, 2 * n + 1))

            ready = pairs_ready(X["at"])
            group(S["attn"], G["attn"], XT, 4, ready=ready)
            group(S["attn"] + 4, G["attn"] + 1, XT, 4, after={2: lambda: turn_merged(0)})

            def turn_h(x, g_o, half):
                for m in range(MT):
                    wait_drained(pe, g_o + half, m)
                for n in (2 * half, 2 * half + 1):
                    turn_tiles(x + n, h, (2 * n, 2 * n + 1))

            ready = pairs_ready(X["mt"])
            group(S["o"], G["o"], YT, 4, ready=ready, after={0: lambda: turn_merged(1)})
            group(S["o"] + 4, G["o"] + 1, YT, 4, after={2: lambda: turn_h(X["h1"], G["o"], 0)})

            def ffn(s_in, s_out, g_in, g_out, x_h, x_hid, second_half, before_last):
                def turn_hidden(g, i=0):
                    for m in range(MT):
                        wait_drained(pe, g_in + g, m, i, 1)
                    turn(x_hid + g, [(n * T + m * P, hid[:, g % 2, m, n * P:(n + 1) * P])
                                     for n in range(2) for m in range(MT)], i, 1)

                ready = pairs_ready(x_h)
                group(s_in, g_in, XT, 4, ready=ready, after={0: second_half})
                with pe.Fori(0, (FG - 1) // 2) as i:
                    for q in range(2):
                        g = 1 + q
                        group(s_in + 4 * g, g_in + g, XT, 4, i, 2, 1, after={1: lambda g=g: turn_hidden(g - 1, i)})
                ready = pairs_ready(x_hid)
                group(s_out, g_out, HID, 11, ready=ready, after={1: lambda: turn_hidden(FG - 1)})
                group(s_out + 11, g_out + 1, HID, 11, after={8: before_last})

            ffn(S["f1i"], S["f1o"], G["f1i"], G["f1o"], X["h1"], X["f1"],
                lambda: turn_h(X["h1"], G["o"], 1), lambda: turn_h(X["h2"], G["f1o"], 0))
            ffn(S["f2i"], S["f2o"], G["f2i"], G["f2o"], X["h2"], X["f2"],
                lambda: turn_h(X["h2"], G["f1o"], 1), lambda: None)

            def turn_new_h(x, uses, count):
                for n in uses:
                    wait(pe, h_new, count + 2 * (n // 2) + 2)
                    turn_tiles(x + n, h, (2 * n, 2 * n + 1))

            turn_new_h(X["h3"], (0, 1), 0)

            def turn_latents():
                for m in range(MT):
                    wait_drained(pe, G["in2"], m)
                turn_tiles(X["c"], u2[:, :, 1536:1952], (0, 1))
                turn_tiles(X["c"] + 1, u2[:, :, 1536:1952], (2,))

            ready = pairs_ready(X["h3"])
            group(S["in2"], G["in2"], XT, 4, width=416, ready=ready,
                  after={0: lambda: turn_new_h(X["h3"], (2,), 0), 1: lambda: turn_new_h(X["h3"], (3,), 0)})
            def turn_nqk(n):
                for m in range(MT):
                    for c in range(2):
                        wait_drained(pe, G["in2"] + 1 + c, m)
                turn_tiles(X["nqk"] + 2 * n, u2, (2 * n, 2 * n + 1))
                turn_tiles(X["nqk"] + 2 * n + 1, u2, (4 + 2 * n, 5 + 2 * n))

            between = ({1: turn_latents}, {}, {1: lambda: turn_nqk(0), 2: lambda: turn_nqk(1)})
            for c in range(3):
                group(S["in2"] + 4 * c + 4, G["in2"] + c + 1, XT, 4, after=between[c])
            def scores(n):
                if n < 8:
                    rows, t = slice(64 * (n % 2), 64 * (n % 2) + 64), n // 2
                    q, k = nqk[rows, t, :], nqk[rows, 4 + t, :]
                    wait_tp_free(pe, X["nqk"] + n // 4 * 2)
                    wait_tp_free(pe, X["nqk"] + n // 4 * 2 + 1)
                else:
                    q, k = mqT[:, n - 8, :], mkT[:, n - 8, :]
                    wait_tp_free(pe, X["mqk"] + (n - 8) // 2 * 2)
                    wait_tp_free(pe, X["mqk"] + (n - 8) // 2 * 2 + 1)
                for m in range(MT):
                    mm = pe.matmul(sc[n % 2][:, m * T:(m + 1) * T], q[:, m * P:(m + 1) * P], k, start=True, stop=True)
                mm.then_inc(scores2, 1)

            scores(0)
            scores(1)
            C = (c_hi, c_lo)
            wait_tp_free(pe, X["c"])
            group(S["uq"], G["uq"], C, 1)
            group(S["uq"] + 1, G["uq"] + 1, C, 1, width=256)
            wait_tp_free(pe, X["c"] + 1)
            s = S["ukv"]
            wait(pe, lo_done[s % RING], s // RING + 1)
            for j in range(2):
                g = G["ukv"] + j
                for m in range(MT):
                    wait_bank(pe, g, m)
                slab_products(s, [(j, 2)], C, W, acc[g % 2 * 2:g % 2 * 2 + 2], True, True,
                              done=(acc0_full[g % 2], kv_half if j == 0 else slab_used[s % RING]))
            def turn_probs(n):
                pe.wait_ge(probs2, n + 1)
                turn(prob_use(n), [(c * P, sb2[:, n % 2, c * P:(c + 1) * P]) for c in range(4)])

            def values(n):
                g = G["na"] if n < 8 else G["mla"]
                if n % 8 == 0:
                    for m in range(MT):
                        wait_bank(pe, g, m)
                wait_tp_free(pe, prob_use(n))
                hd = n % 8
                for m in range(MT):
                    for kt in range(2):
                        v = u2[:, kt, 1024 + HD * hd:1024 + HD * hd + HD] if n < 8 else mv[:, kt, hd, :]
                        mm = pe.matmul(acc[g % 2 * 2 + m][:, HD * hd:HD * hd + HD],
                                       pt2[:, n % 2, (2 * m + kt) * P:(2 * m + kt + 1) * P], v,
                                       start=kt == 0, stop=kt == 1)
                    if m == 0 and hd == 7:
                        mm.then_inc(acc0_full[g % 2], 1)
                mm.then_inc(pv2, 1)

            for m in range(MT):
                wait_drained(pe, G["in2"] + 3, m)
            for n in range(16):
                turn_probs(n)
                if n + 2 < 16:
                    scores(n + 2)
                if n >= 1:
                    values(n - 1)
                if n == 5:
                    pe.wait_ge(rope_q, 2)
                    pe.wait_ge(rope_k, 2)
                    for k in range(4):
                        for which, src in ((0, mq), (1, mk)):
                            turn(X["mqk"] + 2 * k + which, [(c * T + m * P, src[:, m, 2 * k + c, :])
                                                            for c in range(2) for m in range(MT)])
                if n == 10:
                    for m in range(MT):
                        wait_drained(pe, G["na"], m)
                    for k in range(2):
                        turn_tiles(X["ona"] + k, o2[:, 0], (2 * k, 2 * k + 1))
            values(15)
            ready = pairs_ready(X["ona"])
            group(S["out2"], G["top"], XT, 2, ready=ready)
            for m in range(MT):
                wait_drained(pe, G["mla"], m)
            for k in range(2):
                turn_tiles(X["omla"] + k, o2[:, 1], (2 * k, 2 * k + 1))
            group(S["out2"] + 2, G["top"] + 1, XT, 2)
            ready = pairs_ready(X["omla"])
            for c in range(2):
                group(S["out2"] + 4 + 2 * c, G["bot"] + c, XT, 2, k0=4, ready=ready)
            turn_new_h(X["h4"], (0, 1), 4)
            ffn(S["f3i"], S["f3o"], G["f3i"], G["f3o"], X["h4"], X["f3"],
                lambda: turn_new_h(X["h4"], (2, 3), 4), lambda: None)

        @block.vector
        def _(dve):
            steps = [0]

            def step(ins):
                steps[0] += 1
                ins.then_inc(dve_step, 1)
                dve.wait_ge(dve_step, steps[0])

            def feed(s, n=1, i=0, turns=0):
                for q in range(s, min(s + n, S["end"])):
                    if q % 2 == 0:
                        b = q % RING
                        wait(dve, hi_done[b], q // RING + 1, i, turns)
                        dve.tensor_tensor(w_lo[:, b, :], w_raw[:, b, :], w_hi[:, b, :].bitcast(F32),
                                          ALU.subtract).then_inc(lo_done[b], 1)

            def split(x, tiles, gain, hi, lo, index, scale=1.0, i=0, turns=0, hi_turns=0):
                if gain is None:
                    wait(dve, hi_written, index + 1, i, hi_turns)
                    dve.scalar_tensor_tensor(lo, two(tp[x % 2]), scale, hi.bitcast(F32), ALU.mult,
                                             ALU.subtract).then_inc(tp_free[x % 2], 1)
                else:
                    wait(dve, hi_written, index + len(tiles), i, hi_turns)
                    for n, k in enumerate(tiles):
                        ins = dve.scalar_tensor_tensor(lo[:, k, :], tp[x % 2][:, n * T:(n + 1) * T], gain[:, k:k + 1],
                                                       hi[:, k, :].bitcast(F32), ALU.mult, ALU.subtract)
                    ins.then_inc(tp_free[x % 2], 1)

            def mean_square(name):
                _, n, factor = STATS[ST[name]]
                t = ST[name]
                two_halves = name in TWO_HALVES
                wait(dve, ssq_done, max(SQ[k] for k in SQUARES if k[0] == name) + 1)
                src = ssq[:, t, 0, :]
                if two_halves:
                    step(dve.tensor_tensor(ssq[:, t, 0, :], ssq[:, t, 0, :], ssq[:, t, 1, :], ALU.add))
                dve.tensor_scalar(ms[:, t, :], src, factor / n, factor * EPS, ALU.mult, ALU.add).then_inc(ms_done, 1)

            dve.memset(minus_half[:], -0.5).then_inc(set_up, 1)
            dve.memset(carrier[:], 0.0).then_inc(o_drained, 2)
            for b in range(4):
                dve.memset(free_marks[:, b:b + 1], 0.0).then_inc(acc_drained[b], 1)
            dve.memset(free_marks[:, 4:5], 0.0).then_inc(ttr_done, 1)
            dve.memset(xrT[:, :, 0:3], 0.0).then_inc(set_up, 1)
            dve.memset(bias1[0:CHUNK, :, :, 0:CHUNK], MASKED).then_inc(set_up, 1)
            for n in range(4):
                split(X["x"] + n, (2 * n, 2 * n + 1), gain_x, xt_hi, xt_lo, HI["x"] + 2 * n)
                if n == 1:
                    feed(0, 2)
            feed(2, 2)
            mean_square("x")

            def pcol(name, n=KT, off=0):
                return par[:, PAR[name] + off:PAR[name] + off + n]

            def drain_scaled(g, dst, i=0, slab_turns=0, acc_turns=0, last_slab=None, scale=None):
                for m in range(MT):
                    wait_acc(dve, g, m, last_slab, i, slab_turns, acc_turns)
                    dve.tensor_scalar(dst(m), acc[g % 2 * 2 + m][:, :], scale[:, m:m + 1], None,
                                      ALU.mult).then_inc(acc_drained[g % 2 * 2 + m], 1)

            dve.wait_ge(rs_done, ST["x"] + 1)
            rx = rs[:, ST["x"]]
            with dve.Fori(0, 2) as i:
                for g in range(2):
                    feed(4 + 4 * g, 4, i, 2)
                    drain_scaled(g, lambda m: u[:, bass.ds(i, 1), m, g * W:(g + 1) * W].rearrange("p a n -> p (a n)"),
                                 i, 2, 1, 4 * g + 3, rx)
            wait_tp_full(dve, X["par"])
            dve.tensor_copy(par[:, 0:PAR["end"]], tp[X["par"] % 2][:, 0:PAR["end"]]).then_inc(tp_free[X["par"] % 2], 1)
            wait_tp_free(dve, X["par"])

            step(dve.scalar_tensor_tensor(small[:, 0, :], pcol("lam"), -1.0, pcol("lam"), ALU.mult, ALU.max))
            dve.tensor_scalar(small[:, 10, :], pcol("lam"), -1.0, 0.0, ALU.mult, ALU.max).then_inc(abs_lam, 1)
            dve.tensor_scalar(small[:, 8, :], pcol("b_r"), 0.5, None, ALU.mult)
            dve.tensor_scalar(small[:, 9, :], pcol("b_i"), 0.5, None, ALU.mult)
            dve.tensor_tensor(small[:, 11, :], pcol("fin_g"), pcol("f2_g"), ALU.mult)
            for n in range(4):
                x = X["xg"] + 2 * n + 1
                wait_tp_full(dve, x)
                dve.tensor_copy(grT[:, 2 * n:2 * n + 2, :], two(tp[x % 2])).then_inc(tp_free[x % 2], 1)
            wait_tp_free(dve, X["xg"] + 6)
            wait_tp_free(dve, X["xg"] + 7)

            def conv_tiles(tiles):
                base_step = steps[0]
                for j in range(4):
                    for at, n in enumerate(tiles):
                        tap = xrT[:, n, j:j + T]
                        w = par[:, PAR["conv_w"] + 8 * j + n:PAR["conv_w"] + 8 * j + n + 1]
                        if j == 0:
                            ins = dve.tensor_scalar(xcT[:, n, :], tap, w, pcol("conv_b", 1, n), ALU.mult, ALU.add)
                        else:
                            dve.wait_ge(dve_step, base_step + (j - 1) * len(tiles) + at + 1)
                            ins = dve.scalar_tensor_tensor(xcT[:, n, :], tap, w, xcT[:, n, :], ALU.mult, ALU.add)
                        if j == 3:
                            ins.then_inc(conv_done, 1)
                        else:
                            steps[0] += 1
                            ins.then_inc(dve_step, 1)

            def drain_section(g):
                drain_scaled(g, lambda m: u[:, g // 2, m, g % 2 * W:(g % 2 + 1) * W], last_slab=4 * g + 3, scale=rx)

            feed(20, 2)
            conv_tiles((0, 1))
            feed(22, 2)
            conv_tiles((2, 3))
            drain_section(4)
            feed(24, 2)
            dve.wait_ge(exp_lam, 1)
            step(dve.tensor_scalar(small[:, 2, :], small[:, 1, :], 2.0, None, ALU.add))
            step(dve.reciprocal(small[:, 3, :], small[:, 2, :]))
            step(dve.tensor_tensor(small[:, 2, :], small[:, 1, :], small[:, 3, :], ALU.mult))
            step(dve.tensor_tensor(small[:, 4, :], small[:, 2, :], small[:, 2, :], ALU.mult))
            step(dve.tensor_scalar(small[:, 5, :], small[:, 4, :], 1.0 / 17, None, ALU.mult))
            for n in (15, 13, 11, 9, 7, 5, 3):
                step(dve.scalar_tensor_tensor(small[:, 5, :], small[:, 5, :], 1.0 / n, small[:, 4, :], ALU.add, ALU.mult))
            step(dve.scalar_tensor_tensor(small[:, 5, :], small[:, 5, :], 1.0, small[:, 2, :], ALU.add, ALU.mult))
            step(dve.scalar_tensor_tensor(small[:, 5, :], small[:, 5, :], 2.0, small[:, 10, :], ALU.mult, ALU.add))
            step(dve.tensor_scalar(small[:, 6, :], small[:, 5, :], 4.0, None, ALU.mult))
            dve.tensor_scalar(small[:, 7, :], small[:, 5, :], -4.0, None, ALU.mult).then_inc(consts_ready, 1)

            conv_tiles((4, 5))
            feed(26, 2)
            conv_tiles((6, 7))
            drain_section(5)
            dve.wait_ge(table_landed, 16)
            dve.tensor_copy(ext_sb[:, 256:384], ext_sb[:, 255:256].to_broadcast([HEADS, P])).then_inc(ext_done, 1)
            feed(28, 4)
            drain_section(6)
            feed(32, 2)
            aT = xrT[:, :, 0:T]
            dve.wait_ge(decay_done, 16)
            dve.tensor_tensor(sq, aT, aT, ALU.mult).then_inc(mult2_done, 1)
            dve.wait_ge(mult2_done, 1)
            dve.scalar_tensor_tensor(sq, sq, 1.0, trT, ALU.add, ALU.mult).then_inc(mult2_done, 1)
            feed(34, 2)
            wait_tp_free(dve, X["gate"] + 6)
            wait_tp_free(dve, X["gate"] + 7)
            step(dve.scalar_tensor_tensor(ti[:], ti[:], 1.0, xcT, ALU.add, ALU.mult))
            drain_section(7)
            dve.wait_ge(mult_done, 1)
            dve.scalar_tensor_tensor(ti[:], ti[:], 0.5, sq, ALU.mult, ALU.mult).then_inc(bx_done, 1)

            def copy_k(n):
                x = X["qk"] + 2 * n + 1
                wait_tp_full(dve, x)
                dve.tensor_copy(qkT[:, KT + 2 * n:KT + 2 * n + 2, :], two(tp[x % 2])).then_inc(tp_free[x % 2], 1)

            def recur(tiles):
                for n in tiles:
                    dve.tensor_tensor_scan(xcT[:, n, :], xrT[:, n, 0:T], ti[:, n, :], 0.0, ALU.mult,
                                           ALU.add).then_inc(rec_done, 1)

            feed(36, 2)
            copy_k(0)
            dve.wait_ge(bx_done, 1)
            recur(range(0, 4))
            feed(38, 2)
            copy_k(1)
            recur(range(4, 8))
            drain_section(8)
            feed(40, 2)
            copy_k(2)
            copy_k(3)
            dve.wait_ge(gelu_tanh, 1)
            step(dve.scalar_tensor_tensor(gel, gel, 1.0, grT[:], ALU.add, ALU.mult))
            dve.wait_ge(rec_done, KT)
            dve.scalar_tensor_tensor(trT, gel, 0.5, xcT, ALU.mult, ALU.mult).then_inc(rg_out, 1)
            feed(42, 2)
            drain_section(9)
            dve.wait_ge(rg_out, 1)
            dve.wait_ge(hi_written, HI["rg"] + 1)
            dve.tensor_tensor(yt_lo[:], trT, yt_hi[:].bitcast(F32), ALU.subtract).then_inc(yt_ready, 1)

            dve.wait_ge(merge_landed, 16)
            dve.wait_ge(set_up, 3)

            def maxima1(g, r, i):
                if r == 0:
                    wait(dve, bias_landed[g], 32, i, 32)
                for hh in range(2):
                    wait(dve, scores_done, 4 * g + 2 * r + hh + 1, i, 8)
                    dve.memset(carrier[:, 4 * g + 2 * r + hh:4 * g + 2 * r + hh + 1], 0.0)
                    for m in range(MT):
                        n = P * (m + 1)
                        b = bias1[:, g, 2 * r + hh, n - 1::-1]
                        dve.tensor_tensor_reduce(sb1[:, hh, P * m:P * m + n], sc[hh][:, P * m:P * m + n], b, 1.0, -3e38,
                                                 ALU.add, ALU.max, mx1[:, r, 2 * hh + m:2 * hh + m + 1]).then_inc(ttr_done, 1)
                wait(dve, ttr_done, 8 * g + 4 * r + 5, i, 16)
                dve.tensor_scalar(nm1[:, r, :], mx1[:, r, :], -1.0, None, ALU.mult).then_inc(negmax_done, 1)

            def drain_values1(g, r, i):
                wait(dve, probs_done, 4 * g + 2 * r + 2, i, 8)
                dve.reciprocal(inv1[:, r, :], sum1[:, r, :]).then_inc(inv_done, 1)
                wait(dve, inv_done, 2 * g + r + 1, i, 4)
                for hh in range(2):
                    head = i * 8 + (4 * g + 2 * r + hh)
                    wait(dve, pv_done, 4 * g + 2 * r + hh + 1, i, 8)
                    dve.tensor_tensor(att[:, :, bass.ds(head * HD, HD)],
                                      tp[(X["p1"] + hh) % 2][:, 384:512].rearrange("p (m d) -> p m d", m=MT),
                                      inv1[:, r, 2 * hh:2 * hh + 2].unsqueeze(2).to_broadcast([P, MT, HD]),
                                      ALU.mult).then_inc(o_drained, 1)

            with dve.Fori(0, 2) as i:
                for g in range(2):
                    s = 44 + 4 * g
                    maxima1(g, 0, i)
                    feed(s, 2, i, 2)
                    maxima1(g, 1, i)
                    drain_values1(g, 0, i)
                    feed(s + 2, 2, i, 2)
                    for m in range(MT):
                        wait_acc(dve, G["in"] + 10 + g, m, 43 + 4 * g, i, 2, 1)
                        dst = u[:, bass.ds(i + 5, 1), m, g * W:(g + 1) * W].rearrange("p a n -> p (a n)")
                        b = b_merge[:, bass.ds(i * D + g * W, W)]
                        dve.scalar_tensor_tensor(dst, acc[g % 2 * 2 + m][:, :], rx[:, m:m + 1], b, ALU.mult,
                                                 ALU.add).then_inc(acc_drained[g % 2 * 2 + m], 1)
                    drain_values1(g, 1, i)

            feed(S["rnn"] + 4, 4)
            dve.wait_ge(gate_tanh, 8)
            for c in range(2):
                cols = slice(c * W, (c + 1) * W)
                for m in range(MT):
                    wait_acc(dve, G["rnn"] + c, m, S["rnn"] + 4 * c + 3)
                    dve.scalar_tensor_tensor(merged[:, m, cols], u[:, 6, m, cols], 1.0, acc[(G["rnn"] + c) % 2 * 2 + m][:, :],
                                             ALU.add, ALU.mult).then_inc(acc_drained[(G["rnn"] + c) % 2 * 2 + m], 1)
                if c == 0:
                    for n in range(4):
                        if n == 2:
                            feed(S["rnn"] + 8, 1)
                        t = slice(2 * n, 2 * n + 2)
                        split(X["at"] + n, None, None, xt_hi[:, t, :], xt_lo[:, t, :], HI["at"] + n)
                    feed(S["rnn"] + 9, 3)
            feed(S["rnn"] + 12, 4)
            for c in range(2):
                cols = slice(c * W, (c + 1) * W)
                for m in range(MT):
                    b = (G["attn"] + c) % 2 * 2 + m
                    wait_acc(dve, G["attn"] + c, m, S["attn"] + 4 * c + 3)
                    dve.scalar_tensor_tensor(u[:, 5, m, cols], u[:, 5, m, cols], 1.0, acc[b][:, :],
                                             ALU.add, ALU.mult).then_inc(acc_drained[b], 1)
                for m in range(MT):
                    wait_drained(dve, G["attn"] + c, m)
                    wait_drained(dve, G["rnn"] + c, m)
                    dve.tensor_tensor(merged[:, m, cols], merged[:, m, cols], u[:, 5, m, cols], ALU.add).then_inc(m_ready, 1)
                feed(S["attn"] + 8 + 4 * c, 3 if c == 0 else 1)
                for n in (2 * c, 2 * c + 1):
                    t = slice(2 * n, 2 * n + 2)
                    split(X["mt"] + n, None, None, yt_hi[:, t, :], yt_lo[:, t, :], HI["mt"] + n, 0.5)
                feed(S["attn"] + 11 + 2 * c, 1)
            feed(S["o"] + 6, 2)

            def add_to_h(g, c, last_slab):
                for m in range(MT):
                    b = g % 2 * 2 + m
                    wait_acc(dve, g, m, last_slab)
                    dve.tensor_tensor(h[:, m, c * W:(c + 1) * W], h[:, m, c * W:(c + 1) * W], acc[b][:, :],
                                      ALU.add).then_inc(acc_drained[b], 1)

            def split_h(name, gain, uses):
                for n in uses:
                    split(X[name] + n, (2 * n, 2 * n + 1), gain, xt_hi, xt_lo, HI[name] + 2 * n)

            add_to_h(G["o"], 0, S["o"] + 3)
            feed(S["o"] + 8, 3)
            split_h("h1", pcol("ffn_g"), (0, 1))
            feed(S["o"] + 11, 1)
            add_to_h(G["o"] + 1, 1, S["o"] + 7)

            def ffn(n_ffn, s_in, s_out, g_in, x_name, h_name, gain, before, statistics, scale):
                before()
                feed(s_in + 4, 1)
                split_h(h_name, gain, (2, 3))
                feed(s_in + 5, 1)
                statistics()
                feed(s_in + 6, 2)

                def hidden(g, i=0):
                    for m in range(MT):
                        wait(dve, tanh_done, 2 * FG * n_ffn + 2 * g + m + 1, i, 4)
                        dve.scalar_tensor_tensor(u1[:, m, :], th[:, m, :], 1.0, acc[(g_in + g) % 2 * 2 + m][:, 0:256],
                                                 ALU.add, ALU.mult).then_inc(u1_done, 1)
                    for m in range(MT):
                        b = (g_in + g) % 2 * 2 + m
                        wait(dve, u1_done, 2 * FG * n_ffn + 2 * g + m + 1, i, 4)
                        wait_acc(dve, g_in + g, m, s_in + 4 * g + 3, i, 2, 1)
                        dve.scalar_tensor_tensor(hid[:, g % 2, m, :], u1[:, m, :], scale[:, m:m + 1], acc[b][:, 256:512],
                                                 ALU.mult, ALU.mult).then_inc(acc_drained[b], 1)

                hidden(0)
                with dve.Fori(0, (FG - 1) // 2) as i:
                    for q in range(2):
                        g = 1 + q
                        tiles = bass.ds(i * 4 + 2 * q, 2)
                        feed(s_in + 4 * g + 4, 2, i, 2)
                        split(X[x_name] + g - 1, None, None, hid_hi[:, tiles, :], hid_lo[:, tiles, :],
                              HI[x_name] + g - 1, 1.0, i, 1, 2)
                        feed(s_in + 4 * g + 6, 2, i, 2)
                        hidden(g, i)
                feed(s_out + 4, 2)
                split(X[x_name] + FG - 1, None, None, hid_hi[:, FT - 2:FT, :], hid_lo[:, FT - 2:FT, :],
                      HI[x_name] + FG - 1)

            def half_rstd_squared(name, slot):
                dve.wait_ge(rs_done, ST[name] + 1)
                r = rs[:, ST[name]]
                dve.scalar_tensor_tensor(coef[:, slot, :], r, 2.0, r, ALU.mult, ALU.mult).then_inc(coef_done, 1)

            def statistics1():
                half_rstd_squared("h1", 0)
                dve.wait_ge(coef_done, 1)

            ffn(0, S["f1i"], S["f1o"], G["f1i"], "f1", "h1", pcol("ffn_g"), lambda: mean_square("h1"), statistics1, coef[:, 0])
            dve.wait_ge(late_landed, 16 * 5)
            step(dve.memset(ext2_sb[:], 0.0))
            dve.tensor_copy(ext2_sb[:, :, 48:79], rpb_sb[:, 4:11, ::-1]).then_inc(ext2_done, 1)
            feed(S["f1o"] + 6, 9)
            add_to_h(G["f1o"], 0, S["f1o"] + 10)
            feed(S["f1o"] + 15, 7)
            split_h("h2", small[:, 11, :], (0, 1))
            feed(S["f1o"] + 22, 4)
            add_to_h(G["f1o"] + 1, 1, S["f1o"] + 21)
            dve.wait_ge(rows_landed, 64)

            def statistics2():
                dve.wait_ge(rs_done, ST["h2"] + 1)
                wait_tp_full(dve, X["h2"] + 2)
                wait_tp_full(dve, X["h2"] + 3)
                for m in range(MT):
                    dve.scalar_tensor_tensor(h[:, m, :], h[:, m, :], rs[:, ST["h2"], m:m + 1], row_gain[:, 0, :],
                                             ALU.mult, ALU.mult).then_inc(x2_ready, 1)
                mean_square("x2")
                dve.wait_ge(rs_done, ST["x2"] + 1)
                dve.tensor_tensor(coef[:, 1, :], rs[:, ST["h2"]], rs[:, ST["x2"]], ALU.mult).then_inc(coef_done, 1)
                dve.wait_ge(coef_done, 2)
                dve.scalar_tensor_tensor(coef[:, 2, :], coef[:, 1, :], 2.0, coef[:, 1, :], ALU.mult,
                                         ALU.mult).then_inc(coef_done, 1)
                dve.wait_ge(coef_done, 3)

            ffn(1, S["f2i"], S["f2o"], G["f2i"], "f2", "h2", small[:, 11, :], lambda: mean_square("h2"), statistics2, coef[:, 2])

            def gained(name, g, c, row, last_slab):
                for m in range(MT):
                    b = g % 2 * 2 + m
                    wait_acc(dve, g, m, last_slab)
                    dve.wait_ge(ssq_done, SQ[name, c, m] + 1)
                    dve.tensor_tensor(f[:, m, c * W:(c + 1) * W], acc[b][:, :], row_gain[:, row, c * W:(c + 1) * W],
                                      ALU.mult).then_inc(acc_drained[b], 1)

            def add_normed(name, done):
                dve.wait_ge(rs_done, ST[name] + 1)
                for c in range(2):
                    for m in range(MT):
                        v = h[:, m, c * W:(c + 1) * W]
                        dve.scalar_tensor_tensor(v, f[:, m, c * W:(c + 1) * W], rs[:, ST[name], m:m + 1], v, ALU.mult,
                                                 ALU.add).then_inc(done, 1)

            dve.wait_ge(x2_ready, 2)
            feed(S["f2o"] + 6, 9)
            gained("f2", G["f2o"], 0, 1, S["f2o"] + 10)
            feed(S["f2o"] + 15, 11)
            gained("f2", G["f2o"] + 1, 1, 1, S["f2o"] + 21)
            mean_square("f2")
            for g in (G["f2o"], G["f2o"] + 1):
                for m in range(MT):
                    wait_drained(dve, g, m)
            add_normed("f2", h_new)

            mix2_g = pcol("mix2_g")
            split_h("h3", mix2_g, (0, 1))
            feed(S["in2"] + 4, 1)
            split_h("h3", mix2_g, (2,))
            feed(S["in2"] + 5, 1)
            split_h("h3", mix2_g, (3,))
            mean_square("h3")
            feed(S["in2"] + 6, 2)
            dve.wait_ge(rs_done, ST["h3"] + 1)

            def drain_in2(n, col, width):
                g = G["in2"] + n
                for m in range(MT):
                    b = g % 2 * 2 + m
                    wait_acc(dve, g, m, S["in2"] + 4 * n + 3)
                    dve.tensor_scalar(u2[:, m, col:col + width], acc[b][:, 0:width], rs[:, ST["h3"], m:m + 1], None,
                                      ALU.mult).then_inc(acc_drained[b], 1)

            drain_in2(0, 1536, 416)
            feed(S["in2"] + 8, 2)
            mean_square("q")
            mean_square("kv")
            split(X["c"], (0, 1), pcol("q_g", 2), c_hi, c_lo, HI["c"])
            split(X["c"] + 1, (2,), par[:, PAR["kv_g"] - 2:PAR["kv_g"] + 1], c_hi, c_lo, HI["c"] + 2)
            dve.wait_ge(late_landed, 16 * 5)
            for m in range(MT):
                wait_drained(dve, G["in2"], m)
            k1, k2 = u2[:, :, 1920:1936], u2[:, :, 1936:1952]
            dve.tensor_tensor(kr[:, 0], k1, cos[:], ALU.mult)
            dve.tensor_tensor(kr[:, 1], k2, sin[:], ALU.mult)
            dve.tensor_tensor(kr[:, 2], k2, cos[:], ALU.mult)
            step(dve.tensor_tensor(kr[:, 3], k1, sin[:], ALU.mult))

            def over_heads(v):
                return v.unsqueeze(2).to_broadcast([P, MT, 8, 16])

            dve.tensor_tensor(mk[:, :, :, 64:80], over_heads(kr[:, 0]), over_heads(kr[:, 1]), ALU.subtract).then_inc(rope_k, 1)
            dve.tensor_tensor(mk[:, :, :, 80:96], over_heads(kr[:, 2]), over_heads(kr[:, 3]), ALU.add).then_inc(rope_k, 1)
            feed(S["in2"] + 10, 2)
            for n in range(1, 4):
                if n == 3:
                    for t in range(2):
                        x = X["nqk"] + 2 * t + 1
                        wait_tp_full(dve, x)
                        dve.tensor_copy(nqk[:, 4 + 2 * t:6 + 2 * t, :], two(tp[x % 2])).then_inc(tp_free[x % 2], 1)
                        if t == 0:
                            feed(S["in2"] + 18, 1)
                drain_in2(n, W * (n - 1), W)
                if n < 3:
                    feed(S["in2"] + 8 + 4 * n, 4 if n == 1 else 2)
            dve.wait_ge(bias2_ready, 8)

            def maxima2(n):
                dve.wait_ge(scores2, n + 1)
                mx = mx2[:, n % 2, :]
                if n < 8:
                    if n >= 2:
                        wait_tp_full(dve, prob_use(n - 2))
                    for m in range(MT):
                        keys = bias2[:, n, 2 - 2 * m:6 - 2 * m, ::-1]
                        dve.tensor_tensor_reduce(sb2[:, n % 2, m * T:(m + 1) * T].rearrange("p (a b) -> p a b", a=4),
                                                 sc[n % 2][:, m * T:(m + 1) * T].rearrange("p (a b) -> p a b", a=4),
                                                 keys, 1.0, -3e38, ALU.add, ALU.max,
                                                 mx2[:, n % 2, m:m + 1]).then_inc(max2, 1)
                else:
                    dve.tensor_reduce(mx, two(sc[n % 2]), mybir.AxisListType.X, ALU.max).then_inc(max2, 1)
                dve.wait_ge(max2, 2 * n + 2 if n < 8 else 16 + n - 7)
                dve.tensor_scalar(nm2[:, n % 2, :], mx, -1.0 if n < 8 else -MLA_SCALE, None, ALU.mult).then_inc(negmax2, 1)

            maxima2(0)
            maxima2(1)
            dve.wait_ge(rs_done, ST["kv"] + 1)
            rq, rkv = rs[:, ST["q"]], rs[:, ST["kv"]]
            mq_flat = mq[:].rearrange("p m a d -> p m (a d)")
            for c, width in ((0, W), (1, 256)):
                g = G["uq"] + c
                for m in range(MT):
                    b = g % 2 * 2 + m
                    wait_acc(dve, g, m, S["uq"] + c)
                    dve.tensor_scalar(mq_flat[:, m, c * W:c * W + width], acc[b][:, 0:width], rq[:, m:m + 1], None,
                                      ALU.mult).then_inc(acc_drained[b], 1)
            for c in range(2):
                g = G["ukv"] + c
                for m in range(MT):
                    b = g % 2 * 2 + m
                    if m == 0 or c == 1:
                        wait_acc(dve, g, m, S["ukv"])
                    else:
                        dve.wait_ge(kv_half, 1)
                    src = acc[b][:, :].rearrange("p (a d) -> p a d", d=128)
                    dve.tensor_scalar(mk[:, m, 4 * c:4 * c + 4, 0:64], src[:, :, 0:64], rkv[:, m:m + 1], None,
                                      ALU.mult).then_inc(mk_nope, 1)
                    dve.tensor_scalar(mv[:, m, 4 * c:4 * c + 4, :], src[:, :, 64:128], rkv[:, m:m + 1], None,
                                      ALU.mult).then_inc(acc_drained[b], 1)
            def drain_values2(which, g):
                dve.wait_ge(pv2, 8 * which + 8)
                dve.reciprocal(inv2[:, which], sum2[:, which]).then_inc(inv2_done, 1)
                dve.wait_ge(inv2_done, which + 1)
                for m in range(MT):
                    b = g % 2 * 2 + m
                    dve.tensor_tensor(o2[:, which, m, :].rearrange("p (a d) -> p a d", d=HD),
                                      acc[b][:, :].rearrange("p (a d) -> p a d", d=HD),
                                      inv2[:, which, m, :].unsqueeze(2).to_broadcast([P, 8, HD]),
                                      ALU.mult).then_inc(acc_drained[b], 1)

            for n in range(16):
                x = prob_use(n)
                wait_tp_full(dve, x)
                if n >= 2:
                    dve.wait_ge(pv2, n - 1)
                dve.tensor_copy(pt2[:, n % 2, :], tp[x % 2][:, :]).then_inc(tp_free[x % 2], 1)
                if n == 5:
                    for k in range(4):
                        x = X["mqk"] + 2 * k + 1
                        wait_tp_full(dve, x)
                        dve.tensor_copy(mkT[:, 2 * k:2 * k + 2, :], two(tp[x % 2], 96)).then_inc(tp_free[x % 2], 1)
                if n + 2 < 16:
                    maxima2(n + 2)
                if 1 <= n < 5:
                    feed(S["out2"] + n - 1, 1)
                if n == 8:
                    drain_values2(0, G["na"])
                if n == 10:
                    for k in range(2):
                        split(X["ona"] + k, (2 * k, 2 * k + 1), pcol("na_g", 4), xt_hi, xt_lo, HI["ona"] + 2 * k)
                    mean_square("na")
            drain_values2(1, G["mla"])
            for m in range(MT):
                b = G["top"] % 2 * 2 + m
                dve.wait_ge(rs_done, ST["na"] + 1)
                wait_acc(dve, G["top"], m, S["out2"] + 1)
                dve.tensor_scalar(f[:, m, 0:W], acc[b][:, :], rs[:, ST["na"], m:m + 1], None, ALU.mult).then_inc(acc_drained[b], 1)
            feed(S["out2"] + 4, 2)
            for k in range(2):
                split(X["omla"] + k, (4 + 2 * k, 5 + 2 * k), par[:, PAR["mla_g"] - 4:PAR["mla_g"] + 4], xt_hi, xt_lo,
                      HI["omla"] + 2 * k)
            mean_square("mla")
            feed(S["out2"] + 6, 2)
            for m in range(MT):
                b = (G["top"] + 1) % 2 * 2 + m
                wait_acc(dve, G["top"] + 1, m, S["out2"] + 3)
                dve.tensor_scalar(f[:, m, W:D], acc[b][:, :], rs[:, ST["na"], m:m + 1], None, ALU.mult).then_inc(acc_drained[b], 1)
            feed(S["out2"] + 8, 3)
            dve.wait_ge(rs_done, ST["mla"] + 1)
            for c in range(2):
                for m in range(MT):
                    b = (G["bot"] + c) % 2 * 2 + m
                    v = f[:, m, c * W:(c + 1) * W]
                    wait_drained(dve, G["top"] + c, m)
                    wait_acc(dve, G["bot"] + c, m, S["out2"] + 5 + 2 * c)
                    dve.scalar_tensor_tensor(v, acc[b][:, :], rs[:, ST["mla"], m:m + 1], v, ALU.mult,
                                             ALU.add).then_inc(acc_drained[b], 1)
            feed(S["out2"] + 11, 1)
            mean_square("mix")
            for c in range(2):
                for m in range(MT):
                    v = f[:, m, c * W:(c + 1) * W]
                    ins = dve.tensor_tensor(v, v, row_gain[:, 2, c * W:(c + 1) * W], ALU.mult)
            step(ins)
            add_normed("mix", h_new)
            f3_g = pcol("f3_g")
            split_h("h4", f3_g, (0, 1))

            def statistics3():
                mean_square("h4")
                half_rstd_squared("h4", 3)
                dve.wait_ge(coef_done, 4)

            ffn(2, S["f3i"], S["f3o"], G["f3i"], "f3", "h4", f3_g, lambda: None, statistics3, coef[:, 3])
            dve.wait_ge(h_new, 8)
            feed(S["f3o"] + 6, 9)
            gained("f3", G["f3o"], 0, 3, S["f3o"] + 10)
            feed(S["f3o"] + 15, 7)
            gained("f3", G["f3o"] + 1, 1, 3, S["f3o"] + 21)
            mean_square("f3")
            for g in (G["f3o"], G["f3o"] + 1):
                for m in range(MT):
                    wait_drained(dve, g, m)
            add_normed("f3", out_ready)

        @block.gpsimd
        def _(pool):
            def feed(s, n=1, i=0, turns=0):
                for q in range(s, min(s + n, S["end"])):
                    if q % 2 == 1:
                        b = q % RING
                        wait(pool, hi_done[b], q // RING + 1, i, turns)
                        pool.tensor_tensor(w_lo[:, b, :], w_raw[:, b, :], w_hi[:, b, :].bitcast(F32),
                                           ALU.subtract).then_inc(lo_done[b], 1)

            def rstd(name):
                t = ST[name]
                wait(pool, ms_done, t + 1)
                pool.tensor_tensor(rs[:, t, :], ms[:, t, :], minus_half[:], ALU.pow).then_inc(rs_done, 1)

            pool.memset(blockdiag[:], 0.0).then_inc(bd_zero, 1)
            pool.memset(q_stage[:], 0.0).then_inc(q_zero, 1)
            feed(0, 4)
            pool.wait_ge(set_up, 1)
            rstd("x")
            with pool.Fori(0, 2) as i:
                feed(4, 8, i, 2)
            for n in range(4):
                wait_tp_free(pool, X["xg"] + 2 * n + 1)
            feed(20, 2)
            pool.tensor_tensor(gel, grT[:], grT[:], ALU.mult).then_inc(gelu_arg, 1)
            feed(22, 2)
            pool.wait_ge(gelu_arg, 1)
            pool.tensor_scalar(gel, gel, 0.044715, 1.0, ALU.mult, ALU.add).then_inc(gelu_arg, 1)
            feed(24, 2)
            pool.wait_ge(gelu_arg, 2)
            pool.tensor_tensor(gel, gel, grT[:], ALU.mult).then_inc(gelu_arg, 1)
            feed(26, 14)

            def stage(tile, group, i=0):
                pool.tensor_copy(q_stage[0:HD, 0::2, :], qkT[0:HD, tile, :]).then_inc(staged, 1)
                wait(pool, staged, 2 * group + 1, i, 4)
                pool.tensor_copy(q_stage[HD:P, 1::2, :], qkT[HD:P, tile, :]).then_inc(staged, 1)
                wait(pool, staged, 2 * group + 2, i, 4)

            wait_tp_free(pool, X["qk"])
            pool.wait_ge(q_zero, 1)
            stage(slice(0, 2), 0)
            feed(40, 4)
            for n in range(1, 4):
                wait_tp_free(pool, X["qk"] + 2 * n)
            with pool.Fori(0, 2) as i:
                for g in range(2):
                    s = 44 + 4 * g
                    feed(s, 2, i, 2)
                    wait(pool, scores_done, 4 * g + 4, i, 8)
                    stage(bass.ds(i * 4 + (2 * g + 2), 2), g + 1, i)
                    feed(s + 2, 2, i, 2)
            feed(60, S["f1i"] + 4 - 60)
            rstd("h1")
            feed(S["f1i"] + 4, 2)

            def hidden(s_in, s_out, first, between=None):
                feed(first, s_in + 8 - first)
                with pool.Fori(0, (FG - 1) // 2) as i:
                    feed(s_in + 8, 8, i, 2)
                for n in range(9):
                    feed(s_out + 4 + 2 * n, 2)
                    if between is not None and n < 8:
                        between(n)

            hidden(S["f1i"], S["f1o"], S["f1i"] + 6)
            feed(S["f1o"] + 22, 4)
            rstd("h2")
            feed(S["f2i"] + 4, 2)
            rstd("x2")

            def mask_head(hd):
                pool.wait_ge(late_landed, 16 * 5)
                pool.wait_ge(bias2_landed, 16 * 16)
                pool.tensor_tensor(bias2[:, hd], bias2[:, hd], na_mask[:].unsqueeze(1).to_broadcast([P, 6, 64]),
                                   ALU.add).then_inc(bias2_ready, 1)

            hidden(S["f2i"], S["f2o"], S["f2i"] + 6, mask_head)
            feed(S["f2o"] + 22, 4)
            rstd("f2")
            feed(S["in2"] + 4, 2)
            rstd("h3")
            feed(S["in2"] + 6, 4)
            rstd("q")
            rstd("kv")
            feed(S["in2"] + 10, 9)
            for c in range(2):
                for m in range(MT):
                    wait_drained(pool, G["uq"] + c, m)
            q1, q2 = mq[:, :, :, 64:80], mq[:, :, :, 80:96]
            c4 = cos[:].unsqueeze(2).to_broadcast([P, MT, 8, 16])
            s4 = sin[:].unsqueeze(2).to_broadcast([P, MT, 8, 16])
            pool.tensor_tensor(rope[:, 0], q1, c4, ALU.mult).then_inc(pool_step, 1)
            pool.tensor_tensor(rope[:, 1], q2, s4, ALU.mult).then_inc(pool_step, 1)
            pool.tensor_tensor(rope[:, 2], q2, c4, ALU.mult).then_inc(pool_step, 1)
            pool.tensor_tensor(rope[:, 3], q1, s4, ALU.mult).then_inc(pool_step, 1)
            pool.wait_ge(pool_step, 4)
            pool.tensor_tensor(q1, rope[:, 0], rope[:, 1], ALU.subtract).then_inc(rope_q, 1)
            pool.tensor_tensor(q2, rope[:, 2], rope[:, 3], ALU.add).then_inc(rope_q, 1)
            feed(S["out2"], 4)
            rstd("na")
            feed(S["out2"] + 4, 2)
            rstd("mla")
            feed(S["out2"] + 6, 6)
            rstd("mix")
            feed(S["f3i"] + 4, 2)
            rstd("h4")
            hidden(S["f3i"], S["f3o"], S["f3i"] + 6)
            rstd("f3")


_INS = ["x", "norm_mix_g", "w_in", "b_merge", "rel_table", "w_attn_out", "conv_w", "conv_b", "w_rg_r", "b_rg_r",
        "w_rg_i", "b_rg_i", "rg_lambda", "w_rnn_out", "w_o", "norm_ffn_g", "w_ffn_in", "w_ffn_out", "final_norm_g",
        "ffn1_pre_g_2", "ffn1_w_gu_2", "ffn1_w_down_2", "ffn1_post_g_2", "mix_pre_g_2", "w_in_2", "na_rpb_2",
        "mla_q_norm_g_2", "mla_w_uq_2", "mla_kv_norm_g_2", "mla_w_ukv_2", "na_out_norm_g_2", "mla_out_norm_g_2",
        "w_out_2", "mix_post_g_2", "ffn2_pre_g_2", "ffn2_w_gu_2", "ffn2_w_down_2", "ffn2_post_g_2"]


def constants():
    f32 = np.float32
    t = np.arange(T)
    inv_freq = (1.0 / (f32(10000.0) ** (np.arange(8, dtype=f32) / f32(8)))).astype(f32)
    ang = np.concatenate([(t // 64).astype(f32)[:, None] * inv_freq, (t % 64).astype(f32)[:, None] * inv_freq], -1)
    qc, kc = np.arange(64)[:, None], 63 - np.arange(64)[None, :]
    first = np.clip(qc - 8, 0, 48)
    mask = np.where((kc >= first) & (kc < first + 16), f32(0), f32(MASKED)).astype(f32)
    return {"c_cos": np.cos(ang).astype(f32), "c_sin": np.sin(ang).astype(f32), "c_mask": mask,
            "c_ident": np.eye(P, dtype=f32)}


def kernel(**inputs):
    import concourse.bacc as bacc
    from concourse.bass_utils import run_bass_kernel_spmd

    nc = bacc.Bacc("TRN2", target_bir_lowering=False, num_devices=1)
    arrays, aps = {}, {}
    given = {name: np.ascontiguousarray(inputs[name]) for name in _INS}
    for name, v in {**given, **constants()}.items():
        arrays[f"in_{name}"] = v
        aps[name] = nc.dram_tensor(f"in_{name}", v.shape, mybir.dt.from_np(v.dtype), kind="ExternalInput").ap()
    out = nc.dram_tensor("out_dram", (1, T, D), F32, kind="ExternalOutput").ap()
    build(nc, aps, out)
    r = run_bass_kernel_spmd(nc, [arrays], core_ids=[0])
    return r.results[0]["out_dram"]
```

```python
import numpy as np

import concourse.bass as bass
from concourse import mybir

F32 = mybir.dt.float32
F32R = mybir.dt.float32r
BF16 = mybir.dt.bfloat16
ACT = mybir.ActivationFunctionType
ALU = mybir.AluOpType

P = 128
D = 1024
T = 256
MT = T // P
KT = D // P
W = 512
RING = 4
SLAB = 1024
HEADS = 16
HD = 64
FF = 2816
FT = FF // P
FG = FF // 256
TURN = 2
HEAD = 1 + (FG - 1) % TURN
EPS = 1e-6
MASKED = -1e30
MLA_SCALE = 96 ** -0.5
GELU_C = 0.7978845608028654
CHUNK = 64


def starts(parts):
    out, at = {}, 0
    for name, n in parts:
        out[name] = at
        at += n
    out["end"] = at
    return out


S = starts([("in", 56), ("rnn", 8), ("attn", 8), ("o", 8), ("f1i", 4 * FG), ("f1o", 22), ("f2i", 4 * FG),
            ("f2o", 22), ("in2", 16), ("uq", 2), ("ukv", 1), ("out2", 8), ("f3i", 4 * FG), ("f3o", 22)])
G = starts([("in", 14), ("rnn", 2), ("attn", 2), ("o", 2), ("f1i", FG), ("f1o", 2), ("f2i", FG), ("f2o", 2),
            ("in2", 4), ("uq", 2), ("ukv", 2), ("na", 1), ("mla", 1), ("top", 2), ("bot", 2), ("f3i", FG), ("f3o", 2)])
MQK_AT, ONA_AT = 4, 10
X = starts([("x", 4), ("par", 1), ("xg", 8), ("gate", 8), ("qk", 8), ("p1", 16), ("at", 4), ("mt", 4), ("h1", 4),
            ("f1", FG), ("h2", 4), ("f2", FG), ("h3", 4), ("c", 2), ("nqk", 4)]
           + [use for n in range(16) for use in ((f"probs{n}", 1), (f"mqk{n - MQK_AT}", 2 * (0 <= n - MQK_AT < 4)),
                                                  (f"ona{n - ONA_AT}", 0 <= n - ONA_AT < 2))]
           + [("omla", 2), ("h4", 4), ("f3", FG)])
HI = starts([("x", 8), ("rg", 1), ("at", 4), ("mt", 4), ("h1", 8), ("f1", FG), ("h2", 8), ("f2", FG), ("h3", 16),
             ("c", 3), ("ona", 4), ("omla", 4), ("h4", 16), ("f3", FG)])
STATS = [("x", D, 1), ("h1", D, 4), ("h2", D, 1), ("x2", D, 4), ("f2", D, 4), ("h3", D, 1), ("q", 256, 1),
         ("kv", 128, 1), ("na", 512, 1), ("mla", 512, 1), ("mix", D, 1), ("h4", D, 4), ("f3", D, 4)]
ST = {name: n for n, (name, _, _) in enumerate(STATS)}
BY_TILE = ("f2", "mix", "f3")
NTH, _n = {}, 0
for _name, _, _ in STATS:
    _n += MT if _name in BY_TILE else 1
    NTH[_name] = _n
SQUARES = []
for _n in ("x",):
    SQUARES += [(_n, 0, m) for m in range(MT)]
for _n in ("h1", "h2"):
    SQUARES += [(_n, c, m) for c in range(2) for m in range(MT)]
SQUARES += [("x2", 0, m) for m in range(MT)]
SQUARES += [("f2", c, m) for c in range(2) for m in range(MT)]
SQUARES += [("h3", c, m) for m in range(MT) for c in range(2)]
SQUARES += [(_n, 0, m) for _n in ("q", "kv", "na", "mla") for m in range(MT)]
for _n in ("mix", "h4"):
    SQUARES += [(_n, c, m) for m in range(MT) for c in range(2)]
SQUARES += [("f3", c, m) for c in range(2) for m in range(MT)]
SQ = {key: n for n, key in enumerate(SQUARES)}
TWO_HALVES = {key[0] for key in SQUARES if key[1] == 1}

PAR = starts([("mix_g", 8), ("ffn_g", 8), ("fin_g", 8), ("f2_g", 8), ("mix2_g", 8), ("f3_g", 8), ("conv_w", 32),
              ("conv_b", 8), ("b_r", 8), ("b_i", 8), ("lam", 8), ("q_g", 2), ("kv_g", 1), ("na_g", 4), ("mla_g", 4)])


def build(nc, a, out):
    top = [16512]

    def place(name, shape, dt, at=None):
        size = int(np.prod(shape[1:])) * (2 if dt == BF16 else 4)
        size = (size + 31) // 32 * 32
        if at is None:
            at = top[0]
            top[0] += size
        return nc.alloc_sbuf_tensor_at(name, shape, dt, offset=at)

    def size_of(*dims):
        return 4 * int(np.prod(dims))

    w_raw = place("w_raw", [P, RING, SLAB], F32)
    w_hi = place("w_hi", [P, RING, SLAB], F32R)
    w_lo = place("w_lo", [P, RING, SLAB], F32R)
    h = place("h", [P, MT, D], F32)
    xt_hi = place("xt_hi", [P, KT, T], F32R)
    xt_lo = place("xt_lo", [P, KT, T], F32R)
    ident = place("ident", [P, P], F32)
    par_rows = place("par_rows", [P, P], F32)
    par = place("par", [P, P], F32)
    gain_x = place("gain_x", [P, KT], F32)
    small = place("small", [P, 16, KT], F32)
    ssq = place("ssq", [P, len(STATS), 2, MT], F32)
    ms = place("ms", [P, len(STATS), MT], F32)
    rs = place("rs", [P, len(STATS), MT], F32)
    coef = place("coef", [P, 8, MT], F32)
    minus_half = place("minus_half", [P, MT], F32)
    junk = place("junk", [P, D], BF16)
    base = top[0]

    u = place("u", [P, 7, MT, D], F32)
    xrT_at = top[0]
    xrT = place("xrT", [P, KT, T + 4], F32)
    ti = place("ti", [P, KT, T], F32)
    yt_hi = place("yt_hi", [P, KT, T], F32R, at=xrT_at)
    yt_lo = place("yt_lo", [P, KT, T], F32R, at=xrT_at + size_of(KT, T))
    grT = place("grT", [P, KT, T], F32)
    qkT = place("qkT", [P, 2 * KT, T], F32)
    bias1 = place("bias1", [P, 2, 4, T], F32)
    blockdiag = place("blockdiag", [P, 16, P], F32)
    b_merge = place("b_merge", [P, 2 * D], F32)
    q_stage = place("q_stage", [P, 4, T], F32)
    sb1 = place("sb1", [P, 2, 384], F32)
    pt1 = place("pt1", [P, 2, 384], F32)
    ext_sb = nc.alloc_sbuf_tensor_at("ext_sb", [HEADS, 384], F32, offset=top[0] - size_of(2, 384))
    mx1 = place("mx1", [P, 2, 4], F32)
    carrier = place("carrier", [P, 8], F32)
    free_marks = place("free_marks", [P, 8], F32)
    nm1 = place("nm1", [P, 2, 4], F32)
    sum1 = place("sum1", [P, 2, 4], F32)
    inv1 = place("inv1", [P, 2, 4], F32)
    assert top[0] <= 229368, top[0]
    flat = lambda t: t[:, :, :].rearrange("p a b -> p (a b)")
    xcT = u[:, 0].rearrange("p m n -> p (m n)").rearrange("p (k t) -> p k t", t=T)
    trT = u[:, 1].rearrange("p m n -> p (m n)").rearrange("p (k t) -> p k t", t=T)
    gel = u[:, 5].rearrange("p m n -> p (m n)").rearrange("p (k t) -> p k t", t=T)
    sq = u[:, 6].rearrange("p m n -> p (m n)").rearrange("p (k t) -> p k t", t=T)
    att = u[:, 2]
    merged = u[:, 3]

    top[0] = base
    hid_hi = place("hid_hi", [P, FT, T], F32R)
    hid_lo = place("hid_lo", [P, FT, T], F32R)
    th = place("th", [P, MT, 256], F32)
    u1 = place("u1", [P, MT, 256], F32)
    hid = place("hid", [P, 2, MT, 256], F32)
    below = top[0]
    f = place("f", [P, MT, D], F32)
    row_gain = place("row_gain", [P, 4, D], F32)
    ext2_sb = place("ext2_sb", [8, 7, P], F32)
    rpb_sb = place("rpb_sb", [8, 15, 31], F32)
    bias2 = place("bias2", [P, 8, 6, 64], F32)
    na_mask = place("na_mask", [P, 64], F32)
    cos = place("cos", [P, MT, 16], F32)
    sin = place("sin", [P, MT, 16], F32)

    u2 = place("u2", [P, MT, 1952], F32)
    mqT = place("mqT", [96, 8, T], F32)
    mkT = place("mkT", [96, 8, T], F32)
    mx2 = place("mx2", [P, 2, 2], F32)
    nm2 = place("nm2", [P, 2, 2], F32)
    sum2 = place("sum2", [P, 2, MT, 8], F32)
    inv2 = place("inv2", [P, 2, MT, 8], F32)
    assert top[0] <= 229368, top[0]
    top[0] = base
    nqk = place("nqk", [P, 8, T], F32)
    c_hi = place("c_hi", [P, 3, T], F32R)
    c_lo = place("c_lo", [P, 3, T], F32R)
    mq = place("mq", [P, MT, 8, 96], F32)
    mk = place("mk", [P, MT, 8, 96], F32)
    mv = place("mv", [P, MT, 8, 64], F32)
    o2 = place("o2", [P, 2, MT, 512], F32)
    rope = place("rope", [P, 4, MT, 8, 16], F32)
    kr = place("kr", [P, 4, MT, 16], F32)
    sb2 = place("sb2", [P, 2, W], F32)
    pt2 = place("pt2", [P, 2, W], F32)
    assert top[0] <= below, (top[0], below)

    acc = [nc.alloc_psum_tensor(f"acc{b}", [P, W], F32) for b in range(4)]
    tp = [nc.alloc_psum_tensor(f"tp{b}", [P, W], F32) for b in range(2)]
    sc = [nc.alloc_psum_tensor(f"sc{b}", [P, W], F32) for b in range(2)]

    ext_dram = nc.dram_tensor("ext_dram", [HEADS, 384], F32)
    ext2_dram = nc.dram_tensor("ext2_dram", [8, 7, P], F32)

    sem = nc.alloc_semaphore
    raw_landed = [sem(f"raw_landed{b}") for b in range(RING)]
    hi_done = [sem(f"hi_done{b}") for b in range(RING)]
    lo_done = [sem(f"lo_done{b}") for b in range(RING)]
    slab_used = [sem(f"slab_used{b}") for b in range(RING)]
    acc0_full = [sem(f"acc0_full{b}") for b in range(2)]
    acc_drained = [sem(f"acc_drained{b}") for b in range(4)]
    tp_full = [sem(f"tp_full{b}") for b in range(2)]
    tp_free = [sem(f"tp_free{b}") for b in range(2)]
    hi_written = sem("hi_written")
    ssq_done, ms_done, rs_done = sem("ssq_done"), sem("ms_done"), sem("rs_done")
    x_landed = [sem("x_landed0"), sem("x_landed1")]
    ident_landed, gain_x_landed, par_landed = sem("ident_landed"), sem("gain_x_landed"), sem("par_landed")
    bd_zero, bd_landed, q_zero = sem("bd_zero"), sem("bd_landed"), sem("q_zero")
    merge_landed = sem("merge_landed")
    table_landed, ext_done, ext_stored = sem("table_landed"), sem("ext_done"), sem("ext_stored")
    bias_landed = [sem("bias_landed0"), sem("bias_landed1")]
    set_up, warm = sem("set_up"), sem("warm")
    consts_ready = sem("consts_ready")
    abs_lam, exp_lam = sem("abs_lam"), sem("exp_lam")
    conv_done = sem("conv_done")
    gates_done, decay_done = sem("gates_done"), sem("decay_done")
    mult2_done, mult_done, bx_done, rec_done = sem("mult2_done"), sem("mult_done"), sem("bx_done"), sem("rec_done")
    gelu_arg, gelu_tanh, rg_out = sem("gelu_arg"), sem("gelu_tanh"), sem("rg_out")
    yt_ready = sem("yt_ready")
    staged, scores_done, ttr_done, negmax_done = sem("staged"), sem("scores_done"), sem("ttr_done"), sem("negmax_done")
    probs_done, pv_done, inv_done, o_drained = sem("probs_done"), sem("pv_done"), sem("inv_done"), sem("o_drained")
    gate_tanh = sem("gate_tanh")
    m_ready = sem("m_ready")
    coef_done = sem("coef_done")
    x2_ready = sem("x2_ready")
    tanh_done, u1_done = sem("tanh_done"), sem("u1_done")
    rows_landed, late_landed = sem("rows_landed"), sem("late_landed")
    ext2_done, ext2_stored = sem("ext2_done"), sem("ext2_stored")
    bias2_landed, bias2_ready = sem("bias2_landed"), sem("bias2_ready")
    h_new = sem("h_new")
    kv_half = sem("kv_half")
    rope_q, rope_k = sem("rope_q"), sem("rope_k")
    scores2, max2, negmax2, probs2, pv2 = sem("scores2"), sem("max2"), sem("negmax2"), sem("probs2"), sem("pv2")
    inv2_done = sem("inv2_done")
    out_ready, out_stored = sem("out_ready"), sem("out_stored")
    dve_step, pool_step = sem("dve_step"), sem("pool_step")

    def n_of(n, i=0, per=0):
        return n if isinstance(i, int) and i == 0 else i * per + n

    def wait(e, s, n, i=0, per=0):
        assert n > 0 or isinstance(i, int), "a wait in a loop starts above zero"
        if not (isinstance(i, int) and n + i * per <= 0):
            e.wait_ge(s, n_of(n, i, per))

    def wait_acc(e, g, m, last_slab, i=0, slab_turns=0, acc_turns=0):
        if m == 0:
            wait(e, acc0_full[g % 2], g // 2 + 1, i, acc_turns)
        else:
            wait(e, slab_used[last_slab % RING], last_slab // RING + 1, i, slab_turns)

    def wait_drained(e, g, m, i=0, turns=0):
        wait(e, acc_drained[g % 2 * 2 + m], g // 2 + 2, i, turns)

    def wait_bank(e, g, m, i=0, turns=0):
        wait(e, acc_drained[g % 2 * 2 + m], g // 2 + 1, i, turns)

    def wait_both_drained(e, g, i=0, turns=0):
        wait_drained(e, g, 1, i, turns)

    def wait_tp_full(e, x, i=0, turns=0):
        wait(e, tp_full[x % 2], x // 2 + 1, i, turns)

    def wait_tp_free(e, x, i=0, turns=0):
        wait(e, tp_free[x % 2], x // 2 + 1, i, turns)

    def two(bank, parts=P):
        return bank[0:parts, :].rearrange("p (k t) -> p k t", k=2)

    block = nc.Block()
    with block:
        @block.sync
        def _(sp):
            def slab(s, halves, i=0, turns=0):
                if s >= RING or turns:
                    wait(sp, lo_done[s % RING], s // RING, i, turns)
                for dst, src in halves:
                    sp.dma_start(dst, src).then_inc(raw_landed[s % RING], 32 // len(halves))

            def rect(s, w, row, col, n=W):
                dst = w_raw[:, s % RING, 0:2 * n].rearrange("p (j n) -> p j n", j=2)
                return [(dst, w.rearrange("(r p) n -> p r n", p=P)[:, row // P:row // P + 2, bass.ds(col, n)])]

            def gate_up(s, w, row, col):
                src = w.rearrange("(r p) (g n) -> r p g n", p=P, g=2)
                return [(w_raw[:, s % RING, j * W:(j + 1) * W].rearrange("p (g n) -> p g n", g=2),
                         src[row // P + j][:, :, bass.ds(col, 256)]) for j in range(2)]

            def rows_k(w, s0, groups, col0):
                with sp.Fori(0, groups) as c:
                    for q in range(4):
                        s = s0 + q
                        slab(s, rect(s, w, 256 * q, c * W + col0), c, 1)

            def ffn_in(w, s0):
                with sp.Fori(0, FG) as c:
                    for q in range(4):
                        slab(s0 + q, gate_up(s0 + q, w, 256 * q, c * 256), c, 1)

            def ffn_out(w, s0, after={}):
                for n in range(22):
                    slab(s0 + n, rect(s0 + n, w, 256 * (n % 11), n // 11 * W))
                    if n in after:
                        after[n]()

            xv = a["x"].rearrange("b (m p) d -> p (b m) d", p=P)
            sp.dma_start(h[:, 0, :], xv[:, 0, :]).then_inc(x_landed[0], 16)
            sp.dma_start(h[:, 1, :], xv[:, 1, :]).then_inc(x_landed[1], 16)
            w_in = a["w_in"][0]
            for q in range(4):
                slab(q, rect(q, w_in, 256 * q, 3 * D))
            for name, key in (("mix_g", "norm_mix_g"), ("ffn_g", "norm_ffn_g"), ("fin_g", "final_norm_g"),
                              ("f2_g", "ffn1_pre_g_2"), ("mix2_g", "mix_pre_g_2"), ("f3_g", "ffn2_pre_g_2"),
                              ("conv_w", "conv_w"), ("conv_b", "conv_b"), ("b_r", "b_rg_r"), ("b_i", "b_rg_i"),
                              ("lam", "rg_lambda"), ("q_g", "mla_q_norm_g_2"), ("kv_g", "mla_kv_norm_g_2"),
                              ("na_g", "na_out_norm_g_2"), ("mla_g", "mla_out_norm_g_2")):
                v = a[key]
                v = v.rearrange("(r c) -> r c", c=P) if len(v.shape) == 1 else \
                    v.rearrange("a (r c) -> (a r) c", c=P) if len(v.shape) == 2 else \
                    v.rearrange("a b (r c) -> (a b r) c", c=P)
                sp.dma_start(par_rows[PAR[name]:PAR[name] + v.shape[0], :], v).then_inc(par_landed, 16)
            rows_k(w_in, 4, 3, 3 * D + W)
            sp.wait_ge(bd_zero, 1)
            for n, key in enumerate(("w_rg_r", "w_rg_i")):
                wv = a[key][0].rearrange("(k two) d e -> two d k e", two=2)
                for side in range(2):
                    sp.dma_start(blockdiag[64 * side:64 * side + 64, 8 * n:8 * n + 8, 64 * side:64 * side + 64],
                                  wv[side]).then_inc(bd_landed, 16)
            sp.dma_start(ext_sb[:, 0:256], a["rel_table"][0][:, 1:257]).then_inc(table_landed, 16)
            sp.dma_start(b_merge[:], a["b_merge"][0].partition_broadcast(P)).then_inc(merge_landed, 16)
            rows_k(w_in, 16, 6, 0)
            sp.wait_ge(ext_done, 1)
            sp.dma_start(ext_dram.ap(), ext_sb[:]).then_inc(ext_stored, 16)
            sp.wait_ge(ext_stored, 16)
            strips = bass.AP(ext_dram, 0, [[1, P], [384, HEADS], [1, T]])
            with sp.Fori(0, 2) as i:
                for g in range(2):
                    for q in range(4):
                        s = 40 + 4 * g + q
                        slab(s, rect(s, w_in, 256 * q, i * D + (5 * D + g * W)), i, 2)
                    wait(sp, ttr_done, 8 * g + 1, i, 16)
                    heads = strips[:, bass.ds(i * 8 + 4 * g, 4), :]
                    sp.dma_start(bias1[0:CHUNK, g, :, CHUNK:T], heads[0:CHUNK, :, CHUNK:T]).then_inc(bias_landed[g], 16)
                    sp.dma_start(bias1[CHUNK:P, g], heads[CHUNK:P]).then_inc(bias_landed[g], 16)
            rows_k(a["w_rnn_out"][0], S["rnn"], 2, 0)
            rows_k(a["w_attn_out"][0], S["attn"], 2, 0)
            rows_k(a["w_o"][0], S["o"], 2, 0)
            ffn_in(a["w_ffn_in"][0], S["f1i"])
            for n, name in enumerate(("final_norm_g", "ffn1_post_g_2", "mix_post_g_2", "ffn2_post_g_2")):
                if n == 0:
                    for m in range(MT):
                        wait_drained(sp, G["o"] + 1, m)
                v = a[name] if name == "final_norm_g" else a[name][0]
                sp.dma_start(row_gain[:, n, :], v.partition_broadcast(P)).then_inc(rows_landed, 16)
            sp.dma_start(na_mask[0:64, :], a["c_mask"]).then_inc(late_landed, 16)
            sp.dma_start(na_mask[64:128, :], a["c_mask"]).then_inc(late_landed, 16)
            sp.dma_start(cos[:], a["c_cos"].rearrange("(m p) n -> p m n", p=P)).then_inc(late_landed, 16)
            sp.dma_start(sin[:], a["c_sin"].rearrange("(m p) n -> p m n", p=P)).then_inc(late_landed, 16)
            sp.dma_start(rpb_sb[:], a["na_rpb_2"][0]).then_inc(late_landed, 16)

            def store_ext2():
                sp.wait_ge(ext2_done, 1)
                sp.dma_start(ext2_dram.ap(), ext2_sb[:]).then_inc(ext2_stored, 16)

            def load_bias2(hd):
                sp.wait_ge(ext2_stored, 16)
                for qr in range(2):
                    src = bass.AP(ext2_dram, (hd * 7 + 1 - qr) * P, [[1, 64], [P, 6], [1, 64]])
                    sp.dma_start(bias2[64 * qr:64 * qr + 64, hd], src).then_inc(bias2_landed, 16)

            ffn_out(a["w_ffn_out"][0], S["f1o"],
                    after={10: store_ext2, **{12 + hd: lambda hd=hd: load_bias2(hd) for hd in range(8)}})
            ffn_in(a["ffn1_w_gu_2"][0], S["f2i"])
            ffn_out(a["ffn1_w_down_2"][0], S["f2o"])
            w2 = a["w_in_2"][0]
            for q in range(4):
                slab(S["in2"] + q, rect(S["in2"] + q, w2, 256 * q, 1536, 416))
            rows_k(w2, S["in2"] + 4, 3, 0)
            slab(S["uq"], rect(S["uq"], a["mla_w_uq_2"][0], 0, 0))
            slab(S["uq"] + 1, rect(S["uq"] + 1, a["mla_w_uq_2"][0], 0, W, 256))
            slab(S["ukv"], [(w_raw[:, S["ukv"] % RING, :], a["mla_w_ukv_2"][0])])
            for q in range(8):
                half, c, r = q // 4, q // 2 % 2, q % 2
                s = S["out2"] + q
                slab(s, rect(s, a["w_out_2"][0], 512 * half + 256 * r, c * W))
            ffn_in(a["ffn2_w_gu_2"][0], S["f3i"])
            ffn_out(a["ffn2_w_down_2"][0], S["f3o"])
            ov = out.rearrange("b (m p) d -> p (b m) d", p=P)
            for n in range(4):
                m, c = n // 2, n % 2
                sp.wait_ge(out_ready, n + 1)
                sp.dma_start(ov[:, m, c * W:(c + 1) * W], h[:, m, c * W:(c + 1) * W]).then_inc(out_stored, 16)
            sp.wait_ge(out_stored, 64)

        @block.scalar
        def _(act):
            def feed(s, n=1, i=0, turns=0):
                for q in range(s, min(s + n, S["end"])):
                    b = q % RING
                    wait(act, raw_landed[b], 32 * (q // RING + 1), i, 32 * turns)
                    wait(act, slab_used[b], q // RING, i, turns)
                    act.activation(w_hi[:, b, :], w_raw[:, b, :], ACT.Copy).then_inc(hi_done[b], 1)

            def square(stat, c, m, src):
                n = SQ[stat, c, m]
                wait(act, ssq_done, n) if n > 0 else act.wait_ge(warm, 1)
                act.activation(junk[:, 0:src.free_size()], src, ACT.Square,
                               accum_out=ssq[:, ST[stat], c, m:m + 1]).then_inc(ssq_done, 1)

            def split(x, tiles, gain, dst, scale=1.0, i=0, turns=0):
                wait_tp_full(act, x, i, turns)
                if gain is None:
                    act.activation(dst, two(tp[x % 2]), ACT.Copy, scale=scale).then_inc(hi_written, 1)
                else:
                    for n, k in enumerate(tiles):
                        act.activation(dst[:, k, :], tp[x % 2][:, n * T:(n + 1) * T], ACT.Copy,
                                       scale=gain[:, k:k + 1]).then_inc(hi_written, 1)

            act.dma_start(ident[:], a["c_ident"]).then_inc(ident_landed, 16)
            with nc.allow_non_contiguous_dma(reason="a column of gains"):
                act.dma_start(gain_x[:], a["norm_mix_g"][0].rearrange("(k p) -> p k", p=P)).then_inc(gain_x_landed, 16)
            act.wait_ge(set_up, 1)
            act.activation(junk[:, 0:MT], minus_half[:], ACT.Exp).then_inc(warm, 1)
            act.wait_ge(gain_x_landed, 16)
            for n in range(4):
                split(X["x"] + n, (2 * n, 2 * n + 1), gain_x, xt_hi)
                if n > 0:
                    feed(n - 1, 1)
            feed(3, 1)
            for m in range(MT):
                square("x", 0, m, h[:, m, :])
            with act.Fori(0, 2) as i:
                feed(4, 8, i, 2)
            act.wait_ge(set_up, 2)
            for n in range(4):
                x = X["xg"] + 2 * n
                wait_tp_full(act, x)
                act.activation(xrT[:, 2 * n:2 * n + 2, 3:3 + T],
                               two(tp[x % 2]), ACT.Copy).then_inc(tp_free[x % 2], 1)
            act.wait_ge(abs_lam, 1)
            act.activation(small[:, 1, :], small[:, 0, :], ACT.Exp, scale=-1.0).then_inc(exp_lam, 1)
            feed(20, 11)
            act.wait_ge(consts_ready, 1)
            for n in range(KT):
                x = X["gate"] + n
                wait_tp_full(act, x)
                act.activation(trT[:, n, :], tp[x % 2][:, 0:T], ACT.Tanh, scale=0.5,
                               bias=small[:, 8, n:n + 1]).then_inc(gates_done, 1)
                act.activation(ti[:, n, :], tp[x % 2][:, T:2 * T], ACT.Tanh, scale=0.5,
                               bias=small[:, 9, n:n + 1]).then_inc(tp_free[x % 2], 1)
            act.wait_ge(conv_done, KT)
            for n in range(KT):
                act.wait_ge(gates_done, n + 1)
                act.activation(xrT[:, n, 0:T], trT[:, n, :], ACT.Exp, scale=small[:, 7, n:n + 1],
                               bias=small[:, 7, n:n + 1]).then_inc(decay_done, 1)
                act.activation(trT[:, n, :], trT[:, n, :], ACT.Tanh, scale=small[:, 6, n:n + 1],
                               bias=small[:, 6, n:n + 1]).then_inc(decay_done, 1)
                if n % 2 and n < 7:
                    feed(31 + n // 2, 1)
            feed(34, 1)
            act.wait_ge(gelu_arg, 3)
            act.activation(gel, gel, ACT.Tanh, scale=GELU_C).then_inc(gelu_tanh, 1)
            feed(35, 1)
            act.wait_ge(mult2_done, 2)
            act.activation(sq, sq, ACT.Sqrt).then_inc(mult_done, 1)
            feed(36, 2)
            for n in range(4):
                x = X["qk"] + 2 * n
                wait_tp_full(act, x)
                act.activation(qkT[:, 2 * n:2 * n + 2, :], two(tp[x % 2]),
                               ACT.Copy, scale=HD ** -0.5).then_inc(tp_free[x % 2], 1)
                feed((38, 39, 41, 42)[n], (1, 2, 1, 1)[n])
            act.wait_ge(rg_out, 1)
            act.activation(flat(yt_hi), trT.rearrange("p k t -> p (k t)"), ACT.Copy).then_inc(hi_written, 1)
            feed(43, 1)
            def exps1(par_, r, i):
                for hh in range(2):
                    wait(act, negmax_done, 2 * par_ + r + 1, i, 4)
                    for m in range(MT):
                        cols = slice(0, P) if m == 0 else slice(P, 384)
                        v = sb1[:, hh, cols]
                        ins = act.activation(v, v, ACT.Exp, bias=nm1[:, r, 2 * hh + m:2 * hh + m + 1],
                                             accum_out=sum1[:, r, 2 * hh + m:2 * hh + m + 1])
                    ins.then_inc(probs_done, 1)

            def probs_T1(par_, r, i):
                for hh in range(2):
                    x = X["p1"] + 4 * par_ + 2 * r + hh
                    wait_tp_full(act, x, i, 4)
                    act.activation(pt1[:, hh, :], tp[x % 2][:, 0:384], ACT.Copy).then_inc(tp_free[x % 2], 1)

            with act.Fori(0, 2) as i:
                for g in range(2):
                    s = 44 + 4 * g
                    exps1(g, 0, i)
                    feed(s, 2, i, 2)
                    probs_T1(g, 0, i)
                    exps1(g, 1, i)
                    feed(s + 2, 1, i, 2)
                    probs_T1(g, 1, i)
                    feed(s + 3, 1, i, 2)
                    for m in range(MT):
                        wait_drained(act, G["in"] + 10 + g, m, i, 1)
                        v = u[:, bass.ds(i + 5, 1), m, g * W:(g + 1) * W]
                        act.activation(v, v, ACT.Tanh, scale=0.5).then_inc(gate_tanh, 1)
            feed(S["rnn"] + 4, 4)
            for n in range(4):
                split(X["at"] + n, None, None, xt_hi[:, 2 * n:2 * n + 2, :])
                if n == 1:
                    feed(S["rnn"] + 8, 1)
            feed(S["rnn"] + 9, 3)
            feed(S["attn"] + 4, 7)
            for n in range(2):
                split(X["mt"] + n, None, None, yt_hi[:, 2 * n:2 * n + 2, :], 0.5)
            feed(S["attn"] + 11, 2)
            for n in range(2, 4):
                split(X["mt"] + n, None, None, yt_hi[:, 2 * n:2 * n + 2, :], 0.5)
            feed(S["o"] + 5, 3)
            for m in range(MT):
                wait_drained(act, G["o"], m)
                square("h1", 0, m, h[:, m, 0:W])
            feed(S["o"] + 8, 3)
            ffn_g = par[:, PAR["ffn_g"]:PAR["ffn_g"] + KT]
            for n in range(2):
                split(X["h1"] + n, (2 * n, 2 * n + 1), ffn_g, xt_hi)
            feed(S["o"] + 11, 1)

            def ffn(s_in, s_out, g_in, x_hid, x_h, gain, stat, before, half1, hr, after_first):
                before()
                feed(s_in + 4, 1)
                if x_h is not None:
                    for n in range(2, 4):
                        split(x_h + n, (2 * n, 2 * n + 1), gain, xt_hi)
                feed(s_in + 5, 1)
                half1()
                feed(s_in + 6, 1)
                after_first()
                feed(s_in + 7, 1)

                def tanhs(g, i=0):
                    for m in range(MT):
                        wait_acc(act, g_in + g, m, s_in + 4 * g + 3, i, TURN, TURN // 2)
                        wait_drained(act, g_in + g - 1, m, i, TURN // 2)
                        act.activation(th[:, m, :], acc[(g_in + g) % 2 * 2 + m][:, 0:256], ACT.Tanh,
                                       scale=hr[:, m:m + 1]).then_inc(tanh_done, 1)

                wait(act, rs_done if stat is not None else coef_done, stat if stat is not None else 2)
                tanhs(0)

                def one_group(g, i=0):
                    feed(s_in + 4 * g + 4, 2, i, TURN)
                    tiles = bass.ds(i * (2 * TURN) + 2 * (g - 1), 2)
                    split(x_hid + g - 1, None, None, hid_hi[:, tiles, :], 1.0, i, TURN // 2)
                    feed(s_in + 4 * g + 6, 2, i, TURN)
                    tanhs(g, i)

                for g in range(1, HEAD):
                    one_group(g)
                with act.Fori(0, (FG - HEAD) // TURN) as i:
                    for g in range(HEAD, HEAD + TURN):
                        one_group(g, i)
                feed(s_out + 4, 2)
                split(x_hid + FG - 1, None, None, hid_hi[:, FT - 2:FT, :])

            def squares_h(stat, c, g_o):
                for m in range(MT):
                    wait_drained(act, g_o, m)
                    square(stat, c, m, h[:, m, c * W:(c + 1) * W])

            ffn(S["f1i"], S["f1o"], G["f1i"], X["f1"], X["h1"], ffn_g, NTH["h1"],
                lambda: squares_h("h1", 1, G["o"] + 1), lambda: None, rs[:, ST["h1"]], lambda: None)
            feed(S["f1o"] + 6, 9)
            squares_h("h2", 0, G["f1o"])
            feed(S["f1o"] + 15, 7)
            f2_gain = small[:, 11, :]
            for n in range(2):
                split(X["h2"] + n, (2 * n, 2 * n + 1), f2_gain, xt_hi)
            feed(S["f1o"] + 22, 4)

            def second():
                for m in range(MT):
                    act.wait_ge(x2_ready, m + 1)
                    square("x2", 0, m, h[:, m, :])

            ffn(S["f2i"], S["f2o"], G["f2i"], X["f2"], X["h2"], f2_gain, None,
                lambda: squares_h("h2", 1, G["f1o"] + 1), lambda: None, coef[:, 1], second)

            def post_squares(stat, c, g, last_slab, ms=range(MT)):
                for m in ms:
                    wait_acc(act, g, m, last_slab)
                    square(stat, c, m, acc[g % 2 * 2 + m][:, :])

            feed(S["f2o"] + 6, 9)
            post_squares("f2", 0, G["f2o"], S["f2o"] + 10)
            feed(S["f2o"] + 15, 7)
            mix2_g = par[:, PAR["mix2_g"]:PAR["mix2_g"] + KT]

            def split_new(name, m, gain):
                for half in range(2):
                    x = X[name] + 2 * m + half
                    wait_tp_full(act, x)
                    for n in range(4):
                        k = 4 * half + n
                        act.activation(xt_hi[:, k, m * P:(m + 1) * P], tp[x % 2][:, n * P:(n + 1) * P], ACT.Copy,
                                       scale=gain[:, k:k + 1]).then_inc(hi_written, 1)

            def squares_new(name, m):
                for c in range(2):
                    square(name, c, m, h[:, m, c * W:(c + 1) * W])

            post_squares("f2", 1, G["f2o"] + 1, S["f2o"] + 21, (0,))
            feed(S["in2"], 2)
            split_new("h3", 0, mix2_g)
            post_squares("f2", 1, G["f2o"] + 1, S["f2o"] + 21, (1,))
            feed(S["in2"] + 2, 2)
            squares_new("h3", 0)
            split_new("h3", 1, mix2_g)
            squares_new("h3", 1)
            feed(S["in2"] + 4, 6)
            for stat, c0, n in (("q", 1536, 256), ("kv", 1792, 128)):
                for m in range(MT):
                    wait_drained(act, G["in2"], m)
                    square(stat, 0, m, u2[:, m, c0:c0 + n])
            split(X["c"], (0, 1), par[:, PAR["q_g"]:PAR["q_g"] + 2], c_hi)
            split(X["c"] + 1, (2,), par[:, PAR["kv_g"] - 2:PAR["kv_g"] + 1], c_hi)
            feed(S["in2"] + 10, 8)
            for n in range(2):
                x = X["nqk"] + 2 * n
                wait_tp_full(act, x)
                act.activation(nqk[:, 2 * n:2 * n + 2, :], two(tp[x % 2]),
                               ACT.Copy, scale=HD ** -0.5).then_inc(tp_free[x % 2], 1)
            feed(S["ukv"], 1)
            for n in range(16):
                latent = n >= 8
                act.wait_ge(negmax2, n + 1)
                if n >= 2:
                    wait_tp_full(act, X[f"probs{n - 2}"])
                for m in range(MT):
                    dst = sb2[:, n % 2, m * T:(m + 1) * T]
                    src = sc[n % 2][:, m * T:(m + 1) * T] if latent else dst
                    ins = act.activation(dst, src, ACT.Exp, scale=MLA_SCALE if latent else 1.0,
                                         bias=nm2[:, n % 2, m:m + 1],
                                         accum_out=sum2[:, n // 8, m, n % 8:n % 8 + 1])
                ins.then_inc(probs2, 1)
                k = n - 1 - MQK_AT
                if 0 <= k < 4:
                    x = X[f"mqk{k}"]
                    wait_tp_full(act, x)
                    act.activation(mqT[:, 2 * k:2 * k + 2, :], two(tp[x % 2], 96), ACT.Copy).then_inc(tp_free[x % 2], 1)
                if n == ONA_AT:
                    for m in range(MT):
                        wait_drained(act, G["na"], m)
                        square("na", 0, m, o2[:, 0, m, :])
                k = n - 1 - ONA_AT
                if 0 <= k < 2:
                    split(X[f"ona{k}"], (2 * k, 2 * k + 1), par[:, PAR["na_g"]:PAR["na_g"] + 4], xt_hi)
                if 8 <= n < 12:
                    feed(S["out2"] + n - 8, 1)
            for m in range(MT):
                wait_drained(act, G["mla"], m)
                square("mla", 0, m, o2[:, 1, m, :])
            for k in range(2):
                split(X["omla"] + k, (4 + 2 * k, 5 + 2 * k), par[:, PAR["mla_g"] - 4:PAR["mla_g"] + 4], xt_hi)
            feed(S["out2"] + 4, 4)
            f3_g = par[:, PAR["f3_g"]:PAR["f3_g"] + KT]
            for m in range(MT):
                for c in range(2):
                    wait_drained(act, G["bot"] + c, m)
                    square("mix", c, m, f[:, m, c * W:(c + 1) * W])
                if m == 0:
                    feed(S["f3i"], 2)
                else:
                    squares_new("h4", 0)
                split_new("h4", m, f3_g)
                if m == 0:
                    feed(S["f3i"] + 2, 2)
            squares_new("h4", 1)

            ffn(S["f3i"], S["f3o"], G["f3i"], X["f3"], None, f3_g, NTH["h4"], lambda: None, lambda: None, rs[:, ST["h4"]],
                lambda: None)
            feed(S["f3o"] + 6, 9)
            post_squares("f3", 0, G["f3o"], S["f3o"] + 10)
            feed(S["f3o"] + 15, 7)
            post_squares("f3", 1, G["f3o"] + 1, S["f3o"] + 21)

        @block.tensor
        def _(pe):
            def slab_products(s, j_tiles, lhs, width, banks, first, last, ms=range(MT), done=None):
                hi, lo = lhs
                for m in ms:
                    for n, (j, k) in enumerate(j_tiles):
                        rows = slice(m * P, (m + 1) * P)
                        wh = w_hi[:, s % RING, j * width:(j + 1) * width]
                        wl = w_lo[:, s % RING, j * width:(j + 1) * width]
                        o = banks[m][:, 0:width]
                        end = last and n == len(j_tiles) - 1
                        pe.matmul(o, hi[:, k, rows], wh, start=first and n == 0, stop=False)
                        pe.matmul(o, lo[:, k, rows], wh, start=False, stop=False)
                        mm = pe.matmul(o, hi[:, k, rows], wl, start=False, stop=end)
                    if m == 0 and last:
                        mm.then_inc(done[0], 1)
                    if m == 1:
                        mm.then_inc(done[1], 1)

            def group(s, g, lhs, slabs, i=0, slab_turns=0, acc_turns=0, width=W, k0=0, ready=None, after={},
                      by_tile=0):
                banks = acc[g % 2 * 2:g % 2 * 2 + 2]
                done = [(acc0_full[g % 2], slab_used[(s + q) % RING]) for q in range(slabs)]
                for q in range(slabs - by_tile):
                    wait(pe, lo_done[(s + q) % RING], (s + q) // RING + 1, i, slab_turns)
                    if ready is not None:
                        ready(q)
                    if q == 0:
                        wait_bank(pe, g, 1, i, acc_turns)
                    slab_products(s + q, [(0, k0 + 2 * q), (1, k0 + 2 * q + 1)], lhs, width, banks,
                                  q == 0, q == slabs - 1, done=done[q])
                    if q in after:
                        after[q]()
                for m in range(MT):
                    for q in range(slabs - by_tile, slabs):
                        if m == 0:
                            wait(pe, lo_done[(s + q) % RING], (s + q) // RING + 1)
                        if ready is not None:
                            ready(q, m)
                        if q == 0:
                            wait_bank(pe, g, m)
                        slab_products(s + q, [(0, k0 + 2 * q), (1, k0 + 2 * q + 1)], lhs, width, banks,
                                      q == 0, q == slabs - 1, ms=(m,), done=done[q])
                        if (m, q) in after:
                            after[m, q]()

            def turn(x, pieces, i=0, turns=0):
                wait(pe, tp_free[x % 2], x // 2, i, turns)
                for col, src in pieces:
                    rows, cols = src.shape[0], int(np.prod(src.shape[1:]))
                    t = pe.transpose(tp[x % 2][0:cols, col:col + rows], src, ident[0:rows, 0:rows])
                t.then_inc(tp_full[x % 2], 1)

            def turn_tiles(x, src, tiles, i=0, turns=0):
                turn(x, [(n * T + m * P, src[:, m, k * P:(k + 1) * P]) for n, k in enumerate(tiles) for m in range(MT)],
                     i, turns)

            def pairs_ready(x):
                return lambda q: wait_tp_free(pe, x + q)

            XT, YT, HID = (xt_hi, xt_lo), (yt_hi, yt_lo), (hid_hi, hid_lo)

            pe.wait_ge(ident_landed, 16)
            for m in range(MT):
                pe.wait_ge(x_landed[m], 16)
            for n in range(4):
                turn_tiles(X["x"] + n, h, (2 * n, 2 * n + 1))
            ready = pairs_ready(X["x"])
            with pe.Fori(0, 2) as i:
                for g in range(2):
                    group(4 * g, g, XT, 4, i, 2, 1, ready=ready)

            def turn_xr_gr(tile_pairs):
                for g in range(4):
                    wait_both_drained(pe, g)
                for n in tile_pairs:
                    turn_tiles(X["xg"] + 2 * n, u[:, 0], (2 * n, 2 * n + 1))
                    turn_tiles(X["xg"] + 2 * n + 1, u[:, 1], (2 * n, 2 * n + 1))

            def turn_parameters():
                pe.wait_ge(par_landed, 16 * 15)
                turn(X["par"], [(0, par_rows[0:PAR["end"], :])])
                turn_xr_gr((0, 1))

            group(16, 4, XT, 4, after={0: turn_parameters, 1: lambda: turn_xr_gr((2, 3))})
            group(20, 5, XT, 4)

            def gates():
                pe.wait_ge(bd_landed, 64)
                for n in range(KT):
                    x = X["gate"] + n
                    pe.wait_ge(conv_done, n + 1)
                    wait(pe, tp_free[x % 2], x // 2)
                    pe.matmul(tp[x % 2][:, 0:T], blockdiag[:, n, :], xcT[:, n, :], start=True, stop=True)
                    pe.matmul(tp[x % 2][:, T:2 * T], blockdiag[:, KT + n, :], xcT[:, n, :], start=True,
                              stop=True).then_inc(tp_full[x % 2], 1)

            def turn_q_k(n):
                for sec in (2, 3):
                    wait_both_drained(pe, 2 * sec + n // 2)
                    turn_tiles(X["qk"] + 2 * n + sec - 2, u[:, sec], (2 * n, 2 * n + 1))

            group(24, 6, XT, 4, after={2: gates})
            group(28, 7, XT, 4)
            group(32, 8, XT, 4, after={1: lambda: turn_q_k(0), 2: lambda: turn_q_k(1)})
            group(36, 9, XT, 4, after={0: lambda: turn_q_k(2), 1: lambda: turn_q_k(3)})
            wait_tp_free(pe, X["qk"] + 6)
            wait_tp_free(pe, X["qk"] + 7)

            def scores1(g, r, i):
                wait(pe, staged, 2 * g + 2, i, 4)
                for hh in range(2):
                    tile = i * 4 + (2 * g + r + KT)
                    for m in range(MT):
                        n = P * (m + 1)
                        mm = pe.matmul(sc[hh][:, P * m:P * m + n], q_stage[:, 2 * r + hh, m * P:(m + 1) * P],
                                       qkT[:, bass.ds(tile, 1), 0:n].rearrange("p a n -> p (a n)"),
                                       start=True, stop=True)
                    mm.then_inc(scores_done, 1)

            def turn_probs1(g, r, i):
                for hh in range(2):
                    wait(pe, probs_done, 4 * g + 2 * r + hh + 1, i, 8)
                    wait(pe, o_drained, 4 * g + 2 * r + hh + 1, i, 8)
                    turn(X["p1"] + 4 * g + 2 * r + hh, [(P * n, sb1[:, hh, P * n:P * (n + 1)]) for n in range(3)], i, 4)

            def values1(g, r, i):
                for hh in range(2):
                    x = X["p1"] + 4 * g + 2 * r + hh
                    wait_tp_free(pe, x, i, 4)
                    o = tp[x % 2][:, 384:512]
                    head = i * 8 + (4 * g + 2 * r + hh)
                    v = [u[:, 4, m, bass.ds(head * HD, HD)] for m in range(MT)]
                    pe.matmul(o[:, 0:HD], pt1[:, hh, 0:P], v[0], start=True, stop=True)
                    pe.matmul(o[:, HD:2 * HD], pt1[:, hh, P:2 * P], v[0], start=True, stop=False)
                    pe.matmul(o[:, HD:2 * HD], pt1[:, hh, 2 * P:3 * P], v[1], start=False,
                              stop=True).then_inc(pv_done, 1)

            with pe.Fori(0, 2) as i:
                for g in range(2):
                    scores1(g, 0, i)

                    def second_round(g=g):
                        turn_probs1(g, 0, i)
                        scores1(g, 1, i)

                    group(40 + 4 * g, 10 + g, XT, 4, i, 2, 1,
                          after={1: second_round, 2: lambda g=g: values1(g, 0, i)})
                    turn_probs1(g, 1, i)
                    values1(g, 1, i)

            def turn_att(uses):
                wait(pe, o_drained, 18)
                for n in uses:
                    turn_tiles(X["at"] + n, att, (2 * n, 2 * n + 1))

            pe.wait_ge(yt_ready, 1)
            group(S["rnn"], G["rnn"], YT, 4)
            group(S["rnn"] + 4, G["rnn"] + 1, YT, 4, after={0: lambda: turn_att((0, 1)), 1: lambda: turn_att((2, 3))})

            def turn_merged(half):
                wait(pe, m_ready, 2 * half + 2)
                for n in (2 * half, 2 * half + 1):
                    turn_tiles(X["mt"] + n, merged, (2 * n, 2 * n + 1))

            ready = pairs_ready(X["at"])
            group(S["attn"], G["attn"], XT, 4, ready=ready)
            group(S["attn"] + 4, G["attn"] + 1, XT, 4, after={2: lambda: turn_merged(0)})

            def turn_h(x, g_o, half):
                wait_both_drained(pe, g_o + half)
                for n in (2 * half, 2 * half + 1):
                    turn_tiles(x + n, h, (2 * n, 2 * n + 1))

            ready = pairs_ready(X["mt"])
            group(S["o"], G["o"], YT, 4, ready=ready, after={0: lambda: turn_merged(1)})
            group(S["o"] + 4, G["o"] + 1, YT, 4, after={2: lambda: turn_h(X["h1"], G["o"], 0)})

            def ffn(s_in, s_out, g_in, g_out, x_hid, first_group, after, by_tile=0):
                def turn_hidden(g, i=0):
                    wait_both_drained(pe, g_in + g, i, TURN // 2)
                    turn(x_hid + g, [(n * T + m * P, hid[:, g % 2, m, n * P:(n + 1) * P])
                                     for n in range(2) for m in range(MT)], i, TURN // 2)

                def one_group(g, i=0):
                    group(s_in + 4 * g, g_in + g, XT, 4, i, TURN, TURN // 2, after={1: lambda: turn_hidden(g - 1, i)})

                first_group()
                for g in range(1, HEAD):
                    one_group(g)
                with pe.Fori(0, (FG - HEAD) // TURN) as i:
                    for g in range(HEAD, HEAD + TURN):
                        one_group(g, i)

                def ready(q):
                    if q >= FG - 2:
                        wait_tp_free(pe, x_hid + q)

                group(s_out, g_out, HID, 11, ready=ready, after={1: lambda: turn_hidden(FG - 1)})
                group(s_out + 11, g_out + 1, HID, 11, after=after, by_tile=by_tile)

            ffn(S["f1i"], S["f1o"], G["f1i"], G["f1o"], X["f1"],
                lambda: group(S["f1i"], G["f1i"], XT, 4, ready=pairs_ready(X["h1"]),
                              after={0: lambda: turn_h(X["h1"], G["o"], 1)}),
                {8: lambda: turn_h(X["h2"], G["f1o"], 0)})

            def turn_new_h(x, m, half, count):
                wait(pe, h_new, count + 2 * m + half + 1)
                turn(x + 2 * m + half, [(n * P, h[:, m, (4 * half + n) * P:(4 * half + n + 1) * P]) for n in range(4)])

            def new_tile(x, count, m):
                for half in range(2):
                    turn_new_h(x, m, half, count)

            def new_ready(x):
                return lambda q, m: wait_tp_free(pe, x + 2 * m + q // 2)

            ffn(S["f2i"], S["f2o"], G["f2i"], G["f2o"], X["f2"],
                lambda: group(S["f2i"], G["f2i"], XT, 4, ready=pairs_ready(X["h2"]),
                              after={0: lambda: turn_h(X["h2"], G["f1o"], 1)}),
                {(1, 9): lambda: new_tile(X["h3"], 0, 0)}, by_tile=4)

            def turn_latents():
                wait_both_drained(pe, G["in2"])
                turn_tiles(X["c"], u2[:, :, 1536:1952], (0, 1))
                turn_tiles(X["c"] + 1, u2[:, :, 1536:1952], (2,))

            group(S["in2"], G["in2"], XT, 4, width=416, ready=new_ready(X["h3"]),
                  after={(0, 2): lambda: new_tile(X["h3"], 0, 1)}, by_tile=4)
            def turn_nqk(n):
                for m in range(MT):
                    for c in range(2):
                        wait_drained(pe, G["in2"] + 1 + c, m)
                turn_tiles(X["nqk"] + 2 * n, u2, (2 * n, 2 * n + 1))
                turn_tiles(X["nqk"] + 2 * n + 1, u2, (4 + 2 * n, 5 + 2 * n))

            between = ({1: turn_latents}, {}, {1: lambda: turn_nqk(0), 2: lambda: turn_nqk(1)})
            for c in range(3):
                group(S["in2"] + 4 * c + 4, G["in2"] + c + 1, XT, 4, after=between[c])
            def scores(n):
                if n < 8:
                    rows, t = slice(64 * (n % 2), 64 * (n % 2) + 64), n // 2
                    q, k = nqk[rows, t, :], nqk[rows, 4 + t, :]
                    wait_tp_free(pe, X["nqk"] + n // 4 * 2)
                    wait_tp_free(pe, X["nqk"] + n // 4 * 2 + 1)
                else:
                    q, k = mqT[:, n - 8, :], mkT[:, n - 8, :]
                    for which in range(2):
                        wait_tp_free(pe, X[f"mqk{(n - 8) // 2}"] + which)
                for m in range(MT):
                    mm = pe.matmul(sc[n % 2][:, m * T:(m + 1) * T], q[:, m * P:(m + 1) * P], k, start=True, stop=True)
                mm.then_inc(scores2, 1)

            scores(0)
            scores(1)
            C = (c_hi, c_lo)
            wait_tp_free(pe, X["c"])
            group(S["uq"], G["uq"], C, 1)
            group(S["uq"] + 1, G["uq"] + 1, C, 1, width=256)
            wait_tp_free(pe, X["c"] + 1)
            s = S["ukv"]
            wait(pe, lo_done[s % RING], s // RING + 1)
            for j in range(2):
                g = G["ukv"] + j
                for m in range(MT):
                    wait_bank(pe, g, m)
                slab_products(s, [(j, 2)], C, W, acc[g % 2 * 2:g % 2 * 2 + 2], True, True,
                              done=(acc0_full[g % 2], kv_half if j == 0 else slab_used[s % RING]))
            def turn_probs(n):
                pe.wait_ge(probs2, n + 1)
                turn(X[f"probs{n}"], [(c * P, sb2[:, n % 2, c * P:(c + 1) * P]) for c in range(4)])

            def turn_latent_heads(k, which, src):
                if 0 <= k < 4:
                    pe.wait_ge(rope_q if which == 0 else rope_k, 2)
                    for c in range(2):
                        wait_both_drained(pe, (G["uq"], G["ukv"])[which] + c)
                    turn(X[f"mqk{k}"] + which, [(c * T + m * P, src[:, m, 2 * k + c, :])
                                                for c in range(2) for m in range(MT)])

            def values(n):
                g = G["na"] if n < 8 else G["mla"]
                if n % 8 == 0:
                    for m in range(MT):
                        wait_bank(pe, g, m)
                wait_tp_free(pe, X[f"probs{n}"])
                hd = n % 8
                for m in range(MT):
                    for kt in range(2):
                        v = u2[:, kt, 1024 + HD * hd:1024 + HD * hd + HD] if n < 8 else mv[:, kt, hd, :]
                        mm = pe.matmul(acc[g % 2 * 2 + m][:, HD * hd:HD * hd + HD],
                                       pt2[:, n % 2, (2 * m + kt) * P:(2 * m + kt + 1) * P], v,
                                       start=kt == 0, stop=kt == 1)
                    if m == 0 and hd == 7:
                        mm.then_inc(acc0_full[g % 2], 1)
                mm.then_inc(pv2, 1)

            wait_both_drained(pe, G["in2"] + 3)
            for n in range(16):
                turn_probs(n)
                if n + 2 < 16:
                    scores(n + 2)
                turn_latent_heads(n - MQK_AT, 0, mq)
                if n >= 1:
                    values(n - 1)
                turn_latent_heads(n - MQK_AT, 1, mk)
                k = n - ONA_AT
                if 0 <= k < 2:
                    wait_both_drained(pe, G["na"])
                    turn_tiles(X[f"ona{k}"], o2[:, 0], (2 * k, 2 * k + 1))
            values(15)

            def turn_omla():
                wait_both_drained(pe, G["mla"])
                for k in range(2):
                    turn_tiles(X["omla"] + k, o2[:, 1], (2 * k, 2 * k + 1))

            group(S["out2"], G["top"], XT, 2, ready=lambda q: wait_tp_free(pe, X[f"ona{q}"]), after={0: turn_omla})
            group(S["out2"] + 2, G["top"] + 1, XT, 2)
            ready = pairs_ready(X["omla"])
            for m in range(MT):
                for c in range(2):
                    g = G["bot"] + c
                    wait_bank(pe, g, m)
                    for q in range(2):
                        s = S["out2"] + 4 + 2 * c + q
                        wait(pe, lo_done[s % RING], s // RING + 1)
                        ready(q)
                        slab_products(s, [(0, 4 + 2 * q), (1, 5 + 2 * q)], XT, W, acc[g % 2 * 2:g % 2 * 2 + 2],
                                      q == 0, q == 1, ms=(m,), done=(acc0_full[g % 2], slab_used[s % RING]))
                        if (m, c, q) == (1, 1, 0):
                            new_tile(X["h4"], 4, 0)
            ffn(S["f3i"], S["f3o"], G["f3i"], G["f3o"], X["f3"],
                lambda: group(S["f3i"], G["f3i"], XT, 4, ready=new_ready(X["h4"]),
                              after={(0, 2): lambda: new_tile(X["h4"], 4, 1)}, by_tile=4), {}, by_tile=4)

        @block.vector
        def _(dve):
            steps = [0]

            def step(ins):
                steps[0] += 1
                ins.then_inc(dve_step, 1)
                dve.wait_ge(dve_step, steps[0])

            def feed(s, n=1, i=0, turns=0):
                for q in range(s, min(s + n, S["end"])):
                    if q % 2 == 0:
                        b = q % RING
                        wait(dve, hi_done[b], q // RING + 1, i, turns)
                        dve.tensor_tensor(w_lo[:, b, :], w_raw[:, b, :], w_hi[:, b, :].bitcast(F32),
                                          ALU.subtract).then_inc(lo_done[b], 1)

            def split(x, tiles, gain, hi, lo, index, scale=1.0, i=0, turns=0, hi_turns=0):
                if gain is None:
                    wait(dve, hi_written, index + 1, i, hi_turns)
                    dve.scalar_tensor_tensor(lo, two(tp[x % 2]), scale, hi.bitcast(F32), ALU.mult,
                                             ALU.subtract).then_inc(tp_free[x % 2], 1)
                else:
                    wait(dve, hi_written, index + len(tiles), i, hi_turns)
                    for n, k in enumerate(tiles):
                        ins = dve.scalar_tensor_tensor(lo[:, k, :], tp[x % 2][:, n * T:(n + 1) * T], gain[:, k:k + 1],
                                                       hi[:, k, :].bitcast(F32), ALU.mult, ALU.subtract)
                    ins.then_inc(tp_free[x % 2], 1)

            def mean_square(name, m=None):
                _, n, factor = STATS[ST[name]]
                t, ts = ST[name], slice(0, MT) if m is None else slice(m, m + 1)
                wait(dve, ssq_done, max(SQ[k] for k in SQUARES if k[0] == name and m in (None, k[2])) + 1)
                if name in TWO_HALVES:
                    step(dve.tensor_tensor(ssq[:, t, 0, ts], ssq[:, t, 0, ts], ssq[:, t, 1, ts], ALU.add))
                dve.tensor_scalar(ms[:, t, ts], ssq[:, t, 0, ts], factor / n, factor * EPS, ALU.mult,
                                  ALU.add).then_inc(ms_done, 1)

            dve.memset(minus_half[:], -0.5).then_inc(set_up, 1)
            dve.memset(carrier[:], 0.0).then_inc(o_drained, 2)
            for b in range(4):
                dve.memset(free_marks[:, b:b + 1], 0.0).then_inc(acc_drained[b], 1)
            dve.memset(free_marks[:, 4:5], 0.0).then_inc(ttr_done, 1)
            dve.memset(xrT[:, :, 0:3], 0.0).then_inc(set_up, 1)
            dve.memset(bias1[0:CHUNK, :, :, 0:CHUNK], MASKED).then_inc(set_up, 1)
            for n in range(4):
                split(X["x"] + n, (2 * n, 2 * n + 1), gain_x, xt_hi, xt_lo, HI["x"] + 2 * n)
                if n == 1:
                    feed(0, 2)
            feed(2, 2)
            mean_square("x")

            def pcol(name, n=KT, off=0):
                return par[:, PAR[name] + off:PAR[name] + off + n]

            def drain_scaled(g, dst, i=0, slab_turns=0, acc_turns=0, last_slab=None, scale=None):
                for m in range(MT):
                    wait_acc(dve, g, m, last_slab, i, slab_turns, acc_turns)
                    dve.tensor_scalar(dst(m), acc[g % 2 * 2 + m][:, :], scale[:, m:m + 1], None,
                                      ALU.mult).then_inc(acc_drained[g % 2 * 2 + m], 1)

            dve.wait_ge(rs_done, NTH["x"])
            rx = rs[:, ST["x"]]
            with dve.Fori(0, 2) as i:
                for g in range(2):
                    feed(4 + 4 * g, 4, i, 2)
                    drain_scaled(g, lambda m: u[:, bass.ds(i, 1), m, g * W:(g + 1) * W].rearrange("p a n -> p (a n)"),
                                 i, 2, 1, 4 * g + 3, rx)
            wait_tp_full(dve, X["par"])
            dve.tensor_copy(par[:, 0:PAR["end"]], tp[X["par"] % 2][:, 0:PAR["end"]]).then_inc(tp_free[X["par"] % 2], 1)
            wait_tp_free(dve, X["par"])

            step(dve.scalar_tensor_tensor(small[:, 0, :], pcol("lam"), -1.0, pcol("lam"), ALU.mult, ALU.max))
            dve.tensor_scalar(small[:, 10, :], pcol("lam"), -1.0, 0.0, ALU.mult, ALU.max).then_inc(abs_lam, 1)
            dve.tensor_scalar(small[:, 8, :], pcol("b_r"), 0.5, None, ALU.mult)
            dve.tensor_scalar(small[:, 9, :], pcol("b_i"), 0.5, None, ALU.mult)
            dve.tensor_tensor(small[:, 11, :], pcol("fin_g"), pcol("f2_g"), ALU.mult)
            for n in range(4):
                x = X["xg"] + 2 * n + 1
                wait_tp_full(dve, x)
                dve.tensor_copy(grT[:, 2 * n:2 * n + 2, :], two(tp[x % 2])).then_inc(tp_free[x % 2], 1)
            wait_tp_free(dve, X["xg"] + 6)
            wait_tp_free(dve, X["xg"] + 7)

            def conv_tiles(tiles):
                base_step = steps[0]
                for j in range(4):
                    for at, n in enumerate(tiles):
                        tap = xrT[:, n, j:j + T]
                        w = par[:, PAR["conv_w"] + 8 * j + n:PAR["conv_w"] + 8 * j + n + 1]
                        if j == 0:
                            ins = dve.tensor_scalar(xcT[:, n, :], tap, w, pcol("conv_b", 1, n), ALU.mult, ALU.add)
                        else:
                            dve.wait_ge(dve_step, base_step + (j - 1) * len(tiles) + at + 1)
                            ins = dve.scalar_tensor_tensor(xcT[:, n, :], tap, w, xcT[:, n, :], ALU.mult, ALU.add)
                        if j == 3:
                            ins.then_inc(conv_done, 1)
                        else:
                            steps[0] += 1
                            ins.then_inc(dve_step, 1)

            def drain_section(g):
                drain_scaled(g, lambda m: u[:, g // 2, m, g % 2 * W:(g % 2 + 1) * W], last_slab=4 * g + 3, scale=rx)

            feed(20, 2)
            conv_tiles((0, 1))
            feed(22, 2)
            conv_tiles((2, 3))
            drain_section(4)
            feed(24, 2)
            dve.wait_ge(exp_lam, 1)
            step(dve.tensor_scalar(small[:, 2, :], small[:, 1, :], 2.0, None, ALU.add))
            step(dve.reciprocal(small[:, 3, :], small[:, 2, :]))
            step(dve.tensor_tensor(small[:, 2, :], small[:, 1, :], small[:, 3, :], ALU.mult))
            step(dve.tensor_tensor(small[:, 4, :], small[:, 2, :], small[:, 2, :], ALU.mult))
            step(dve.tensor_scalar(small[:, 5, :], small[:, 4, :], 1.0 / 17, None, ALU.mult))
            for n in (15, 13, 11, 9, 7, 5, 3):
                step(dve.scalar_tensor_tensor(small[:, 5, :], small[:, 5, :], 1.0 / n, small[:, 4, :], ALU.add, ALU.mult))
            step(dve.scalar_tensor_tensor(small[:, 5, :], small[:, 5, :], 1.0, small[:, 2, :], ALU.add, ALU.mult))
            step(dve.scalar_tensor_tensor(small[:, 5, :], small[:, 5, :], 2.0, small[:, 10, :], ALU.mult, ALU.add))
            step(dve.tensor_scalar(small[:, 6, :], small[:, 5, :], 4.0, None, ALU.mult))
            dve.tensor_scalar(small[:, 7, :], small[:, 5, :], -4.0, None, ALU.mult).then_inc(consts_ready, 1)

            conv_tiles((4, 5))
            feed(26, 2)
            conv_tiles((6, 7))
            drain_section(5)
            dve.wait_ge(table_landed, 16)
            dve.tensor_copy(ext_sb[:, 256:384], ext_sb[:, 255:256].to_broadcast([HEADS, P])).then_inc(ext_done, 1)
            feed(28, 4)
            drain_section(6)
            feed(32, 2)
            aT = xrT[:, :, 0:T]
            dve.wait_ge(decay_done, 16)
            dve.tensor_tensor(sq, aT, aT, ALU.mult).then_inc(mult2_done, 1)
            dve.wait_ge(mult2_done, 1)
            dve.scalar_tensor_tensor(sq, sq, 1.0, trT, ALU.add, ALU.mult).then_inc(mult2_done, 1)
            feed(34, 2)
            wait_tp_free(dve, X["gate"] + 6)
            wait_tp_free(dve, X["gate"] + 7)
            step(dve.scalar_tensor_tensor(ti[:], ti[:], 1.0, xcT, ALU.add, ALU.mult))
            drain_section(7)

            def copy_k(n):
                x = X["qk"] + 2 * n + 1
                wait_tp_full(dve, x)
                dve.tensor_copy(qkT[:, KT + 2 * n:KT + 2 * n + 2, :], two(tp[x % 2])).then_inc(tp_free[x % 2], 1)

            def recur(tiles):
                for n in tiles:
                    dve.tensor_tensor_scan(xcT[:, n, :], xrT[:, n, 0:T], ti[:, n, :], 0.0, ALU.mult,
                                           ALU.add).then_inc(rec_done, 1)

            feed(36, 2)
            copy_k(0)
            dve.wait_ge(mult_done, 1)
            dve.scalar_tensor_tensor(ti[:], ti[:], 0.5, sq, ALU.mult, ALU.mult).then_inc(bx_done, 1)
            dve.wait_ge(bx_done, 1)
            recur(range(0, 4))
            feed(38, 2)
            copy_k(1)
            recur(range(4, 8))
            drain_section(8)
            feed(40, 2)
            copy_k(2)
            copy_k(3)
            dve.wait_ge(gelu_tanh, 1)
            step(dve.scalar_tensor_tensor(gel, gel, 1.0, grT[:], ALU.add, ALU.mult))
            dve.wait_ge(rec_done, KT)
            dve.scalar_tensor_tensor(trT, gel, 0.5, xcT, ALU.mult, ALU.mult).then_inc(rg_out, 1)
            feed(42, 2)
            drain_section(9)
            dve.wait_ge(rg_out, 1)
            dve.wait_ge(hi_written, HI["rg"] + 1)
            dve.tensor_tensor(yt_lo[:], trT, yt_hi[:].bitcast(F32), ALU.subtract).then_inc(yt_ready, 1)

            dve.wait_ge(merge_landed, 16)
            dve.wait_ge(set_up, 3)

            def maxima1(g, r, i):
                if r == 0:
                    wait(dve, bias_landed[g], 32, i, 32)
                for hh in range(2):
                    wait(dve, scores_done, 4 * g + 2 * r + hh + 1, i, 8)
                    dve.memset(carrier[:, 4 * g + 2 * r + hh:4 * g + 2 * r + hh + 1], 0.0)
                    for m in range(MT):
                        n = P * (m + 1)
                        b = bias1[:, g, 2 * r + hh, n - 1::-1]
                        dve.tensor_tensor_reduce(sb1[:, hh, P * m:P * m + n], sc[hh][:, P * m:P * m + n], b, 1.0, -3e38,
                                                 ALU.add, ALU.max, mx1[:, r, 2 * hh + m:2 * hh + m + 1]).then_inc(ttr_done, 1)
                wait(dve, ttr_done, 8 * g + 4 * r + 5, i, 16)
                dve.tensor_scalar(nm1[:, r, :], mx1[:, r, :], -1.0, None, ALU.mult).then_inc(negmax_done, 1)

            def drain_values1(g, r, i):
                wait(dve, probs_done, 4 * g + 2 * r + 2, i, 8)
                dve.reciprocal(inv1[:, r, :], sum1[:, r, :]).then_inc(inv_done, 1)
                wait(dve, inv_done, 2 * g + r + 1, i, 4)
                for hh in range(2):
                    head = i * 8 + (4 * g + 2 * r + hh)
                    wait(dve, pv_done, 4 * g + 2 * r + hh + 1, i, 8)
                    dve.tensor_tensor(att[:, :, bass.ds(head * HD, HD)],
                                      tp[(X["p1"] + hh) % 2][:, 384:512].rearrange("p (m d) -> p m d", m=MT),
                                      inv1[:, r, 2 * hh:2 * hh + 2].unsqueeze(2).to_broadcast([P, MT, HD]),
                                      ALU.mult).then_inc(o_drained, 1)

            with dve.Fori(0, 2) as i:
                for g in range(2):
                    s = 44 + 4 * g
                    maxima1(g, 0, i)
                    feed(s, 2, i, 2)
                    maxima1(g, 1, i)
                    drain_values1(g, 0, i)
                    feed(s + 2, 2, i, 2)
                    for m in range(MT):
                        wait_acc(dve, G["in"] + 10 + g, m, 43 + 4 * g, i, 2, 1)
                        dst = u[:, bass.ds(i + 5, 1), m, g * W:(g + 1) * W].rearrange("p a n -> p (a n)")
                        b = b_merge[:, bass.ds(i * D + g * W, W)]
                        dve.scalar_tensor_tensor(dst, acc[g % 2 * 2 + m][:, :], rx[:, m:m + 1], b, ALU.mult,
                                                 ALU.add).then_inc(acc_drained[g % 2 * 2 + m], 1)
                    drain_values1(g, 1, i)

            feed(S["rnn"] + 4, 4)
            dve.wait_ge(gate_tanh, 8)
            for c in range(2):
                cols = slice(c * W, (c + 1) * W)
                for m in range(MT):
                    wait_acc(dve, G["rnn"] + c, m, S["rnn"] + 4 * c + 3)
                    dve.scalar_tensor_tensor(merged[:, m, cols], u[:, 6, m, cols], 1.0, acc[(G["rnn"] + c) % 2 * 2 + m][:, :],
                                             ALU.add, ALU.mult).then_inc(acc_drained[(G["rnn"] + c) % 2 * 2 + m], 1)
                if c == 0:
                    for n in range(4):
                        if n == 2:
                            feed(S["rnn"] + 8, 1)
                        t = slice(2 * n, 2 * n + 2)
                        split(X["at"] + n, None, None, xt_hi[:, t, :], xt_lo[:, t, :], HI["at"] + n)
                    feed(S["rnn"] + 9, 3)
            feed(S["rnn"] + 12, 4)
            for c in range(2):
                cols = slice(c * W, (c + 1) * W)
                for m in range(MT):
                    b = (G["attn"] + c) % 2 * 2 + m
                    wait_acc(dve, G["attn"] + c, m, S["attn"] + 4 * c + 3)
                    dve.scalar_tensor_tensor(u[:, 5, m, cols], u[:, 5, m, cols], 1.0, acc[b][:, :],
                                             ALU.add, ALU.mult).then_inc(acc_drained[b], 1)
                for m in range(MT):
                    wait_drained(dve, G["attn"] + c, m)
                    wait_drained(dve, G["rnn"] + c, m)
                    dve.tensor_tensor(merged[:, m, cols], merged[:, m, cols], u[:, 5, m, cols], ALU.add).then_inc(m_ready, 1)
                feed(S["attn"] + 8 + 4 * c, 3 if c == 0 else 1)
                for n in (2 * c, 2 * c + 1):
                    t = slice(2 * n, 2 * n + 2)
                    split(X["mt"] + n, None, None, yt_hi[:, t, :], yt_lo[:, t, :], HI["mt"] + n, 0.5)
                feed(S["attn"] + 11 + 2 * c, 1)
            feed(S["o"] + 6, 2)

            def add_to_h(g, c, last_slab):
                for m in range(MT):
                    b = g % 2 * 2 + m
                    wait_acc(dve, g, m, last_slab)
                    dve.tensor_tensor(h[:, m, c * W:(c + 1) * W], h[:, m, c * W:(c + 1) * W], acc[b][:, :],
                                      ALU.add).then_inc(acc_drained[b], 1)

            def split_h(name, gain, uses):
                for n in uses:
                    split(X[name] + n, (2 * n, 2 * n + 1), gain, xt_hi, xt_lo, HI[name] + 2 * n)

            add_to_h(G["o"], 0, S["o"] + 3)
            feed(S["o"] + 8, 3)
            split_h("h1", pcol("ffn_g"), (0, 1))
            feed(S["o"] + 11, 1)
            add_to_h(G["o"] + 1, 1, S["o"] + 7)

            def ffn(n_ffn, s_in, s_out, g_in, x_name, h_name, gain, before, statistics, scale):
                before()
                feed(s_in + 4, 1)
                if h_name is not None:
                    split_h(h_name, gain, (2, 3))
                feed(s_in + 5, 1)
                statistics()
                feed(s_in + 6, 2)

                def hidden(g, i=0):
                    for m in range(MT):
                        wait(dve, tanh_done, 2 * FG * n_ffn + 2 * g + m + 1, i, 2 * TURN)
                        dve.scalar_tensor_tensor(u1[:, m, :], th[:, m, :], 1.0, acc[(g_in + g) % 2 * 2 + m][:, 0:256],
                                                 ALU.add, ALU.mult).then_inc(u1_done, 1)
                    for m in range(MT):
                        b = (g_in + g) % 2 * 2 + m
                        wait(dve, u1_done, 2 * FG * n_ffn + 2 * g + m + 1, i, 2 * TURN)
                        wait_acc(dve, g_in + g, m, s_in + 4 * g + 3, i, TURN, TURN // 2)
                        dve.scalar_tensor_tensor(hid[:, g % 2, m, :], u1[:, m, :], scale[:, m:m + 1], acc[b][:, 256:512],
                                                 ALU.mult, ALU.mult).then_inc(acc_drained[b], 1)

                hidden(0)

                def one_group(g, i=0):
                    tiles = bass.ds(i * (2 * TURN) + 2 * (g - 1), 2)
                    feed(s_in + 4 * g + 4, 2, i, TURN)
                    split(X[x_name] + g - 1, None, None, hid_hi[:, tiles, :], hid_lo[:, tiles, :],
                          HI[x_name] + g - 1, 1.0, i, TURN // 2, TURN)
                    feed(s_in + 4 * g + 6, 2, i, TURN)
                    hidden(g, i)

                for g in range(1, HEAD):
                    one_group(g)
                with dve.Fori(0, (FG - HEAD) // TURN) as i:
                    for g in range(HEAD, HEAD + TURN):
                        one_group(g, i)
                feed(s_out + 4, 2)
                split(X[x_name] + FG - 1, None, None, hid_hi[:, FT - 2:FT, :], hid_lo[:, FT - 2:FT, :],
                      HI[x_name] + FG - 1)

            def half_rstd_squared(name, slot):
                dve.wait_ge(rs_done, NTH[name])
                r = rs[:, ST[name]]
                dve.scalar_tensor_tensor(coef[:, slot, :], r, 2.0, r, ALU.mult, ALU.mult).then_inc(coef_done, 1)

            def statistics1():
                half_rstd_squared("h1", 0)
                dve.wait_ge(coef_done, 1)

            ffn(0, S["f1i"], S["f1o"], G["f1i"], "f1", "h1", pcol("ffn_g"), lambda: mean_square("h1"), statistics1, coef[:, 0])
            dve.wait_ge(late_landed, 16 * 5)
            step(dve.memset(ext2_sb[:], 0.0))
            dve.tensor_copy(ext2_sb[:, :, 48:79], rpb_sb[:, 4:11, ::-1]).then_inc(ext2_done, 1)
            feed(S["f1o"] + 6, 9)
            add_to_h(G["f1o"], 0, S["f1o"] + 10)
            feed(S["f1o"] + 15, 7)
            split_h("h2", small[:, 11, :], (0, 1))
            feed(S["f1o"] + 22, 4)
            add_to_h(G["f1o"] + 1, 1, S["f1o"] + 21)
            dve.wait_ge(rows_landed, 64)

            def statistics2():
                dve.wait_ge(rs_done, NTH["h2"])
                wait_tp_full(dve, X["h2"] + 2)
                wait_tp_full(dve, X["h2"] + 3)
                for m in range(MT):
                    dve.scalar_tensor_tensor(h[:, m, :], h[:, m, :], rs[:, ST["h2"], m:m + 1], row_gain[:, 0, :],
                                             ALU.mult, ALU.mult).then_inc(x2_ready, 1)
                mean_square("x2")
                dve.wait_ge(rs_done, NTH["x2"])
                dve.tensor_tensor(coef[:, 1, :], rs[:, ST["h2"]], rs[:, ST["x2"]], ALU.mult).then_inc(coef_done, 1)
                dve.wait_ge(coef_done, 2)
                dve.scalar_tensor_tensor(coef[:, 2, :], coef[:, 1, :], 2.0, coef[:, 1, :], ALU.mult,
                                         ALU.mult).then_inc(coef_done, 1)
                dve.wait_ge(coef_done, 3)

            ffn(1, S["f2i"], S["f2o"], G["f2i"], "f2", "h2", small[:, 11, :], lambda: mean_square("h2"), statistics2, coef[:, 2])

            def gained(name, g, c, row, last_slab, ms=range(MT)):
                for m in ms:
                    b = g % 2 * 2 + m
                    wait_acc(dve, g, m, last_slab)
                    dve.wait_ge(ssq_done, SQ[name, c, m] + 1)
                    dve.tensor_tensor(f[:, m, c * W:(c + 1) * W], acc[b][:, :], row_gain[:, row, c * W:(c + 1) * W],
                                      ALU.mult).then_inc(acc_drained[b], 1)

            def add_normed(name, m, done, gained_f):
                dve.wait_ge(rs_done, NTH[name] - 1 + m)
                for c in range(2):
                    v = h[:, m, c * W:(c + 1) * W]
                    dve.scalar_tensor_tensor(v, gained_f(m, c), rs[:, ST[name], m:m + 1], v, ALU.mult,
                                             ALU.add).then_inc(done, 1)

            def split_new(name, m, gain):
                for half in range(2):
                    x = X[name] + 2 * m + half
                    dve.wait_ge(hi_written, HI[name] + 4 * (2 * m + half) + 4)
                    for n in range(4):
                        k, t = 4 * half + n, slice(m * P, (m + 1) * P)
                        ins = dve.scalar_tensor_tensor(xt_lo[:, k, t], tp[x % 2][:, n * P:(n + 1) * P], gain[:, k:k + 1],
                                                       xt_hi[:, k, t].bitcast(F32), ALU.mult, ALU.subtract)
                    ins.then_inc(tp_free[x % 2], 1)

            dve.wait_ge(x2_ready, 2)
            feed(S["f2o"] + 6, 9)
            gained("f2", G["f2o"], 0, 1, S["f2o"] + 10)
            feed(S["f2o"] + 15, 7)
            mix2_g = pcol("mix2_g")
            for m in range(MT):
                mean_square("f2", m)
                gained("f2", G["f2o"] + 1, 1, 1, S["f2o"] + 21, (m,))
                feed(S["in2"] + 2 * m, 1)
                for g in (G["f2o"], G["f2o"] + 1):
                    wait_drained(dve, g, m)
                add_normed("f2", m, h_new, lambda m, c: f[:, m, c * W:(c + 1) * W])
                split_new("h3", m, mix2_g)

            mean_square("h3")
            feed(S["in2"] + 4, 2)
            feed(S["in2"] + 6, 2)
            dve.wait_ge(rs_done, NTH["h3"])

            def drain_in2(n, col, width):
                g = G["in2"] + n
                for m in range(MT):
                    b = g % 2 * 2 + m
                    wait_acc(dve, g, m, S["in2"] + 4 * n + 3)
                    dve.tensor_scalar(u2[:, m, col:col + width], acc[b][:, 0:width], rs[:, ST["h3"], m:m + 1], None,
                                      ALU.mult).then_inc(acc_drained[b], 1)

            drain_in2(0, 1536, 416)
            feed(S["in2"] + 8, 2)
            mean_square("q")
            mean_square("kv")
            split(X["c"], (0, 1), pcol("q_g", 2), c_hi, c_lo, HI["c"])
            split(X["c"] + 1, (2,), par[:, PAR["kv_g"] - 2:PAR["kv_g"] + 1], c_hi, c_lo, HI["c"] + 2)
            dve.wait_ge(late_landed, 16 * 5)
            for m in range(MT):
                wait_drained(dve, G["in2"], m)
            k1, k2 = u2[:, :, 1920:1936], u2[:, :, 1936:1952]
            dve.tensor_tensor(kr[:, 0], k1, cos[:], ALU.mult)
            dve.tensor_tensor(kr[:, 1], k2, sin[:], ALU.mult)
            dve.tensor_tensor(kr[:, 2], k2, cos[:], ALU.mult)
            step(dve.tensor_tensor(kr[:, 3], k1, sin[:], ALU.mult))

            def over_heads(v):
                return v.unsqueeze(2).to_broadcast([P, MT, 8, 16])

            dve.tensor_tensor(mk[:, :, :, 64:80], over_heads(kr[:, 0]), over_heads(kr[:, 1]), ALU.subtract).then_inc(rope_k, 1)
            dve.tensor_tensor(mk[:, :, :, 80:96], over_heads(kr[:, 2]), over_heads(kr[:, 3]), ALU.add).then_inc(rope_k, 1)
            feed(S["in2"] + 10, 2)
            for n in range(1, 4):
                if n == 3:
                    for t in range(2):
                        x = X["nqk"] + 2 * t + 1
                        wait_tp_full(dve, x)
                        dve.tensor_copy(nqk[:, 4 + 2 * t:6 + 2 * t, :], two(tp[x % 2])).then_inc(tp_free[x % 2], 1)
                        if t == 0:
                            feed(S["in2"] + 18, 1)
                drain_in2(n, W * (n - 1), W)
                if n < 3:
                    feed(S["in2"] + 8 + 4 * n, 4 if n == 1 else 2)
            dve.wait_ge(bias2_ready, 8)

            def maxima2(n):
                dve.wait_ge(scores2, n + 1)
                mx = mx2[:, n % 2, :]
                if n < 8:
                    if n >= 2:
                        wait_tp_full(dve, X[f"probs{n - 2}"])
                    for m in range(MT):
                        keys = bias2[:, n, 2 - 2 * m:6 - 2 * m, ::-1]
                        dve.tensor_tensor_reduce(sb2[:, n % 2, m * T:(m + 1) * T].rearrange("p (a b) -> p a b", a=4),
                                                 sc[n % 2][:, m * T:(m + 1) * T].rearrange("p (a b) -> p a b", a=4),
                                                 keys, 1.0, -3e38, ALU.add, ALU.max,
                                                 mx2[:, n % 2, m:m + 1]).then_inc(max2, 1)
                else:
                    dve.tensor_reduce(mx, two(sc[n % 2]), mybir.AxisListType.X, ALU.max).then_inc(max2, 1)
                dve.wait_ge(max2, 2 * n + 2 if n < 8 else 16 + n - 7)
                dve.tensor_scalar(nm2[:, n % 2, :], mx, -1.0 if n < 8 else -MLA_SCALE, None, ALU.mult).then_inc(negmax2, 1)

            maxima2(0)
            maxima2(1)
            dve.wait_ge(rs_done, NTH["kv"])
            rq, rkv = rs[:, ST["q"]], rs[:, ST["kv"]]
            mq_flat = mq[:].rearrange("p m a d -> p m (a d)")
            for c, width in ((0, W), (1, 256)):
                g = G["uq"] + c
                for m in range(MT):
                    b = g % 2 * 2 + m
                    wait_acc(dve, g, m, S["uq"] + c)
                    dve.tensor_scalar(mq_flat[:, m, c * W:c * W + width], acc[b][:, 0:width], rq[:, m:m + 1], None,
                                      ALU.mult).then_inc(acc_drained[b], 1)
            for c in range(2):
                g = G["ukv"] + c
                for m in range(MT):
                    b = g % 2 * 2 + m
                    if m == 0 or c == 1:
                        wait_acc(dve, g, m, S["ukv"])
                    else:
                        dve.wait_ge(kv_half, 1)
                    src = acc[b][:, :].rearrange("p (a d) -> p a d", d=128)
                    dve.tensor_scalar(mk[:, m, 4 * c:4 * c + 4, 0:64], src[:, :, 0:64], rkv[:, m:m + 1], None,
                                      ALU.mult)
                    dve.tensor_scalar(mv[:, m, 4 * c:4 * c + 4, :], src[:, :, 64:128], rkv[:, m:m + 1], None,
                                      ALU.mult).then_inc(acc_drained[b], 1)
            def drain_values2(which, g):
                dve.wait_ge(pv2, 8 * which + 8)
                dve.reciprocal(inv2[:, which], sum2[:, which]).then_inc(inv2_done, 1)
                dve.wait_ge(inv2_done, which + 1)
                for m in range(MT):
                    b = g % 2 * 2 + m
                    dve.tensor_tensor(o2[:, which, m, :].rearrange("p (a d) -> p a d", d=HD),
                                      acc[b][:, :].rearrange("p (a d) -> p a d", d=HD),
                                      inv2[:, which, m, :].unsqueeze(2).to_broadcast([P, 8, HD]),
                                      ALU.mult).then_inc(acc_drained[b], 1)

            for n in range(16):
                x = X[f"probs{n}"]
                wait_tp_full(dve, x)
                if n >= 2:
                    dve.wait_ge(pv2, n - 1)
                dve.tensor_copy(pt2[:, n % 2, :], tp[x % 2][:, :]).then_inc(tp_free[x % 2], 1)
                k = n - 1 - ONA_AT
                if 0 <= k < 2:
                    split(X[f"ona{k}"], (2 * k, 2 * k + 1), pcol("na_g", 4), xt_hi, xt_lo, HI["ona"] + 2 * k)
                if n + 2 < 16:
                    maxima2(n + 2)
                k = n - MQK_AT
                if 0 <= k < 4:
                    x = X[f"mqk{k}"] + 1
                    wait_tp_full(dve, x)
                    dve.tensor_copy(mkT[:, 2 * k:2 * k + 2, :], two(tp[x % 2], 96)).then_inc(tp_free[x % 2], 1)
                if 8 <= n < 12:
                    feed(S["out2"] + n - 8, 1)
                if n == 8:
                    drain_values2(0, G["na"])
                if n == ONA_AT + 2:
                    mean_square("na")
            drain_values2(1, G["mla"])
            for k in range(2):
                split(X["omla"] + k, (4 + 2 * k, 5 + 2 * k), par[:, PAR["mla_g"] - 4:PAR["mla_g"] + 4], xt_hi, xt_lo,
                      HI["omla"] + 2 * k)
            mean_square("mla")
            for m in range(MT):
                b = G["top"] % 2 * 2 + m
                dve.wait_ge(rs_done, NTH["na"])
                wait_acc(dve, G["top"], m, S["out2"] + 1)
                dve.tensor_scalar(f[:, m, 0:W], acc[b][:, :], rs[:, ST["na"], m:m + 1], None, ALU.mult).then_inc(acc_drained[b], 1)
            feed(S["out2"] + 4, 2)
            for m in range(MT):
                b = (G["top"] + 1) % 2 * 2 + m
                wait_acc(dve, G["top"] + 1, m, S["out2"] + 3)
                dve.tensor_scalar(f[:, m, W:D], acc[b][:, :], rs[:, ST["na"], m:m + 1], None, ALU.mult).then_inc(acc_drained[b], 1)
            feed(S["out2"] + 6, 2)
            dve.wait_ge(rs_done, NTH["mla"])
            f3_g = pcol("f3_g")
            for m in range(MT):
                for c in range(2):
                    b = (G["bot"] + c) % 2 * 2 + m
                    v = f[:, m, c * W:(c + 1) * W]
                    wait_drained(dve, G["top"] + c, m)
                    wait_acc(dve, G["bot"] + c, m, S["out2"] + 5 + 2 * c)
                    dve.scalar_tensor_tensor(v, acc[b][:, :], rs[:, ST["mla"], m:m + 1], v, ALU.mult,
                                             ALU.add).then_inc(acc_drained[b], 1)
                for c in range(2):
                    if c == 1:
                        mean_square("mix", m)
                    wait_drained(dve, G["bot"] + c, m)
                    ins = dve.tensor_tensor(o2[:, c, m, :], f[:, m, c * W:(c + 1) * W], row_gain[:, 2, c * W:(c + 1) * W],
                                            ALU.mult)
                if m == 1:
                    feed(S["f3i"] + 2, 2)
                step(ins)
                add_normed("mix", m, h_new, lambda m, c: o2[:, c, m, :])
                if m == 0:
                    feed(S["f3i"], 2)
                split_new("h4", m, f3_g)

            def statistics3():
                half_rstd_squared("h4", 3)
                dve.wait_ge(coef_done, 4)

            ffn(2, S["f3i"], S["f3o"], G["f3i"], "f3", None, f3_g, lambda: mean_square("h4"), statistics3, coef[:, 3])
            dve.wait_ge(h_new, 8)
            feed(S["f3o"] + 6, 9)
            gained("f3", G["f3o"], 0, 3, S["f3o"] + 10)
            feed(S["f3o"] + 15, 7)
            for m in range(MT):
                mean_square("f3", m)
                gained("f3", G["f3o"] + 1, 1, 3, S["f3o"] + 21, (m,))
                for g in (G["f3o"], G["f3o"] + 1):
                    wait_drained(dve, g, m)
                add_normed("f3", m, out_ready, lambda m, c: f[:, m, c * W:(c + 1) * W])

        @block.gpsimd
        def _(pool):
            def feed(s, n=1, i=0, turns=0):
                for q in range(s, min(s + n, S["end"])):
                    if q % 2 == 1:
                        b = q % RING
                        wait(pool, hi_done[b], q // RING + 1, i, turns)
                        pool.tensor_tensor(w_lo[:, b, :], w_raw[:, b, :], w_hi[:, b, :].bitcast(F32),
                                           ALU.subtract).then_inc(lo_done[b], 1)

            def rstd(name, m=None):
                t, ts = ST[name], slice(0, MT) if m is None else slice(m, m + 1)
                wait(pool, ms_done, NTH[name] - (1 if m == 0 else 0))
                pool.tensor_tensor(rs[:, t, ts], ms[:, t, ts], minus_half[:, ts], ALU.pow).then_inc(rs_done, 1)

            pool.memset(blockdiag[:], 0.0).then_inc(bd_zero, 1)
            pool.memset(q_stage[:], 0.0).then_inc(q_zero, 1)
            feed(0, 4)
            pool.wait_ge(set_up, 1)
            rstd("x")
            with pool.Fori(0, 2) as i:
                feed(4, 8, i, 2)
            for n in range(4):
                wait_tp_free(pool, X["xg"] + 2 * n + 1)
            feed(20, 2)
            pool.tensor_tensor(gel, grT[:], grT[:], ALU.mult).then_inc(gelu_arg, 1)
            feed(22, 2)
            pool.wait_ge(gelu_arg, 1)
            pool.tensor_scalar(gel, gel, 0.044715, 1.0, ALU.mult, ALU.add).then_inc(gelu_arg, 1)
            feed(24, 2)
            pool.wait_ge(gelu_arg, 2)
            pool.tensor_tensor(gel, gel, grT[:], ALU.mult).then_inc(gelu_arg, 1)
            feed(26, 14)

            def stage(tile, group, i=0):
                pool.tensor_copy(q_stage[0:HD, 0::2, :], qkT[0:HD, tile, :]).then_inc(staged, 1)
                wait(pool, staged, 2 * group + 1, i, 4)
                pool.tensor_copy(q_stage[HD:P, 1::2, :], qkT[HD:P, tile, :]).then_inc(staged, 1)
                wait(pool, staged, 2 * group + 2, i, 4)

            wait_tp_free(pool, X["qk"])
            pool.wait_ge(q_zero, 1)
            stage(slice(0, 2), 0)
            feed(40, 4)
            for n in range(1, 4):
                wait_tp_free(pool, X["qk"] + 2 * n)
            with pool.Fori(0, 2) as i:
                for g in range(2):
                    s = 44 + 4 * g
                    feed(s, 2, i, 2)
                    wait(pool, scores_done, 4 * g + 4, i, 8)
                    stage(bass.ds(i * 4 + (2 * g + 2), 2), g + 1, i)
                    feed(s + 2, 2, i, 2)
            feed(60, S["f1i"] + 4 - 60)
            rstd("h1")
            feed(S["f1i"] + 4, 2)

            def hidden(s_in, s_out, first, between=None):
                feed(first, s_in + 4 + 4 * HEAD - first)
                with pool.Fori(0, (FG - HEAD) // TURN) as i:
                    feed(s_in + 4 + 4 * HEAD, 4 * TURN, i, TURN)
                for n in range(9):
                    feed(s_out + 4 + 2 * n, 2)
                    if between is not None and n < 8:
                        between(n)

            hidden(S["f1i"], S["f1o"], S["f1i"] + 6)
            feed(S["f1o"] + 22, 4)
            rstd("h2")
            feed(S["f2i"] + 4, 2)
            rstd("x2")

            def mask_head(hd):
                pool.wait_ge(late_landed, 16 * 5)
                pool.wait_ge(bias2_landed, 16 * 16)
                pool.tensor_tensor(bias2[:, hd], bias2[:, hd], na_mask[:].unsqueeze(1).to_broadcast([P, 6, 64]),
                                   ALU.add).then_inc(bias2_ready, 1)

            hidden(S["f2i"], S["f2o"], S["f2i"] + 6, mask_head)
            for m in range(MT):
                rstd("f2", m)
                feed(S["in2"] + 2 * m, 2)
            rstd("h3")
            feed(S["in2"] + 4, 2)
            feed(S["in2"] + 6, 4)
            rstd("q")
            rstd("kv")
            feed(S["in2"] + 10, 9)
            for c in range(2):
                for m in range(MT):
                    wait_drained(pool, G["uq"] + c, m)
            q1, q2 = mq[:, :, :, 64:80], mq[:, :, :, 80:96]
            c4 = cos[:].unsqueeze(2).to_broadcast([P, MT, 8, 16])
            s4 = sin[:].unsqueeze(2).to_broadcast([P, MT, 8, 16])
            pool.tensor_tensor(rope[:, 0], q1, c4, ALU.mult).then_inc(pool_step, 1)
            pool.tensor_tensor(rope[:, 1], q2, s4, ALU.mult).then_inc(pool_step, 1)
            pool.tensor_tensor(rope[:, 2], q2, c4, ALU.mult).then_inc(pool_step, 1)
            pool.tensor_tensor(rope[:, 3], q1, s4, ALU.mult).then_inc(pool_step, 1)
            pool.wait_ge(pool_step, 4)
            pool.tensor_tensor(q1, rope[:, 0], rope[:, 1], ALU.subtract).then_inc(rope_q, 1)
            pool.tensor_tensor(q2, rope[:, 2], rope[:, 3], ALU.add).then_inc(rope_q, 1)
            feed(S["out2"], 4)
            rstd("na")
            feed(S["out2"] + 4, 2)
            rstd("mla")
            feed(S["out2"] + 6, 2)
            rstd("mix", 0)
            feed(S["f3i"], 4)
            rstd("mix", 1)
            rstd("h4")
            feed(S["f3i"] + 4, 2)
            hidden(S["f3i"], S["f3o"], S["f3i"] + 6)
            for m in range(MT):
                rstd("f3", m)


_INS = ["x", "norm_mix_g", "w_in", "b_merge", "rel_table", "w_attn_out", "conv_w", "conv_b", "w_rg_r", "b_rg_r",
        "w_rg_i", "b_rg_i", "rg_lambda", "w_rnn_out", "w_o", "norm_ffn_g", "w_ffn_in", "w_ffn_out", "final_norm_g",
        "ffn1_pre_g_2", "ffn1_w_gu_2", "ffn1_w_down_2", "ffn1_post_g_2", "mix_pre_g_2", "w_in_2", "na_rpb_2",
        "mla_q_norm_g_2", "mla_w_uq_2", "mla_kv_norm_g_2", "mla_w_ukv_2", "na_out_norm_g_2", "mla_out_norm_g_2",
        "w_out_2", "mix_post_g_2", "ffn2_pre_g_2", "ffn2_w_gu_2", "ffn2_w_down_2", "ffn2_post_g_2"]


def constants():
    f32 = np.float32
    t = np.arange(T)
    inv_freq = (1.0 / (f32(10000.0) ** (np.arange(8, dtype=f32) / f32(8)))).astype(f32)
    ang = np.concatenate([(t // 64).astype(f32)[:, None] * inv_freq, (t % 64).astype(f32)[:, None] * inv_freq], -1)
    qc, kc = np.arange(64)[:, None], 63 - np.arange(64)[None, :]
    first = np.clip(qc - 8, 0, 48)
    mask = np.where((kc >= first) & (kc < first + 16), f32(0), f32(MASKED)).astype(f32)
    return {"c_cos": np.cos(ang).astype(f32), "c_sin": np.sin(ang).astype(f32), "c_mask": mask,
            "c_ident": np.eye(P, dtype=f32)}


def kernel(**inputs):
    import concourse.bacc as bacc
    from concourse.bass_utils import run_bass_kernel_spmd

    nc = bacc.Bacc("TRN2", target_bir_lowering=False, num_devices=1)
    arrays, aps = {}, {}
    given = {name: np.ascontiguousarray(inputs[name]) for name in _INS}
    for name, v in {**given, **constants()}.items():
        arrays[f"in_{name}"] = v
        aps[name] = nc.dram_tensor(f"in_{name}", v.shape, mybir.dt.from_np(v.dtype), kind="ExternalInput").ap()
    out = nc.dram_tensor("out_dram", (1, T, D), F32, kind="ExternalOutput").ap()
    build(nc, aps, out)
    r = run_bass_kernel_spmd(nc, [arrays], core_ids=[0])
    return r.results[0]["out_dram"]
```
